# Optimizing a Trainium2 kernel written in Bass

```python
import math
import jax, jax.numpy as jnp
from jax import lax
import numpy as np

D_MODEL = 2048
BATCH = 1
SEQ = 512
DEPTH = 1
DEC_BATCH = 8
DEC_SEQ = 8
PAST_LEN = 1024
PAGE_SIZE = 128

HEAD_DIM = 128
POOL_WINDOWS = (2, 4, 8, 16)
POOL_GROUPS = len(POOL_WINDOWS)
POOL_GROUP_WIDTH = D_MODEL // 16
POOL_WIDTH = POOL_GROUPS * POOL_GROUP_WIDTH
POOL_STATE = max(POOL_WINDOWS) - 1
FOX_HEADS = D_MODEL // 256
FOX_WIDTH = FOX_HEADS * HEAD_DIM
MEM_HEADS = 4
MEM_WIDTH = MEM_HEADS * HEAD_DIM
N_MEM = 256
N_BRANCH = 3
IN_COLS = POOL_WIDTH + 3 * FOX_WIDTH + FOX_HEADS + MEM_WIDTH + N_BRANCH * D_MODEL
Q_BLOCK = 128
FORGET_BIAS = 3.0
PEER_HEADS = 8
PEER_N_KEYS = 128
PEER_N_EXPERTS = PEER_N_KEYS * PEER_N_KEYS
PEER_KEY_DIM = 256
PEER_HALF = PEER_KEY_DIM // 2
PEER_TOPK = 16
PEER_BLOCK = 128
RMS_EPS = 1e-6

kernel_name = "pool_fox_mem_peer_hybrid_step"

F32 = jnp.float32

def rms_norm(x, g):
    xf = x.astype(F32)
    y = xf * lax.rsqrt(jnp.mean(xf * xf, axis=-1, keepdims=True) + RMS_EPS)
    return (y * g.astype(F32)).astype(x.dtype)

def split_in(z, b_f):
    B, T, _ = z.shape
    o = 0
    u_pool = z[..., o:o + POOL_WIDTH]; o += POOL_WIDTH
    q = z[..., o:o + FOX_WIDTH].reshape(B, T, FOX_HEADS, HEAD_DIM); o += FOX_WIDTH
    k = z[..., o:o + FOX_WIDTH].reshape(B, T, FOX_HEADS, HEAD_DIM); o += FOX_WIDTH
    v = z[..., o:o + FOX_WIDTH].reshape(B, T, FOX_HEADS, HEAD_DIM); o += FOX_WIDTH
    f_logit = z[..., o:o + FOX_HEADS]; o += FOX_HEADS
    q_mem = z[..., o:o + MEM_WIDTH].reshape(B, T, MEM_HEADS, HEAD_DIM); o += MEM_WIDTH
    gates = z[..., o:].reshape(B, T, N_BRANCH, D_MODEL)
    logf = jax.nn.log_sigmoid(f_logit.astype(F32) + b_f.astype(F32))
    return u_pool, q, k, v, logf, q_mem, gates

def pool_mix(u_full, n_prefix, pos0, pool_w, pool_scale):
    B, L, _ = u_full.shape
    T = L - n_prefix
    uf = u_full.astype(F32).reshape(B, L, POOL_GROUPS, POOL_GROUP_WIDTH)
    cs = jnp.concatenate([jnp.zeros_like(uf[:, :1]), jnp.cumsum(uf, axis=1)], axis=1)
    r = n_prefix + jnp.arange(T)
    pos = pos0 + jnp.arange(T)
    win = jnp.array(POOL_WINDOWS, jnp.int32)
    lo = jnp.maximum(r[:, None] + 1 - win[None, :], 0)
    cnt = jnp.minimum(pos[:, None] + 1, win[None, :]).astype(F32)
    gidx = jnp.arange(POOL_GROUPS)[None, :]
    win_sum = cs[:, r + 1] - cs[:, lo, gidx]
    pooled = win_sum / cnt[None, :, :, None] - uf[:, n_prefix:]
    y = jnp.einsum('btgc,gcd->btgd', pooled.astype(u_full.dtype), pool_w)
    y = y * pool_scale.reshape(POOL_GROUPS, POOL_GROUP_WIDTH)
    return y.reshape(B, T, POOL_WIDTH)

def fox_prompt(q, k, v, logf):
    B, S, H, Dh = q.shape
    scale = Dh ** -0.5
    c = jnp.cumsum(logf, axis=1)
    c_k = c.transpose(0, 2, 1)
    nb = S // Q_BLOCK
    qb = q.reshape(B, nb, Q_BLOCK, H, Dh).transpose(1, 0, 2, 3, 4)
    cb = c.reshape(B, nb, Q_BLOCK, H).transpose(1, 0, 3, 2)
    kpos = jnp.arange(S)

    def block(args):
        qi, ci, i = args
        s = jnp.einsum('bqhd,bkhd->bhqk', qi, k, preferred_element_type=F32) * scale
        s = s + ci[..., None] - c_k[:, :, None, :]
        qpos = i * Q_BLOCK + jnp.arange(Q_BLOCK)
        s = jnp.where(kpos[None, :] <= qpos[:, None], s, -jnp.inf)
        p = jax.nn.softmax(s, axis=-1).astype(v.dtype)
        return jnp.einsum('bhqk,bkhd->bqhd', p, v)

    o = lax.map(block, (qb, cb, jnp.arange(nb)))
    return o.transpose(1, 0, 2, 3, 4).reshape(B, S, H * Dh)

def fox_sample(q, k_new, v_new, logf_new, k_past, v_past, logf_past):
    B, T, H, Dh = q.shape
    P = k_past.shape[1]
    scale = Dh ** -0.5
    c = jnp.cumsum(jnp.concatenate([logf_past.astype(F32), logf_new], axis=1), axis=1)
    bias = c[:, P:].transpose(0, 2, 1)[..., None] - c.transpose(0, 2, 1)[:, :, None, :]
    s_past = jnp.einsum('bqhd,bkhd->bhqk', q, k_past, preferred_element_type=F32)
    s_new = jnp.einsum('bqhd,bkhd->bhqk', q, k_new, preferred_element_type=F32)
    s = jnp.concatenate([s_past, s_new], axis=-1) * scale + bias
    causal = jnp.arange(T)[None, :] <= jnp.arange(T)[:, None]
    mask = jnp.concatenate([jnp.ones((T, P), bool), causal], axis=1)
    s = jnp.where(mask, s, -jnp.inf)
    p = jax.nn.softmax(s, axis=-1).astype(v_new.dtype)
    o = (jnp.einsum('bhqk,bkhd->bqhd', p[..., :P], v_past)
         + jnp.einsum('bhqk,bkhd->bqhd', p[..., P:], v_new))
    return o.reshape(B, T, H * Dh)

def mem_kv(mem, g, w_k, w_v):
    B, M, _ = mem.shape
    mn = rms_norm(mem, g)
    mk = (mn @ w_k).reshape(B, M, MEM_HEADS, HEAD_DIM)
    mv = (mn @ w_v).reshape(B, M, MEM_HEADS, HEAD_DIM)
    return mk, mv

def mem_attend(q, mk, mv):
    B, T, H, Dh = q.shape
    s = jnp.einsum('bqhd,bmhd->bhqm', q, mk, preferred_element_type=F32) * (Dh ** -0.5)
    p = jax.nn.softmax(s, axis=-1).astype(mv.dtype)
    return jnp.einsum('bhqm,bmhd->bqhd', p, mv).reshape(B, T, H * Dh)

def merge(b_pool, b_fox, b_mem, gates, w_up_pool, w_up_fox, w_up_mem, w_out):
    g = jax.nn.sigmoid(gates.astype(F32)).astype(b_pool.dtype)
    m = (g[..., 0, :] * (b_pool @ w_up_pool)
         + g[..., 1, :] * (b_fox @ w_up_fox)
         + g[..., 2, :] * (b_mem @ w_up_mem))
    return m @ w_out

def peer_ffn(h, w_q, subkeys, u, v):
    B, T, D = h.shape
    n = B * T
    xt = h.reshape(n, D)
    q = (xt @ w_q).reshape(n, PEER_HEADS, 2, PEER_HALF)
    s = jnp.einsum('nhpd,hpkd->nhpk', q, subkeys, preferred_element_type=F32)
    s_top, i_top = lax.top_k(s, PEER_TOPK)
    cand = s_top[:, :, 0, :, None] + s_top[:, :, 1, None, :]
    cand_idx = i_top[:, :, 0, :, None] * PEER_N_KEYS + i_top[:, :, 1, None, :]
    best, sel = lax.top_k(cand.reshape(n, PEER_HEADS, PEER_TOPK * PEER_TOPK), PEER_TOPK)
    eidx = jnp.take_along_axis(cand_idx.reshape(n, PEER_HEADS, -1), sel, axis=-1)
    gate = jax.nn.softmax(best, axis=-1).astype(h.dtype)
    E = PEER_HEADS * PEER_TOPK
    eidx = eidx.reshape(n, E)
    gate = gate.reshape(n, E)
    pad = (-n) % PEER_BLOCK
    xp = jnp.pad(xt, ((0, pad), (0, 0)))
    ip = jnp.pad(eidx, ((0, pad), (0, 0)))
    gp = jnp.pad(gate, ((0, pad), (0, 0)))
    nb = (n + pad) // PEER_BLOCK

    def block(args):
        xb, ib, gb = args
        a = jax.nn.gelu(jnp.einsum('ted,td->te', u[ib], xb), approximate=False)
        return jnp.einsum('te,ted->td', gb * a, v[ib])

    out = lax.map(block, (xp.reshape(nb, PEER_BLOCK, D), ip.reshape(nb, PEER_BLOCK, E),
                          gp.reshape(nb, PEER_BLOCK, E)))
    return out.reshape(nb * PEER_BLOCK, D)[:n].reshape(B, T, D)

def setup_inputs(seed: int = 0) -> dict:
    key = jax.random.key(seed)
    ks = jax.random.split(key, 32)
    nrm = lambda k, shape, s=1.0: jax.random.normal(k, shape, F32) * s
    n_pages = PAST_LEN // PAGE_SIZE
    n_used = DEC_BATCH * n_pages
    n_phys = (5 * n_used + 3) // 4
    page_table = jax.random.permutation(ks[0], n_phys)[:n_used].reshape(DEC_BATCH, n_pages).astype(jnp.int32)
    D = D_MODEL
    return {
        "x_prompt": nrm(ks[1], (BATCH, SEQ, D)),
        "x_sample": nrm(ks[2], (DEC_BATCH, DEC_SEQ, D)),
        "cache_k": nrm(ks[3], (DEPTH, n_phys, PAGE_SIZE, FOX_HEADS, HEAD_DIM)),
        "cache_v": nrm(ks[4], (DEPTH, n_phys, PAGE_SIZE, FOX_HEADS, HEAD_DIM)),
        "cache_logf": jax.nn.log_sigmoid(FORGET_BIAS + nrm(ks[5], (DEPTH, n_phys, PAGE_SIZE, FOX_HEADS))),
        "state_pool": nrm(ks[6], (DEPTH, DEC_BATCH, POOL_STATE, POOL_WIDTH)),
        "cache_mem_k": nrm(ks[7], (DEPTH, DEC_BATCH, N_MEM, MEM_HEADS, HEAD_DIM)),
        "cache_mem_v": nrm(ks[8], (DEPTH, DEC_BATCH, N_MEM, MEM_HEADS, HEAD_DIM)),
        "page_table": page_table,
        "mem_prompt": nrm(ks[9], (BATCH, N_MEM, D)),
        "norm_mix_g": 1.0 + nrm(ks[10], (DEPTH, D), 0.1),
        "w_in": nrm(ks[11], (DEPTH, D, IN_COLS), D ** -0.5),
        "b_f": FORGET_BIAS + nrm(ks[12], (DEPTH, FOX_HEADS), 0.1),
        "pool_w": nrm(ks[13], (DEPTH, POOL_GROUPS, POOL_GROUP_WIDTH, POOL_GROUP_WIDTH), POOL_GROUP_WIDTH ** -0.5),
        "pool_scale": 1.0 + nrm(ks[14], (DEPTH, POOL_WIDTH), 0.1),
        "mem_norm_g": 1.0 + nrm(ks[15], (DEPTH, D), 0.1),
        "w_mem_k": nrm(ks[16], (DEPTH, D, MEM_WIDTH), D ** -0.5),
        "w_mem_v": nrm(ks[17], (DEPTH, D, MEM_WIDTH), D ** -0.5),
        "w_up_pool": nrm(ks[18], (DEPTH, POOL_WIDTH, D), POOL_WIDTH ** -0.5),
        "w_up_fox": nrm(ks[19], (DEPTH, FOX_WIDTH, D), FOX_WIDTH ** -0.5),
        "w_up_mem": nrm(ks[20], (DEPTH, MEM_WIDTH, D), MEM_WIDTH ** -0.5),
        "w_out": nrm(ks[21], (DEPTH, D, D), D ** -0.5),
        "norm_ffn_g": 1.0 + nrm(ks[22], (DEPTH, D), 0.1),
        "w_peer_q": nrm(ks[23], (DEPTH, D, PEER_HEADS * PEER_KEY_DIM), D ** -0.5),
        "peer_subkeys": nrm(ks[24], (DEPTH, PEER_HEADS, 2, PEER_N_KEYS, PEER_HALF), PEER_HALF ** -0.5),
        "peer_u": nrm(ks[25], (DEPTH, PEER_N_EXPERTS, D), D ** -0.5),
        "peer_v": nrm(ks[26], (DEPTH, PEER_N_EXPERTS, D), PEER_HEADS ** -0.5),
        "norm_final_g": 1.0 + nrm(ks[27], (D,), 0.1),
    }

def reference(x_prompt, x_sample, cache_k, cache_v, cache_logf, state_pool, cache_mem_k, cache_mem_v,
              page_table, mem_prompt, norm_mix_g, w_in, b_f, pool_w, pool_scale, mem_norm_g, w_mem_k,
              w_mem_v, w_up_pool, w_up_fox, w_up_mem, w_out, norm_ffn_g, w_peer_q, peer_subkeys,
              peer_u, peer_v, norm_final_g):
    xp = x_prompt
    kp_l, vp_l, fp_l, pp_l, mkp_l, mvp_l = [], [], [], [], [], []
    for layer in range(DEPTH):
        xn = rms_norm(xp, norm_mix_g[layer])
        u_pool, q, k, v, logf, q_mem, gates = split_in(xn @ w_in[layer], b_f[layer])
        b_pool = pool_mix(u_pool, 0, 0, pool_w[layer], pool_scale[layer])
        b_fox = fox_prompt(q, k, v, logf)
        mk, mv = mem_kv(mem_prompt, mem_norm_g[layer], w_mem_k[layer], w_mem_v[layer])
        b_mem = mem_attend(q_mem, mk, mv)
        xp = xp + merge(b_pool, b_fox, b_mem, gates, w_up_pool[layer], w_up_fox[layer],
                        w_up_mem[layer], w_out[layer])
        xp = xp + peer_ffn(rms_norm(xp, norm_ffn_g[layer]), w_peer_q[layer], peer_subkeys[layer],
                           peer_u[layer], peer_v[layer])
        kp_l.append(k); vp_l.append(v); fp_l.append(logf)
        pp_l.append(u_pool[:, -POOL_STATE:]); mkp_l.append(mk); mvp_l.append(mv)
    y_prompt = rms_norm(xp, norm_final_g)

    xs = x_sample
    DB = xs.shape[0]
    ks_l, vs_l, fs_l, ps_l = [], [], [], []
    for layer in range(DEPTH):
        xn = rms_norm(xs, norm_mix_g[layer])
        u_pool, q, k, v, logf, q_mem, gates = split_in(xn @ w_in[layer], b_f[layer])
        pool_full = jnp.concatenate([state_pool[layer].astype(u_pool.dtype), u_pool], axis=1)
        b_pool = pool_mix(pool_full, POOL_STATE, PAST_LEN, pool_w[layer], pool_scale[layer])
        k_past = cache_k[layer][page_table].reshape(DB, -1, FOX_HEADS, HEAD_DIM)
        v_past = cache_v[layer][page_table].reshape(DB, -1, FOX_HEADS, HEAD_DIM)
        f_past = cache_logf[layer][page_table].reshape(DB, -1, FOX_HEADS)
        b_fox = fox_sample(q, k, v, logf, k_past, v_past, f_past)
        b_mem = mem_attend(q_mem, cache_mem_k[layer], cache_mem_v[layer])
        xs = xs + merge(b_pool, b_fox, b_mem, gates, w_up_pool[layer], w_up_fox[layer],
                        w_up_mem[layer], w_out[layer])
        xs = xs + peer_ffn(rms_norm(xs, norm_ffn_g[layer]), w_peer_q[layer], peer_subkeys[layer],
                           peer_u[layer], peer_v[layer])
        ks_l.append(k); vs_l.append(v); fs_l.append(logf); ps_l.append(pool_full[:, -POOL_STATE:])
    y_sample = rms_norm(xs, norm_final_g)

    k_prompt = jnp.stack(kp_l); v_prompt = jnp.stack(vp_l); logf_prompt = jnp.stack(fp_l)
    pool_prompt = jnp.stack(pp_l); mem_k_prompt = jnp.stack(mkp_l); mem_v_prompt = jnp.stack(mvp_l)
    k_sample = jnp.stack(ks_l); v_sample = jnp.stack(vs_l); logf_sample = jnp.stack(fs_l)
    pool_sample = jnp.stack(ps_l)
    return (y_prompt, y_sample, k_prompt, v_prompt, logf_prompt, pool_prompt, mem_k_prompt, mem_v_prompt,
            k_sample, v_sample, logf_sample, pool_sample)


_drawn_inputs = setup_inputs


def setup_inputs(seed=0):
    import zlib

    import numpy as np

    out = dict(_drawn_inputs(seed))
    spreads = {}
    factors = {}
    for name, (base, spread) in spreads.items():
        noise = np.random.default_rng([zlib.crc32(name.encode()), seed]).standard_normal(out[name].shape)
        drawn = base * np.exp(spread * noise) if base else spread * noise
        out[name] = __import__('jax').numpy.asarray(drawn.astype(out[name].dtype))
    for name, factor in factors.items():
        out[name] = (out[name] * factor).astype(out[name].dtype)
    return out
```

```python
import numpy as np
from contextlib import ExitStack

import concourse.bass as bass
from concourse import mybir

F32, F32R, I32, U32 = mybir.dt.float32, mybir.dt.float32r, mybir.dt.int32, mybir.dt.uint32
ACT, ALU, AX = mybir.ActivationFunctionType, mybir.AluOpType, mybir.AxisListType

D = 2048
P = 128
KC = D // P
T_P, T_S = 512, 64
T = T_P + T_S
HALF = T // 2
NBLK = 5
ROWS = [128, 128, 128, 128, 64]
DB, DT = 8, 8
FOX, MEM, HD = 8, 4, 128
N_MEM = 256
PAGES, PAGE = 8, 128
N_PHYS = 80
WINDOWS = (2, 4, 8, 16)
STATE = 15
SCALE = float(HD) ** -0.5
EPS = 1e-6
NEG = -1e30
PH, PK, PTOP, NKEY = 8, 16, 16, 128
NEXP = PH * PTOP
Q0, QM0, K0, V0, U0, F0, NZ = 0, 8, 12, 20, 28, 32, 33
NGATE = 3 * KC
RING = 6

BASE = 16512
O_IDENT, O_SMALL, O_MKT, O_MVTOK, O_GB, O_ATT, O_Z, O_R1 = 0, 512, 1536, 5632, 9728, 17920, 27168, 103200
O_R2, O_W = O_R1 + KC * T * 4, O_R1 + 2 * KC * T * 4


def build(nc, a):
    ctx = ExitStack()
    names = {}

    def at(name, shape, dtype, offset):
        return nc.alloc_sbuf_tensor_at(name, shape, dtype, offset=BASE + offset)

    live = []

    def sem(name):
        live.append(nc.alloc_semaphore(name=name))
        return live[-1]

    def recycle():
        nc.clear_and_free_semaphores(live)
        live.clear()
        nc.all_engine_barrier()

    with ctx:
        gates_dram = nc.dram_tensor("gates_scratch", [NGATE, P, T], F32, kind="Internal").ap()

        ident = at("ident", [P, P], F32, O_IDENT)
        small = at("small", [P, 64], F32, O_SMALL)
        b_f, pool_scale = small[0:FOX, 0:1], small[:, 4:8]
        ss, ms, rstd = small[:, 8:13], small[:, 16:21], small[:, 24:29]
        ss_m, ms_m, rstd_m = small[:, 32:34], small[:, 36:38], small[:, 40:42]
        ss2, ms2, rstd2 = small[:, 44:49], small[:, 50:55], small[:, 56:61]
        mk_t = at("mk_t", [P, MEM, N_MEM], F32, O_MKT)
        mv_tok = at("mv_tok", [P, 2, MEM * HD], F32, O_MVTOK)
        g_row = at("g_row", [P, D], F32, O_GB)

        raw = at("w_raw", [P, 4, 1024], F32, O_W)
        w_hi = at("w_hi", [P, 2, 1024], F32R, O_W + 16384)
        w_lo = at("w_lo", [P, 2, 1024], F32R, O_W + 24576)

        acc = ctx.enter_context(nc.psum_tensor("acc", [P, 2, 2, 512], F32))
        tps = ctx.enter_context(nc.psum_tensor("tps", [P, 4, 512], F32))

        def stream_sems(tag):
            return dict(loaded=[sem(f"{tag}_w_loaded{k}") for k in range(4)], hi=sem(f"{tag}_hi_ready"),
                        lo=sem(f"{tag}_lo_ready"), mm=sem(f"{tag}_half_done"),
                        act=sem(f"{tag}_act_drained"), dve=sem(f"{tag}_dve_drained"))

        def load_stripes(sp, w, n, q):
            nj = 2 * n
            for j in range(4):
                sp.dma_start(raw[:, j, :], w[j * P:(j + 1) * P, :]).then_inc(q["loaded"][j], 16)
            with sp.Fori(1, nj // 4) as i:
                for k in range(4):
                    sp.wait_ge(q["lo"], 4 * i + k - 3)
                    sp.dma_start(raw[:, k, :], w[bass.ds((4 * i + k) * P, P), :]).then_inc(q["loaded"][k], 16)
            for j in range(nj // 4 * 4, nj):
                sp.wait_ge(q["lo"], j - 3)
                sp.dma_start(raw[:, j % 4, :], w[j * P:(j + 1) * P, :]).then_inc(q["loaded"][j % 4], 16)

        def split_hi(act, i, s, q):
            for h in range(2):
                j = 2 * s + h
                act.wait_ge(q["loaded"][j % 4], 16 * (i + j // 4 + 1))
                act.wait_ge(q["mm"], 4 * i + j + 1)
                nc.scalar.activation(w_hi[:, h, :], raw[:, j % 4, :], ACT.Copy).then_inc(q["hi"], 1)

        def split_lo(dve, i, s, q):
            for h in range(2):
                j = 2 * s + h
                dve.wait_ge(q["loaded"][j % 4], 16 * (i + j // 4 + 1))
                dve.wait_ge(q["hi"], 4 * i + j + 1)
                nc.vector.tensor_tensor(w_lo[:, h, :], raw[:, j % 4, :], w_hi[:, h, :].bitcast(F32),
                                        ALU.subtract).then_inc(q["lo"], 1)

        def lagged(eng, n, split, drain):
            split(0, 0)
            pairs = (n - 1) // 2
            with eng.Fori(0, pairs) as i:
                split(i, 1)
                drain(i, 0)
                split(i, 2)
                drain(i, 1)
            if n % 2 == 0:
                split(pairs, 1)
                drain(pairs, 0)
                drain(pairs, 1)
            else:
                drain(pairs, 0)

        def multiply_half(pe, j, par, h, x_hi, x_lo, cols, q, out=None):
            for c in range(8):
                cc = 8 * h + c
                wh, wl = w_hi[:, h, c * P:(c + 1) * P], w_lo[:, h, c * P:(c + 1) * P]
                for (p_, l_, r_) in ((0, wh, x_hi), (1, wh, x_lo), (2, wl, x_hi)):
                    for b, (c0, cn) in enumerate(cols):
                        dst, first, last_c = out(cc, b, cn) if out else (acc[:, par, b, 0:cn], 0, KC - 1)
                        last = nc.tensor.matmul(dst, l_, r_[:, cc, c0:c0 + cn],
                                                start=(cc == first and p_ == 0),
                                                stop=(cc == last_c and p_ == 2))
            last.then_inc(q["mm"], 1)

        HALVES = [(0, HALF), (HALF, HALF)]

        def multiply_stripes(pe, n, x_hi, x_lo, cols, q, use=("act", "dve"), after=None):
            def one(i, s):
                for h in range(2):
                    pe.wait_ge(q["lo"], 4 * i + 2 * s + h + 1)
                    if h == 0:
                        for u in use:
                            pe.wait_ge(q[u], 2 * i + s + 1)
                    multiply_half(pe, None, s % 2, h, x_hi, x_lo, cols, q)

            pe.sem_inc(q["mm"], 2)
            for u in use:
                pe.sem_inc(q[u], 2)
            if after is None:
                with pe.Fori(0, n // 2) as i:
                    one(i, 0)
                    one(i, 1)
                if n % 2:
                    one(n // 2, 0)
            else:
                lagged(pe, n, one, after)

        def norm_transposed(tag, n_blk, rows, g_in, x_of, load, x_hi, x_lo, stat, xn):
            ss_, ms_, r_ = stat
            s_g, s_sq, s_ms, s_rt, s_r, s_xn = (sem(f"{tag}_{x}") for x in ("g_loaded", "squared", "mean", "root", "rstd", "normed"))
            s_tp, s_hi, s_lo = (sem(f"{tag}_{x}") for x in ("transposed", "hi_out", "lo_out"))
            s_x = [sem(f"{tag}_x_loaded{k}") for k in range(2)] if load else None
            with nc.Block() as block:
                @block.sync
                def _(sp):
                    sp.dma_start(g_row[:], g_in.rearrange("(o d) -> o d", o=1).to_broadcast([P, D])).then_inc(s_g, 16)
                    if tag == "mem":
                        for dst, name in ((ident[:], "ident"), (pool_scale, "pool_scale"), (b_f, "b_f")):
                            sp.dma_start(dst, a[name]).then_inc(s_g, 16)
                    if load:
                        for b in range(n_blk):
                            if b >= 2:
                                sp.wait_ge(s_xn, b - 1)
                            sp.dma_start(x_of(b), load(b)).then_inc(s_x[b % 2], 16)

                @block.scalar
                def _(act):
                    def squares(b):
                        if load:
                            act.wait_ge(s_x[b % 2], 16 * (b // 2 + 1))
                        if b >= 2:
                            act.wait_ge(s_tp, 4 * (b - 1))
                        nc.scalar.activation(xn[0:rows[b], b % 2, :], x_of(b), ACT.Square,
                                             accum_out=ss_[0:rows[b], b:b + 1]).then_inc(s_sq, 1)
                        act.wait_ge(s_ms, b + 1)
                        nc.scalar.activation(ms_[0:rows[b], b:b + 1], ms_[0:rows[b], b:b + 1], ACT.Sqrt).then_inc(s_rt, 1)

                    squares(0)
                    for b in range(n_blk):
                        if b + 1 < n_blk:
                            squares(b + 1)
                        for g in range(4):
                            act.wait_ge(s_tp, 4 * b + g + 1)
                            nc.scalar.activation(x_hi[:, 4 * g:4 * g + 4, b * P:b * P + rows[b]],
                                                 tps[:, g, 0:4 * rows[b]].rearrange("p (c t) -> p c t", c=4),
                                                 ACT.Copy).then_inc(s_hi, 1)

                @block.vector
                def _(dve):
                    def norm(b):
                        n = rows[b]
                        dve.wait_ge(s_sq, b + 1)
                        nc.vector.tensor_scalar(ms_[0:n, b:b + 1], ss_[0:n, b:b + 1], 1.0 / D, EPS, ALU.mult,
                                                ALU.add).then_inc(s_ms, 1)
                        dve.wait_ge(s_rt, b + 1)
                        nc.vector.reciprocal(r_[0:n, b:b + 1], ms_[0:n, b:b + 1]).then_inc(s_r, 1)
                        dve.wait_ge(s_r, b + 1)
                        nc.vector.scalar_tensor_tensor(out=xn[0:n, b % 2, :], in0=x_of(b), scalar=r_[0:n, b:b + 1],
                                                       in1=g_row[0:n, :], op0=ALU.mult, op1=ALU.mult).then_inc(s_xn, 1)

                    dve.wait_ge(s_g, 64 if tag == "mem" else 16)
                    norm(0)
                    for b in range(n_blk):
                        if b + 1 < n_blk:
                            norm(b + 1)
                        for g in range(4):
                            dve.wait_ge(s_hi, 4 * b + g + 1)
                            nc.vector.tensor_tensor(x_lo[:, 4 * g:4 * g + 4, b * P:b * P + rows[b]],
                                                    tps[:, g, 0:4 * rows[b]].rearrange("p (c t) -> p c t", c=4),
                                                    x_hi[:, 4 * g:4 * g + 4, b * P:b * P + rows[b]].bitcast(F32),
                                                    ALU.subtract).then_inc(s_lo, 1)

                @block.tensor
                def _(pe):
                    pe.wait_ge(s_g, 64 if tag == "mem" else 16)
                    for b in range(n_blk):
                        n = rows[b]
                        pe.wait_ge(s_xn, b + 1)
                        for g in range(4):
                            if b >= 1:
                                pe.wait_ge(s_lo, 4 * (b - 1) + g + 1)
                            for c in range(4):
                                last = nc.tensor.transpose(tps[:, g, c * n:(c + 1) * n],
                                                           xn[0:n, b % 2, (4 * g + c) * P:(4 * g + c + 1) * P],
                                                           ident[0:n, 0:n])
                            last.then_inc(s_tp, 1)

        z = at("z", [P, NZ, T], F32, O_Z)
        xb_m = at("xb_m", [P, 2, D], F32, O_Z)
        xn_m = at("xn_m", [P, 2, D], F32, O_Z + 16384)
        mn_hi = at("mn_hi", [P, KC, N_MEM], F32R, O_R1)
        mn_lo = at("mn_lo", [P, KC, N_MEM], F32R, O_R2)
        norm_transposed("mem", 2, [128, 128], a["mem_norm_g"], lambda b: xb_m[:, b % 2, :],
                        lambda b: a["mem_prompt"][b * P:(b + 1) * P, :], mn_hi, mn_lo, (ss_m, ms_m, rstd_m), xn_m)

        mkv_t = at("mkv_t", [P, 2 * MEM, N_MEM], F32, O_Z)
        q = stream_sems("mem")
        s_vt, s_vo, s_mout = sem("mem_v_transposed"), sem("mem_v_copied"), sem("mem_stored")
        with nc.Block() as block:
            @block.sync
            def _(sp):
                load_stripes(sp, a["w_mem"], 2 * MEM, q)
                sp.wait_ge(q["act"], 2 + 2 * MEM)
                sp.dma_start(a["mem_out"], mkv_t[:]).then_inc(s_mout, 16)
                sp.wait_ge(s_mout, 16)

            def drain_mem(act, i, s):
                act.wait_ge(q["mm"], 4 * i + 2 * s + 4)
                nc.scalar.activation(mkv_t[:, bass.ds(2 * i + s, 1), :], acc[:, s % 2, 0:1, 0:N_MEM], ACT.Copy).then_inc(q["act"], 1)

            @block.scalar
            def _(act):
                lagged(act, 2 * MEM, lambda i, s: split_hi(act, i, s, q), lambda i, s: drain_mem(act, i, s))
                act.wait_ge(q["act"], 2 + MEM)
                nc.scalar.activation(mk_t[:], mkv_t[:, 0:MEM, :], ACT.Copy)

            @block.vector
            def _(dve):
                with dve.Fori(0, MEM) as i:
                    split_lo(dve, i, 0, q)
                    split_lo(dve, i, 1, q)
                for m in range(2):
                    dve.wait_ge(s_vt, m + 1)
                    nc.vector.tensor_copy(mv_tok[:, m, :], tps[:, m, :]).then_inc(s_vo, 1)

            @block.tensor
            def _(pe):
                multiply_stripes(pe, 2 * MEM, mn_hi, mn_lo, [(0, N_MEM)], q, use=("act",))
                pe.wait_ge(q["act"], 2 + 2 * MEM)
                for m in range(2):
                    for h in range(MEM):
                        last = nc.tensor.transpose(tps[:, m, h * P:(h + 1) * P], mkv_t[:, MEM + h, m * P:(m + 1) * P], ident[:])
                    last.then_inc(s_vt, 1)

        recycle()

        x_hi = at("x_hi", [P, KC, T], F32R, O_R1)
        x_lo = at("x_lo", [P, KC, T], F32R, O_R2)
        xb = at("xb", [P, 2, D], F32, O_Z)
        xn = at("xn", [P, 2, D], F32, O_Z + 16384)
        norm_transposed("mix", NBLK, ROWS, a["norm_mix_g"], lambda b: xb[0:ROWS[b], b % 2, :],
                        lambda b: a["x"][b * P:b * P + ROWS[b], :], x_hi, x_lo, (ss, ms, rstd), xn)

        def drain_to(dst_t, q):
            def by_act(act, i, s):
                act.wait_ge(q["mm"], 4 * i + 2 * s + 4)
                nc.scalar.activation(dst_t[:, bass.ds(2 * i + s, 1), 0:HALF], acc[:, s % 2, 0, 0:HALF], ACT.Copy).then_inc(q["act"], 1)

            def by_dve(dve, i, s):
                dve.wait_ge(q["mm"], 4 * i + 2 * s + 4)
                nc.vector.tensor_copy(dst_t[:, bass.ds(2 * i + s, 1), HALF:T], acc[:, s % 2, 1, 0:HALF]).then_inc(q["dve"], 1)
            return by_act, by_dve

        q1 = stream_sems("proj")
        act_z, dve_z = drain_to(z, q1)
        with nc.Block() as block:
            @block.sync
            def _(sp):
                load_stripes(sp, a["w_z"], NZ, q1)

            @block.scalar
            def _(act):
                lagged(act, NZ, lambda i, s: split_hi(act, i, s, q1), lambda i, s: act_z(act, i, s))

            @block.vector
            def _(dve):
                lagged(dve, NZ, lambda i, s: split_lo(dve, i, s, q1), lambda i, s: dve_z(dve, i, s))

            @block.tensor
            def _(pe):
                multiply_stripes(pe, NZ, x_hi, x_lo, HALVES, q1)

        gate_out = at("gate_out", [P, 2, T], F32, O_GB)
        q2 = stream_sems("gate")
        s_gfree, s_gst, s_zst = sem("gate_buffer_free"), sem("gate_stored"), sem("z_stored")
        with nc.Block() as block:
            @block.sync
            def _(sp):
                load_stripes(sp, a["w_gate"], NGATE, q2)

            @block.gpsimd
            def _(pool):
                pool.sem_inc(s_gfree, 2)
                pool.dma_start(a["z_out"], z[:, K0:F0, :]).then_inc(s_zst, 16)
                with pool.Fori(0, NGATE // 2) as i:
                    for s in range(2):
                        pool.wait_ge(q2["act"], 2 * i + s + 3)
                        pool.dma_start(gates_dram[bass.ds(2 * i + s, 1), :, :].rearrange("o p t -> p (o t)"),
                                       gate_out[:, s, :]).then_inc(s_gst, 16)
                        pool.wait_ge(s_gst, 32 * i + 16 * s + 16)
                        pool.sem_inc(s_gfree, 1)
                pool.wait_ge(s_zst, 16)

            def drain_gate(act, i, s):
                act.wait_ge(q2["mm"], 4 * i + 2 * s + 4)
                act.wait_ge(s_gfree, 2 * i + s + 1)
                nc.scalar.activation(gate_out[:, s % 2, :].rearrange("p (b t) -> p b t", b=2), acc[:, s % 2, :, 0:HALF],
                                     ACT.Sigmoid).then_inc(q2["act"], 1)

            @block.scalar
            def _(act):
                lagged(act, NGATE, lambda i, s: split_hi(act, i, s, q2), lambda i, s: drain_gate(act, i, s))

            @block.vector
            def _(dve):
                with dve.Fori(0, NGATE // 2) as i:
                    split_lo(dve, i, 0, q2)
                    split_lo(dve, i, 1, q2)

            @block.tensor
            def _(pe):
                multiply_stripes(pe, NGATE, x_hi, x_lo, HALVES, q2, use=("act",))

        recycle()

        O_CAUS, O_LF, O_CP, O_CS, O_CNT = O_ATT, O_ATT + 512, O_ATT + 2816, O_ATT + 4864, O_ATT + 8992
        negsel_p = at("negsel_p", [FOX, FOX, P], F32, O_GB)
        negsel_s = at("negsel_s", [DB * FOX, DB, FOX * DT], F32, O_GB + 4096)
        smask = at("smask", [FOX * DT, DB, T_S], F32, O_GB + 6144)
        causal = at("causal", [P, P], F32, O_CAUS)
        logf = at("logf", [FOX, T], F32, O_LF)
        c_p = at("c_p", [FOX, T_P], F32, O_CP)
        c_s = at("c_s", [DB * FOX, PAGES * PAGE + DT], F32, O_CS)
        cnt_inv = at("cnt_inv", [P, 4, 16], F32, O_CNT)
        b_t = at("b_t", [P, KC, T], F32, O_R1)
        v_tok = at("v_tok", [P, NBLK, FOX * HD], F32, O_R2)
        O_K = O_R2 + NBLK * FOX * HD * 4
        PW, SW = 16 + T_P, 24
        ua = at("ua", [P, PW + DB * SW], F32, O_K)
        ub = at("ub", [P, PW + DB * SW], F32, O_K + 2880)
        uc = at("uc", [P, PW + DB * SW], F32, O_K + 5760)
        pooled = at("pooled", [P, T], F32, O_K + 8640)
        pool_w = at("pool_w", [P, 4, P], F32, O_K + 11008)
        ones = at("ones", [DB * FOX, PAGES * PAGE + DT], F32, O_K + 13120)
        lf_raw = at("lf_raw", [DB * FOX, PAGES * PAGE + DT], F32, O_K + 17280)
        lt1 = at("lt1", [FOX, T], F32, O_K + 21440)
        lt2 = at("lt2", [FOX, T], F32, O_K + 23808)
        pt = at("pt", [1, DB * PAGES], I32, O_SMALL + 512)
        st_buf = at("state_buf", [P, 4, DB, STATE], F32, O_W + 20000)
        st_new = at("state_new", [P, 4, DB, STATE], F32, O_W + 22016)
        t16 = at("pool_head", [P, 16], F32, O_W + 24000)

        s_pc, s_pt, s_plf, s_pln, s_lfo = (sem(f"prep_{x}") for x in ("consts", "page_table", "past_logf", "new_logf", "logf_stored"))
        s_fa, s_fv, s_init = sem("prep_logf_act"), sem("prep_logf_dve"), sem("prep_cleared")
        s_un, s_st, s_pd, s_ym, s_yo = (sem(f"pool_{x}") for x in ("chain", "state_loaded", "pooled", "mixed", "drained"))
        s_sn = sem("state_assembled")
        s_vtp, s_vtc = sem("v_transposed"), sem("v_copied")
        with nc.Block() as block:
            @block.sync
            def _(sp):
                sp.dma_start(pt[:], a["page_table"]).then_inc(s_pt, 16)
                for dst, name in ((negsel_p[:], "negsel_p"), (negsel_s[:], "negsel_s"), (smask[:], "smask"), (causal[:], "causal"),
                                  (cnt_inv[:], "cnt_inv"), (pool_w[:], "pool_w")):
                    sp.dma_start(dst, a[name]).then_inc(s_pc, 16)
                sp.dma_start(st_buf[:], a["state_pool"]).then_inc(s_st, 16)
                sp.wait_ge(s_pt, 16)
                for b in range(DB):
                    for j in range(PAGES):
                        page = sp.value_load(pt[0:1, b * PAGES + j:b * PAGES + j + 1], min_val=0, max_val=N_PHYS - 1)
                        sp.dma_start(lf_raw[b * FOX:(b + 1) * FOX, j * PAGE:(j + 1) * PAGE],
                                     a["cache_logf"][bass.ds(page * FOX, FOX), :]).then_inc(s_plf, 16)

            @block.gpsimd
            def _(pool):
                nc.gpsimd.memset(ones[:], 1.0).then_inc(s_init, 1)
                pool.wait_ge(s_st, 16)
                for g in range(4):
                    nc.gpsimd.tensor_copy(st_new[:, g, :, 0:STATE - DT], st_buf[:, g, :, DT:STATE])
                    last = nc.gpsimd.tensor_copy(st_new[:, g, :, STATE - DT:STATE],
                                                 z[:, U0 + g, T_P:T].rearrange("p (b t) -> p b t", b=DB))
                last.then_inc(s_sn, 1)
                pool.wait_ge(s_sn, 1)
                pool.dma_start(a["state_out"], st_new[:]).then_inc(s_lfo, 16)
                pool.wait_ge(s_fv, 3)
                pool.dma_start(a["logf_out"], logf[:]).then_inc(s_lfo, 16)
                for b in range(DB):
                    pool.dma_start(lf_raw[b * FOX:(b + 1) * FOX, PAGES * PAGE:],
                                   logf[:, T_P + b * DT:T_P + (b + 1) * DT]).then_inc(s_pln, 16)
                pool.wait_ge(s_lfo, 32)

            @block.scalar
            def _(act):
                act.wait_ge(s_fv, 1)
                nc.scalar.activation(lt2[:], lt1[:], ACT.Abs).then_inc(s_fa, 1)
                act.wait_ge(s_fa, 1)
                nc.scalar.activation(lt2[:], lt2[:], ACT.Exp, scale=-1.0).then_inc(s_fa, 1)
                act.wait_ge(s_fa, 2)
                act.wait_ge(s_fv, 2)
                nc.scalar.activation(lt2[:], lt2[:], ACT.Ln, bias=1.0).then_inc(s_fa, 1)
                for n in range(2 * NBLK):
                    r = ROWS[n // 2]
                    act.wait_ge(s_vtp, n + 1)
                    nc.scalar.activation(v_tok[0:r, n // 2, (n % 2) * 512:(n % 2 + 1) * 512], tps[0:r, n % 2, :],
                                         ACT.Copy).then_inc(s_vtc, 1)

            @block.vector
            def _(dve):
                chain = [0]

                def link(ins):
                    chain[0] += 1
                    ins.then_inc(s_un, 1)
                    dve.wait_ge(s_un, chain[0])

                nc.vector.tensor_scalar(lt1[:], z[0:FOX, F0, :], b_f, None, ALU.add).then_inc(s_fv, 1)
                dve.wait_ge(s_fa, 1)
                nc.vector.tensor_scalar(lt1[:], lt1[:], 0.0, None, ALU.min).then_inc(s_fv, 1)
                dve.wait_ge(s_fa, 3)
                dve.wait_ge(s_fv, 2)
                nc.vector.tensor_tensor(logf[:], lt1[:], lt2[:], ALU.subtract).then_inc(s_fv, 1)
                dve.wait_ge(s_fv, 3)
                dve.wait_ge(s_init, 1)
                nc.vector.tensor_tensor_scan(c_p[:], ones[0:FOX, 0:T_P], logf[:, 0:T_P], 0.0, ALU.mult, ALU.add)
                link(nc.vector.memset(ua[:, 0:16], 0.0))
                dve.wait_ge(s_pc, 96)
                dve.wait_ge(s_st, 16)
                for g, w in enumerate(WINDOWS):
                    u = z[:, U0 + g, :]
                    u_s = u[:, T_P:T].rearrange("p (b t) -> p b t", b=DB)
                    nc.vector.tensor_copy(ua[:, 16:PW], u[:, 0:T_P])
                    nc.vector.tensor_copy(ua[:, PW:].rearrange("p (b c) -> p b c", b=DB)[:, :, 16:SW], u_s)
                    link(nc.vector.tensor_copy(ua[:, PW:].rearrange("p (b c) -> p b c", b=DB)[:, :, 1:16], st_buf[:, g]))
                    src, sh = ua, 1
                    lo = 1
                    while sh < w:
                        dst = ub if src is not ub else uc
                        s3 = src[:, PW:].rearrange("p (b c) -> p b c", b=DB)
                        d3 = dst[:, PW:].rearrange("p (b c) -> p b c", b=DB)
                        nc.vector.tensor_tensor(dst[:, lo + sh - 1:PW], src[:, lo + sh - 1:PW], src[:, lo - 1:PW - sh], ALU.add)
                        link(nc.vector.tensor_tensor(d3[:, :, lo + sh:SW], s3[:, :, lo + sh:SW], s3[:, :, lo:SW - sh], ALU.add))
                        src, lo, sh = dst, lo + sh, 2 * sh
                    if g >= 1:
                        dve.wait_ge(s_ym, g)
                    link(nc.vector.tensor_tensor(t16[:], src[:, 16:32], cnt_inv[:, g, :], ALU.mult))
                    nc.vector.tensor_tensor(pooled[:, 0:16], t16[:], u[:, 0:16], ALU.subtract)
                    nc.vector.scalar_tensor_tensor(out=pooled[:, 16:T_P], in0=src[:, 32:PW], scalar=1.0 / w, in1=u[:, 16:T_P],
                                                   op0=ALU.mult, op1=ALU.subtract)
                    nc.vector.scalar_tensor_tensor(out=pooled[:, T_P:T].rearrange("p (b t) -> p b t", b=DB),
                                                   in0=src[:, PW:].rearrange("p (b c) -> p b c", b=DB)[:, :, 16:SW],
                                                   scalar=1.0 / w, in1=u_s, op0=ALU.mult, op1=ALU.subtract).then_inc(s_pd, 1)
                    dve.wait_ge(s_ym, g + 1)
                    nc.vector.tensor_scalar(b_t[:, g, :].rearrange("p (b t) -> p b t", b=2), acc[:, 0, :, 0:HALF],
                                            pool_scale[:, g:g + 1], None, ALU.mult).then_inc(s_yo, 1)
                dve.wait_ge(s_plf, 16 * DB * PAGES)
                dve.wait_ge(s_pln, 16 * DB)
                nc.vector.tensor_tensor_scan(c_s[:], ones[:], lf_raw[:], 0.0, ALU.mult, ALU.add)

            @block.tensor
            def _(pe):
                for n in range(2 * NBLK):
                    r = ROWS[n // 2]
                    if n >= 2:
                        pe.wait_ge(s_vtc, n - 1)
                    for k in range(4):
                        c0 = (n // 2) * P
                        last = nc.tensor.transpose(tps[0:r, n % 2, k * P:(k + 1) * P], z[:, V0 + 4 * (n % 2) + k, c0:c0 + r], ident[:])
                    last.then_inc(s_vtp, 1)
                pe.wait_ge(s_pc, 96)
                for g in range(4):
                    pe.wait_ge(s_pd, g + 1)
                    if g >= 1:
                        pe.wait_ge(s_yo, g)
                    for b in range(2):
                        last = nc.tensor.matmul(acc[:, 0, b, 0:HALF], pool_w[:, g, :], pooled[:, b * HALF:(b + 1) * HALF],
                                                start=True, stop=True)
                    last.then_inc(s_ym, 1)

        recycle()

        k_ring = at("k_ring", [P, RING, 1024], F32, O_K)
        v_ring = at("v_ring", [P, RING, 1024], F32, O_Z + V0 * T * 4)
        O_P = O_K + RING * 4096
        probs = at("probs", [P, 2, PAGES * PAGE + T_S], F32, O_P)
        p_t = at("p_t", [P, 2, 9, P], F32, O_P + 8704)
        qz = at("qz", [P, 2, FOX * 72], F32, O_P + 17920)
        qzm = at("qzm", [P, 4, MEM * 40], F32, O_P + 22528)
        stat_a = at("stat_a", [P, 2, 4], F32, O_P + 25088)
        rsum = at("rsum", [P, 2, 4], F32, O_P + 25120)
        nmax = at("nmax", [P, 2], F32, O_P + 25152)
        rinv = at("rinv", [P, 2], F32, O_P + 25184)
        prompt = [("fox", h, i) for i in range(4) for h in range(FOX)] + [("mem", h, i) for i in range(4) for h in range(MEM)]
        samples = [("sfox", g, 0) for g in range(DB // 2)] + [("smem", g, 0) for g in range(DB // 4)]
        units = []
        for n, u in enumerate(samples):
            units += prompt[8 * n:8 * n + 8] + [u]
        units += prompt[48:]
        NU = len(units)

        def keys(u):
            kind, _, i = u
            return {"fox": (i + 1) * P, "mem": N_MEM, "sfox": PAGES * PAGE + T_S, "smem": N_MEM}[kind]

        def chunks(u):
            return (keys(u) + P - 1) // P

        def t_groups(u):
            return (chunks(u) + 3) // 4

        groups_before = [sum(t_groups(v) for v in units[:n]) for n in range(NU + 1)]
        n_samp = [sum(v[0] in ("sfox", "smem") for v in units[:n]) for n in range(NU + 1)]
        n_sfox = [sum(v[0] == "sfox" for v in units[:n]) for n in range(NU + 1)]
        n_smem = [sum(v[0] == "smem" for v in units[:n]) for n in range(NU + 1)]
        pages_of = {"sfox": 2 * PAGES, "smem": 4}
        pages_before = [sum(pages_of.get(v[0], 0) for v in units[:n]) for n in range(NU + 1)]

        s_kl = [sem(f"k_page_loaded{k}") for k in range(RING)]
        s_vl = [sem(f"v_page_loaded{k}") for k in range(RING)]
        s_ku, s_vu = sem("k_page_used"), sem("v_page_used")
        s_qz, s_qc = sem("q_rows_placed"), sem("q_rows_cleared")
        s_s, s_m, s_e, s_rs, s_pr = (sem(f"att_{x}") for x in ("logits", "negmax", "exps", "recips", "probs"))
        s_ng = sem("att_max")
        s_t, s_tc, s_pv, s_o = (sem(f"att_{x}") for x in ("transposed", "transposed_copied", "weighted", "drained"))

        def logits(n):
            return [acc[:, 0, 0, :], acc[:, 0, 1, :], acc[:, 1, 0, :]] if n % 2 == 0 else [acc[:, 1, 1, :], tps[:, 0, :], tps[:, 1, :]]

        tbank, obank = tps[:, 2, :], tps[:, 3, :]

        with nc.Block() as block:
            @block.sync
            def _(sp):
                n = 0
                for u in units:
                    if u[0] not in pages_of:
                        continue
                    m = pages_of[u[0]]
                    for which, ring, used, loaded in (("k", k_ring, s_ku, s_kl), ("v", v_ring, s_vu, s_vl)):
                        for k in range(m):
                            j = n + k
                            if j >= RING:
                                sp.wait_ge(used, j - RING + 1)
                            if u[0] == "sfox":
                                row = 2 * u[1] * PAGES + k
                                page = sp.value_load(pt[0:1, row:row + 1], min_val=0, max_val=N_PHYS - 1)
                                src = a["cache_" + which][bass.ds(page * P, P), :]
                            else:
                                row = 4 * u[1] + k
                                src = a["mem_cache_" + which][row * P:(row + 1) * P, :]
                            sp.dma_start(ring[:, j % RING, :], src).then_inc(loaded[j % RING], 16)
                    n += m

            @block.gpsimd
            def _(pool):
                nc.gpsimd.memset(qz[:], 0.0).then_inc(s_qc, 1)
                nc.gpsimd.memset(qzm[:], 0.0).then_inc(s_qc, 1)
                pool.wait_ge(s_qc, 2)
                for n, u in enumerate(units):
                    if u[0] == "sfox":
                        if n_sfox[n]:
                            m = max(k for k in range(n) if units[k][0] == "sfox")
                            pool.wait_ge(s_s, m + 1)
                        for b in range(2):
                            c0 = T_P + (2 * u[1] + b) * DT
                            last = nc.gpsimd.tensor_copy(qz[:, b, :].rearrange("p (h c) -> p h c", h=FOX)[:, :, 0:DT],
                                                         z[:, Q0:Q0 + FOX, c0:c0 + DT])
                        last.then_inc(s_qz, 1)
                    elif u[0] == "smem":
                        if n_smem[n]:
                            m = max(k for k in range(n) if units[k][0] == "smem")
                            pool.wait_ge(s_s, m + 1)
                        for b in range(4):
                            c0 = T_P + (4 * u[1] + b) * DT
                            last = nc.gpsimd.tensor_copy(qzm[:, b, :].rearrange("p (h c) -> p h c", h=MEM)[:, :, 0:DT],
                                                         z[:, QM0:QM0 + MEM, c0:c0 + DT])
                        last.then_inc(s_qz, 1)

            def softmax_parts(n):
                k = keys(units[n])
                return [(bank[:, 0:min(512, k - 512 * j)], 512 * j) for j, bank in enumerate(logits(n)) if k > 512 * j]

            @block.vector
            def _(dve):
                def negmax(n):
                    dve.wait_ge(s_s, n + 1)
                    if n >= 2:
                        dve.wait_ge(s_e, n - 1)
                    parts = softmax_parts(n)
                    for j, (src, _) in enumerate(parts):
                        last = nc.vector.reduce_max(stat_a[:, n % 2, j:j + 1], src, AX.X)
                    last.then_inc(s_ng, 1)
                    dve.wait_ge(s_ng, 2 * n + 1)
                    if len(parts) > 1:
                        nc.vector.reduce_max(stat_a[:, n % 2, 3:4], stat_a[:, n % 2, 0:3], AX.X).then_inc(s_ng, 1)
                    else:
                        nc.vector.tensor_copy(stat_a[:, n % 2, 3:4], stat_a[:, n % 2, 0:1]).then_inc(s_ng, 1)
                    dve.wait_ge(s_ng, 2 * n + 2)
                    nc.vector.tensor_scalar(nmax[:, n % 2:n % 2 + 1], stat_a[:, n % 2, 3:4], -SCALE, None, ALU.mult).then_inc(s_m, 1)

                def normalise(n):
                    dve.wait_ge(s_e, n + 1)
                    parts = len(softmax_parts(n))
                    if parts > 1:
                        nc.vector.reduce_sum(rsum[:, n % 2, 3:4], rsum[:, n % 2, 0:parts], AX.X).then_inc(s_rs, 1)
                    else:
                        nc.vector.tensor_copy(rsum[:, n % 2, 3:4], rsum[:, n % 2, 0:1]).then_inc(s_rs, 1)
                    dve.wait_ge(s_rs, 2 * n + 1)
                    nc.vector.reciprocal(rinv[:, n % 2:n % 2 + 1], rsum[:, n % 2, 3:4]).then_inc(s_rs, 1)
                    dve.wait_ge(s_rs, 2 * n + 2)
                    nk = keys(units[n])
                    nc.vector.tensor_scalar(probs[:, n % 2, 0:nk], probs[:, n % 2, 0:nk], rinv[:, n % 2:n % 2 + 1], None,
                                            ALU.mult).then_inc(s_pr, 1)

                def drain(n):
                    kind, h, i = units[n]
                    dve.wait_ge(s_pv, n + 1)
                    if kind in ("fox", "mem"):
                        c = (4 if kind == "fox" else 12) + h
                        nc.vector.tensor_copy(b_t[:, c, i * P:(i + 1) * P], obank[:, 0:P]).then_inc(s_o, 1)
                    else:
                        nb, nh, c = (2, FOX, 4) if kind == "sfox" else (4, MEM, 12)
                        t0 = T_P + h * nb * DT
                        for b in range(nb):
                            last = nc.vector.tensor_copy(b_t[:, c:c + nh, t0 + b * DT:t0 + (b + 1) * DT],
                                                         obank[:, b * nh * DT:(b + 1) * nh * DT].rearrange("p (h t) -> p h t", h=nh))
                        last.then_inc(s_o, 1)

                for n in range(NU + 2):
                    if n < NU:
                        negmax(n)
                    if 1 <= n <= NU:
                        normalise(n - 1)
                    if n >= 2:
                        drain(n - 2)

            @block.scalar
            def _(act):
                for n in range(NU + 1):
                    if n < NU:
                        act.wait_ge(s_m, n + 1)
                        if n >= 2:
                            act.wait_ge(s_t, groups_before[n - 1])
                            act.wait_ge(s_rs, 2 * (n - 1))
                        parts = softmax_parts(n)
                        for j, (src, k0) in enumerate(parts):
                            ins = nc.scalar.activation(probs[:, n % 2, k0:k0 + src.shape[1]], src, ACT.Exp,
                                                       bias=nmax[:, n % 2:n % 2 + 1], scale=SCALE,
                                                       accum_out=rsum[:, n % 2, j:j + 1])
                        ins.then_inc(s_e, 1)
                    if n >= 1:
                        m = n - 1
                        r = P
                        for g in range(t_groups(units[m])):
                            act.wait_ge(s_t, groups_before[m] + g + 1)
                            if m >= 2 and g == 0:
                                act.wait_ge(s_pv, m - 1)
                            nch = min(4, chunks(units[m]) - 4 * g)
                            rows = min(P, keys(units[m]) - 4 * g * P)
                            nc.scalar.activation(p_t[0:rows, m % 2, 4 * g:4 * g + nch, :],
                                                 tbank[0:rows, 0:nch * P].rearrange("p (c t) -> p c t", c=nch),
                                                 ACT.Copy).then_inc(s_tc, 1)

            @block.tensor
            def _(pe):
                def make_logits(n):
                    kind, h, i = units[n]
                    banks = logits(n)
                    if n >= 2:
                        pe.wait_ge(s_e, n - 1)
                    if kind == "fox":
                        nk = keys(units[n])
                        nc.tensor.matmul(banks[0][:, 0:nk], z[:, Q0 + h, i * P:(i + 1) * P], z[:, K0 + h, 0:nk], start=True, stop=False)
                        nc.tensor.matmul(banks[0][:, 0:nk], negsel_p[:, h, :], c_p[:, 0:nk], start=False, stop=False)
                        last = nc.tensor.matmul(banks[0][:, i * P:nk], ident[:], causal[:], start=False, stop=True)
                    elif kind == "mem":
                        last = nc.tensor.matmul(banks[0][:, 0:N_MEM], z[:, QM0 + h, i * P:(i + 1) * P], mk_t[:, h, :], start=True, stop=True)
                    elif kind == "sfox":
                        pe.wait_ge(s_qz, n_samp[n] + 1)
                        for b in range(2):
                            r0 = b * 64
                            for k in range(PAGES):
                                j = pages_before[n] + b * PAGES + k
                                pe.wait_ge(s_kl[j % RING], 16 * (j // RING + 1))
                                dst = banks[k // 4][r0:r0 + 64, (k % 4) * P:(k % 4 + 1) * P]
                                nc.tensor.matmul(dst, negsel_s[:, 2 * h + b, :], c_s[:, k * PAGE:(k + 1) * PAGE], start=True, stop=False)
                                for hh in range(FOX):
                                    last = nc.tensor.matmul(dst, qz[:, b, hh * 64:(hh + 1) * 64], k_ring[:, j % RING, hh * P:(hh + 1) * P],
                                                            start=False, stop=(hh == FOX - 1))
                                last.then_inc(s_ku, 1)
                            dst = banks[2][r0:r0 + 64, 0:T_S]
                            nc.tensor.matmul(dst, ident[0:64, 0:64], smask[:, 2 * h + b, :], start=True, stop=False)
                            nc.tensor.matmul(dst, negsel_s[:, 2 * h + b, :],
                                             c_s[:, PAGES * PAGE:].rearrange("p (o t) -> p o t", o=1).to_broadcast([64, DB, DT]),
                                             start=False, stop=False)
                            for hh in range(FOX):
                                last = nc.tensor.matmul(dst, qz[:, b, hh * 64:(hh + 1) * 64], z[:, K0 + hh, T_P:T],
                                                        start=False, stop=(hh == FOX - 1))
                    else:
                        pe.wait_ge(s_qz, n_samp[n] + 1)
                        for b in range(4):
                            j = pages_before[n] + b
                            pe.wait_ge(s_kl[j % RING], 16 * (j // RING + 1))
                            for hh in range(MEM):
                                last = nc.tensor.matmul(banks[0][b * 32:(b + 1) * 32, 0:N_MEM], qzm[:, b, hh * 32:(hh + 1) * 32],
                                                        k_ring[:, j % RING, hh * N_MEM:(hh + 1) * N_MEM],
                                                        start=(hh == 0), stop=(hh == MEM - 1), tile_position=(0, b * 32))
                            if b < 3:
                                last.then_inc(s_ku, 1)
                    last.then_inc(s_s, 1)
                    if kind == "smem":
                        pe.wait_ge(s_s, n + 1)
                        pe.sem_inc(s_ku, 1)

                def transpose_probs(n):
                    u = units[n]
                    pe.wait_ge(s_pr, n + 1)
                    for g in range(t_groups(u)):
                        if groups_before[n] + g >= 1:
                            pe.wait_ge(s_tc, groups_before[n] + g)
                        for c in range(4 * g, min(4 * g + 4, chunks(u))):
                            w = min(P, keys(u) - c * P)
                            last = nc.tensor.transpose(tbank[0:w, (c % 4) * P:(c % 4 + 1) * P], probs[:, n % 2, c * P:c * P + w], ident[:])
                        last.then_inc(s_t, 1)

                def weigh(n):
                    kind, h, i = units[n]
                    pe.wait_ge(s_tc, groups_before[n + 1])
                    if n >= 1:
                        pe.wait_ge(s_o, n)
                    nch = chunks(units[n])
                    if kind in ("fox", "mem"):
                        v = v_tok if kind == "fox" else mv_tok
                        for c in range(nch):
                            last = nc.tensor.matmul(obank[:, 0:P], v[:, c, h * HD:(h + 1) * HD], p_t[:, n % 2, c, :],
                                                    start=(c == 0), stop=(c == nch - 1))
                    elif kind == "sfox":
                        for b in range(2):
                            for k in range(PAGES + 1):
                                j = pages_before[n] + b * PAGES + k
                                if k < PAGES:
                                    pe.wait_ge(s_vl[j % RING], 16 * (j // RING + 1))
                                for hh in range(FOX):
                                    r0 = b * 64 + hh * DT
                                    if k < PAGES:
                                        l_, r_ = v_ring[:, j % RING, hh * HD:(hh + 1) * HD], p_t[:, n % 2, k, r0:r0 + DT]
                                    else:
                                        l_, r_ = v_tok[0:64, 4, hh * HD:(hh + 1) * HD], p_t[0:64, n % 2, k, r0:r0 + DT]
                                    last = nc.tensor.matmul(obank[:, r0:r0 + DT], l_, r_, start=(b == 0 and k == 0 and hh == 0),
                                                            stop=(b == 1 and k == PAGES and hh == FOX - 1), skip_group_check=True)
                                if k < PAGES:
                                    last.then_inc(s_vu, 1)
                    else:
                        for b in range(4):
                            j = pages_before[n] + b
                            pe.wait_ge(s_vl[j % RING], 16 * (j // RING + 1))
                            for hh in range(MEM):
                                for c in range(2):
                                    r0 = b * 32 + hh * DT
                                    last = nc.tensor.matmul(obank[:, r0:r0 + DT], v_ring[:, j % RING, c * 512 + hh * HD:c * 512 + (hh + 1) * HD],
                                                            p_t[:, n % 2, c, r0:r0 + DT], start=(c == 0), stop=(c == 1))
                            if b < 3:
                                last.then_inc(s_vu, 1)
                    last.then_inc(s_pv, 1)
                    if kind == "smem":
                        pe.wait_ge(s_pv, n + 1)
                        pe.sem_inc(s_vu, 1)

                for n in range(NU + 1):
                    if n < NU:
                        make_logits(n)
                    if n >= 1:
                        transpose_probs(n - 1)
                        weigh(n - 1)

        recycle()

        bt_hi = at("bt_hi", [P, KC, T], F32R, O_Z)
        bt_lo = at("bt_lo", [P, KC, T], F32R, O_Z + KC * T * 4)
        m_hi = at("m_hi", [P, KC, T], F32R, O_R1)
        m_lo = at("m_lo", [P, KC, T], F32R, O_R2)
        g_in = at("g_in", [P, 2, 3, T], F32, O_GB)
        tmp = at("merge_tmp", [P, T], F32, O_GB + 13824)
        merged = at("merged", [P, T], F32, O_Z + 2 * KC * T * 4)
        s_bh = sem("branches_split")
        with nc.Block() as block:
            @block.scalar
            def _(act):
                for g in range(4):
                    nc.scalar.activation(bt_hi[:, 4 * g:4 * g + 4, :], b_t[:, 4 * g:4 * g + 4, :], ACT.Copy).then_inc(s_bh, 1)

            @block.vector
            def _(dve):
                for g in range(4):
                    dve.wait_ge(s_bh, g + 1)
                    nc.vector.tensor_tensor(bt_lo[:, 4 * g:4 * g + 4, :], b_t[:, 4 * g:4 * g + 4, :],
                                            bt_hi[:, 4 * g:4 * g + 4, :].bitcast(F32), ALU.subtract)

        q3 = stream_sems("merge")
        s_gl = [sem(f"gates_loaded{k}") for k in range(2)]
        s_m0, s_m1, s_m2 = sem("pool_branch_taken"), sem("fox_branch_taken"), sem("mem_branch_taken")
        s_mch, s_mrd, s_mh, s_ml = sem("merge_chain"), sem("merged_ready"), sem("merged_hi"), sem("merged_lo")
        with nc.Block() as block:
            @block.sync
            def _(sp):
                load_stripes(sp, a["w_up"], KC, q3)

            @block.gpsimd
            def _(pool):
                for s in range(KC):
                    if s >= 2:
                        pool.wait_ge(s_m2, s)
                    pool.dma_start(g_in[:, s % 2, :, :], gates_dram[3 * s:3 * s + 3, :, :].rearrange("g p t -> p g t")).then_inc(s_gl[s % 2], 16)

            @block.scalar
            def _(act):
                def drain(i, s):
                    act.wait_ge(s_mrd, 2 * i + s + 1)
                    nc.scalar.activation(m_hi[:, bass.ds(2 * i + s, 1), :], merged[:].rearrange("p (o t) -> p o t", o=1), ACT.Copy).then_inc(s_mh, 1)
                lagged(act, KC, lambda i, s: split_hi(act, i, s, q3), drain)

            @block.vector
            def _(dve):
                def two(t_):
                    return t_.rearrange("p (b t) -> p b t", b=2)

                def drain(i, s):
                    n = 2 * i + s
                    par = s % 2
                    dve.wait_ge(q3["mm"], 4 * i + 2 * s + 4)
                    dve.wait_ge(s_gl[par], 16 * (i + s // 2 + 1))
                    dve.wait_ge(s_ml, n + 1)
                    nc.vector.tensor_tensor(two(merged[:]), acc[:, par, :, 0:HALF], two(g_in[:, par, 0, :]), ALU.mult).then_inc(s_m0, 1)
                    nc.vector.tensor_tensor(two(tmp[:]), tps[:, 0:2, 0:HALF], two(g_in[:, par, 1, :]), ALU.mult).then_inc(s_m1, 1)
                    dve.wait_ge(s_m1, n + 2)
                    nc.vector.tensor_tensor(merged[:], merged[:], tmp[:], ALU.add).then_inc(s_mch, 1)
                    dve.wait_ge(s_mch, n + 1)
                    nc.vector.tensor_tensor(two(tmp[:]), tps[:, 2:4, 0:HALF], two(g_in[:, par, 2, :]), ALU.mult).then_inc(s_m2, 1)
                    dve.wait_ge(s_m2, n + 2)
                    nc.vector.tensor_tensor(merged[:], merged[:], tmp[:], ALU.add).then_inc(s_mrd, 1)
                    dve.wait_ge(s_mh, n + 1)
                    nc.vector.tensor_tensor(m_lo[:, bass.ds(n, 1), :], merged[:].rearrange("p (o t) -> p o t", o=1),
                                            m_hi[:, bass.ds(n, 1), :].bitcast(F32), ALU.subtract).then_inc(s_ml, 1)
                lagged(dve, KC, lambda i, s: split_lo(dve, i, s, q3), drain)

            @block.tensor
            def _(pe):
                pe.sem_inc(q3["mm"], 2)
                pe.sem_inc(s_m0, 2)
                pe.sem_inc(s_m1, 1)
                pe.sem_inc(s_m2, 1)
                pe.sem_inc(s_ml, 1)

                def one(i, s):
                    par = s % 2

                    def out(cc, b, cn):
                        if cc < 4:
                            return acc[:, par, b, 0:cn], 0, 3
                        if cc < 12:
                            return tps[:, b, 0:cn], 4, 11
                        return tps[:, 2 + b, 0:cn], 12, KC - 1

                    for h in range(2):
                        pe.wait_ge(q3["lo"], 4 * i + 2 * s + h + 1)
                        if h == 0:
                            pe.wait_ge(s_m0, 2 * i + s + 1)
                            pe.wait_ge(s_m1, 2 * i + s + 1)
                        else:
                            pe.wait_ge(s_m2, 2 * i + s + 1)
                        multiply_half(pe, None, par, h, bt_hi, bt_lo, HALVES, q3, out=out)

                with pe.Fori(0, KC // 2) as i:
                    one(i, 0)
                    one(i, 1)

        recycle()

        O_X1 = O_ATT
        O_T = O_X1 + NBLK * D * 4
        x1 = at("x1", [P, NBLK, D], F32, O_X1)
        mo = at("mo", [P, 2, T], F32, O_T)
        q4 = stream_sems("out")
        s_xl, s_ot, s_oa = sem("x_reloaded"), sem("out_transposed"), sem("out_added")
        with nc.Block() as block:
            @block.sync
            def _(sp):
                load_stripes(sp, a["w_out"], KC, q4)

            @block.gpsimd
            def _(pool):
                pool.dma_start(x1[:, 0:4, :], a["x"][0:T_P, :].rearrange("(b p) d -> p b d", p=P)).then_inc(s_xl, 16)
                pool.dma_start(x1[0:T_S, 4, :], a["x"][T_P:T, :]).then_inc(s_xl, 16)

            @block.scalar
            def _(act):
                def drain(i, s):
                    act.wait_ge(q4["mm"], 4 * i + 2 * s + 4)
                    act.wait_ge(s_ot, 2 * i + s + 1)
                    nc.scalar.activation(mo[:, s % 2, :].rearrange("p (b t) -> p b t", b=2), acc[:, s % 2, :, 0:HALF], ACT.Copy).then_inc(q4["act"], 1)
                lagged(act, KC, lambda i, s: split_hi(act, i, s, q4), drain)

            @block.vector
            def _(dve):
                def drain(i, s):
                    n, par = 2 * i + s, s % 2
                    dve.wait_ge(s_ot, n + 3)
                    dst = x1[:, 0:4, bass.ds(n * P, P)]
                    nc.vector.tensor_tensor(dst, tps[:, 2 * par, :].rearrange("p (b t) -> p b t", b=4), dst, ALU.add)
                    dst = x1[0:T_S, 4, bass.ds(n * P, P)]
                    nc.vector.tensor_tensor(dst, tps[0:T_S, 2 * par + 1, 0:P], dst, ALU.add).then_inc(s_oa, 1)
                dve.wait_ge(s_xl, 32)
                lagged(dve, KC, lambda i, s: split_lo(dve, i, s, q4), drain)

            @block.tensor
            def _(pe):
                def after(i, s):
                    n, par = 2 * i + s, s % 2
                    pe.wait_ge(q4["act"], n + 3)
                    pe.wait_ge(s_oa, n + 1)
                    for b in range(NBLK):
                        dst = tps[:, 2 * par, b * P:(b + 1) * P] if b < 4 else tps[0:T_S, 2 * par + 1, 0:P]
                        last = nc.tensor.transpose(dst, mo[:, par, b * P:b * P + ROWS[b]], ident[:])
                    last.then_inc(s_ot, 1)
                pe.sem_inc(s_ot, 2)
                pe.sem_inc(s_oa, 2)
                multiply_stripes(pe, KC, m_hi, m_lo, HALVES, q4, use=("act",), after=after)

        recycle()

        h_hi = at("h_hi", [P, KC, T], F32R, O_R1)
        h_lo = at("h_lo", [P, KC, T], F32R, O_R2)
        hn = at("hn", [P, 2, D], F32, O_T)
        norm_transposed("ffn", NBLK, ROWS, a["norm_ffn_g"], lambda b: x1[0:ROWS[b], b, :], None, h_hi, h_lo, (ss2, ms2, rstd2), hn)

        qp = at("qp", [P, 2 * PH, T], F32, O_T)
        q5 = stream_sems("peerq")
        act_q, dve_q = drain_to(qp, q5)
        with nc.Block() as block:
            @block.sync
            def _(sp):
                load_stripes(sp, a["w_pq"], 2 * PH, q5)

            @block.scalar
            def _(act):
                lagged(act, 2 * PH, lambda i, s: split_hi(act, i, s, q5), lambda i, s: act_q(act, i, s))

            @block.vector
            def _(dve):
                lagged(dve, 2 * PH, lambda i, s: split_lo(dve, i, s, q5), lambda i, s: dve_q(dve, i, s))

            @block.tensor
            def _(pe):
                multiply_stripes(pe, 2 * PH, h_hi, h_lo, HALVES, q5)

        recycle()

        place = [O_T + 2 * PH * T * 4]

        def then(name, shape, dtype):
            size = int(np.prod(shape[1:])) * 4
            t_ = at(name, shape, dtype, place[0])
            place[0] += (size + 31) // 32 * 32
            return t_

        eidx = at("eidx", [P, NBLK, NEXP], I32, O_MKT)
        gate = at("gate", [P, NBLK, NEXP], F32, O_MKT + NBLK * NEXP * 4)
        sk = then("sk", [P, 2 * PH, NKEY], F32)
        sc = then("sc", [P, 2, 2 * PH, NKEY], F32)
        sc_b = then("sc_b", [P, 2 * PH, NKEY], F32)
        top = then("top", [P, 2 * PH, PTOP], F32)
        tidx = then("tidx", [P, 2 * PH, PTOP], U32)
        tidx_f = then("tidx_f", [P, 2 * PH, PTOP], F32)
        cand = then("cand", [P, PH, PTOP * PTOP], F32)
        cand_b = then("cand_b", [P, PH, PTOP * PTOP], F32)
        best = then("best", [P, PH, PTOP], F32)
        sel = then("sel", [P, PH, PTOP], U32)
        sel_a = then("sel_a", [P, 2, NEXP], U32)
        sel_f = then("sel_f", [P, 2, NEXP], F32)
        onehot = then("onehot", [P, NEXP, PTOP], F32)
        part = then("part", [P, 2, NEXP], F32)
        iota = then("iota16", [P, PTOP], F32)
        ebest = then("ebest", [P, PH, PTOP], F32)
        esum = then("esum", [P, 2, PH], F32)
        s_skl, s_qk, s_qkc, s_dd, s_tk, s_ex = (sem(f"topk_{x}") for x in ("keys_loaded", "scores", "copied", "block_done", "chain", "exps"))
        s_tick = sem("topk_tick")
        LINKS = 21
        with nc.Block() as block:
            @block.sync
            def _(sp):
                sp.dma_start(sk[:], a["subkeys"]).then_inc(s_skl, 16)
                sp.dma_start(iota[:], a["iota16"]).then_inc(s_skl, 16)

            @block.tensor
            def _(pe):
                pe.wait_ge(s_skl, 32)
                for b in range(NBLK):
                    r = ROWS[b]
                    for g in range(4):
                        n = 4 * b + g
                        bank = acc[:, n % 4 // 2, n % 2, :]
                        if n >= 4:
                            pe.wait_ge(s_qkc, n - 3)
                        for k in range(4):
                            last = nc.tensor.matmul(bank[0:r, k * P:(k + 1) * P], qp[:, 4 * g + k, b * P:b * P + r], sk[:, 4 * g + k, :],
                                                    start=True, stop=True)
                        last.then_inc(s_qk, 1)

            @block.scalar
            def _(act):
                for b in range(NBLK + 1):
                    if b < NBLK:
                        if b >= 2:
                            act.wait_ge(s_dd, b - 1)
                        for g in range(4):
                            n = 4 * b + g
                            r = ROWS[b]
                            act.wait_ge(s_qk, n + 1)
                            nc.scalar.activation(sc[0:r, b % 2, 4 * g:4 * g + 4, :],
                                                 acc[0:r, n % 4 // 2, n % 2, :].rearrange("p (k c) -> p k c", k=4), ACT.Copy).then_inc(s_qkc, 1)
                    if b >= 1:
                        r = ROWS[b - 1]
                        act.wait_ge(s_tk, LINKS * (b - 1) + 10)
                        nc.scalar.activation(ebest[0:r], ebest[0:r], ACT.Exp).then_inc(s_ex, 1)

            @block.vector
            def _(dve):
                def topk(b, par, r):
                    count = [0]

                    def link(ins):
                        count[0] += 1
                        ins.then_inc(s_tk, 1)
                        dve.wait_ge(s_tk, LINKS * b + count[0])
                        dve.sem_inc(s_tick, 1)

                    dve.wait_ge(s_qkc, 4 * b + 4)
                    dve.sem_inc(s_tick, 1)
                    for src, src_b, vals, idx, m in ((sc[0:r, par], sc_b[0:r], top[0:r], tidx[0:r], 2 * PH), (cand[0:r], cand_b[0:r], best[0:r], sel[0:r], PH)):
                        if m == PH:
                            tv = top[0:r].rearrange("p (h two) k -> p h two k", two=2)
                            link(nc.vector.tensor_tensor(
                                cand[0:r].rearrange("p h (x y) -> p h x y", x=PTOP),
                                tv[:, :, 0, :].unsqueeze(3).to_broadcast([r, PH, PTOP, PTOP]),
                                tv[:, :, 1, :].unsqueeze(2).to_broadcast([r, PH, PTOP, PTOP]), ALU.add))
                        for h in range(m):
                            last = nc.vector.max(out=vals[:, h, 0:8], in_=src[:, h, :])
                        link(last)
                        for h in range(m):
                            nc.vector.max_index(out=idx[:, h, 0:8], in_max=vals[:, h, 0:8], in_values=src[:, h, :])
                            last = nc.vector.match_replace(out=src_b[:, h, :], in_to_replace=vals[:, h, 0:8], in_values=src[:, h, :], imm_value=-3.0e38)
                        link(last)
                        for h in range(m):
                            last = nc.vector.max(out=vals[:, h, 8:16], in_=src_b[:, h, :])
                        link(last)
                        for h in range(m):
                            last = nc.vector.max_index(out=idx[:, h, 8:16], in_max=vals[:, h, 8:16], in_values=src_b[:, h, :])
                        link(last)
                    link(nc.vector.tensor_tensor(ebest[0:r], best[0:r], best[0:r, :, 0:1].to_broadcast([r, PH, PTOP]), ALU.subtract))
                    sf = sel[0:r].rearrange("p h k -> p (h k)")
                    nc.vector.tensor_scalar(sel_a[0:r, 0], sf, 4, None, ALU.logical_shift_right)
                    link(nc.vector.tensor_scalar(sel_a[0:r, 1], sf, PTOP - 1, None, ALU.bitwise_and))
                    nc.vector.tensor_copy(tidx_f[0:r], tidx[0:r])
                    link(nc.vector.tensor_copy(sel_f[0:r], sel_a[0:r]))
                    for side in range(2):
                        link(nc.vector.tensor_tensor(onehot[0:r], sel_f[0:r, side, :].unsqueeze(2).to_broadcast([r, NEXP, PTOP]),
                                                     iota[0:r].unsqueeze(1).to_broadcast([r, NEXP, PTOP]), ALU.is_equal))
                        oh4 = onehot[0:r].rearrange("p (h k) x -> p h k x", h=PH)
                        lists = tidx_f[0:r].rearrange("p (h two) k -> p h two k", two=2)[:, :, side, :]
                        link(nc.vector.tensor_tensor(oh4, oh4, lists.unsqueeze(2).to_broadcast([r, PH, PTOP, PTOP]), ALU.mult))
                        link(nc.vector.reduce_sum(part[0:r, side, :], onehot[0:r], AX.X))
                    nc.vector.scalar_tensor_tensor(out=eidx[0:r, bass.ds(b, 1), :], in0=part[0:r, 0:1, :], scalar=float(NKEY),
                                                   in1=part[0:r, 1:2, :], op0=ALU.mult, op1=ALU.add)
                    dve.wait_ge(s_ex, b + 1)
                    link(nc.vector.reduce_sum(esum[0:r, 0, :], ebest[0:r], AX.X))
                    link(nc.vector.reciprocal(esum[0:r, 1, :], esum[0:r, 0, :]))
                    link(nc.vector.tensor_tensor(gate[0:r, bass.ds(b, 1), :].rearrange("p o (h k) -> p (o h) k", h=PH), ebest[0:r],
                                                 esum[0:r, 1, :].unsqueeze(2).to_broadcast([r, PH, PTOP]), ALU.mult))
                    assert count[0] == LINKS
                    dve.sem_inc(s_dd, 1)

                dve.wait_ge(s_skl, 32)
                with dve.Fori(0, 2) as i:
                    topk(2 * i, 0, P)
                    topk(2 * i + 1, 1, P)
                topk(4, 0, T_S)

        recycle()

        NSLOT, GRP = 8, 8
        place[0] = O_T
        ring = then("ring", [P, NSLOT, D], F32)
        hrow = then("h_row", [P, D], F32)
        junk = then("junk", [P, D], F32)
        y = then("y", [P, D], F32)
        g_fin = then("g_final", [P, D], F32)
        dots = then("dots", [P, NEXP], F32)
        wts = then("weights", [P, NEXP], F32)
        stage = then("index_stage", [P, 2, GRP], I32)
        fin = then("fin", [P, 8], F32)
        s_gf, s_gat = sem("final_g_loaded"), [sem(f"row_gathered{k}") for k in range(NSLOT)]
        s_used, s_stg, s_dots, s_gel, s_hr, s_fa2, s_fd, s_y, s_w = (sem(f"peer_{x}") for x in (
            "row_used", "indices_staged", "dots_done", "gelu_done", "h_ready", "final_act", "final_dve", "y_stored", "weights_ready"))
        s_ptick, s_vtick = sem("gather_tick"), sem("peer_tick")
        with nc.Block() as block:
            @block.sync
            def _(sp):
                sp.dma_start(g_fin[:], a["norm_final_g"].rearrange("(o d) -> o d", o=1).to_broadcast([P, D])).then_inc(s_gf, 16)

                def store(b, row, r):
                    sp.wait_ge(s_fd, 3 * b + 3)
                    sp.dma_start(a["y"][row, :], y[0:r, :]).then_inc(s_y, 16)
                with sp.Fori(0, 4) as b:
                    store(b, bass.ds(b * P, P), P)
                store(4, slice(T_P, T), T_S)
                sp.wait_ge(s_y, 16 * NBLK)

            @block.gpsimd
            def _(pool):
                pool.sem_inc(s_used, NSLOT)

                def gather(b, r):
                    for t_, table in enumerate(("peer_u", "peer_v")):
                        with pool.Fori(0, NEXP // (2 * GRP)) as i:
                            for s in range(2):
                                n0 = 256 * b + 128 * t_ + 16 * i + 8 * s
                                pool.wait_ge(s_used, n0 + 1)
                                nc.gpsimd.tensor_copy(stage[0:r, s, :], eidx[0:r, bass.ds(b, 1), bass.ds(16 * i + 8 * s, GRP)]
                                                      .rearrange("p o k -> p (o k)")).then_inc(s_stg, 1)
                                pool.wait_ge(s_stg, 32 * b + 16 * t_ + 2 * i + s + 1)
                                for k in range(GRP):
                                    if k:
                                        pool.wait_ge(s_used, n0 + k + 1)
                                    pool.sem_inc(s_ptick, 1)
                                    pool.indirect_dma_start(ring[0:r, k, :], None, a[table],
                                                            bass.IndirectOffsetOnAxis(ap=stage[0:r, s, k:k + 1], axis=0)).then_inc(s_gat[k], 16)
                with pool.Fori(0, 4) as b:
                    gather(b, P)
                gather(4, T_S)

            @block.scalar
            def _(act):
                def block_of(b, r):
                    act.wait_ge(s_dots, b + 1)
                    nc.scalar.activation(dots[0:r], dots[0:r], ACT.Gelu).then_inc(s_gel, 1)
                    act.wait_ge(s_used, 256 * b + 256 + NSLOT)
                    nc.scalar.activation(junk[0:r], x1[0:r, bass.ds(b, 1), :].rearrange("p o d -> p (o d)"), ACT.Square,
                                         accum_out=fin[0:r, 0:1]).then_inc(s_fa2, 1)
                    act.wait_ge(s_fd, 3 * b + 1)
                    nc.scalar.activation(fin[0:r, 1:2], fin[0:r, 1:2], ACT.Sqrt).then_inc(s_fa2, 1)
                with act.Fori(0, 4) as b:
                    block_of(b, P)
                block_of(4, T_S)

            @block.vector
            def _(dve):
                def row(ap):
                    return ap.rearrange("p o d -> p (o d)")

                def block_of(b, r):
                    xr = row(x1[0:r, bass.ds(b, 1), :])
                    nc.vector.scalar_tensor_tensor(out=hrow[0:r], in0=xr, scalar=rstd2[0:r, bass.ds(b, 1)], in1=g_row[0:r],
                                                   op0=ALU.mult, op1=ALU.mult).then_inc(s_hr, 1)
                    dve.wait_ge(s_hr, b + 1)
                    dve.sem_inc(s_vtick, 1)
                    with dve.Fori(0, NEXP // GRP) as i:
                        for k in range(GRP):
                            dve.wait_ge(s_gat[k], 512 * b + 16 * i + 16)
                            ins = nc.vector.scalar_tensor_tensor(out=ring[0:r, k, :], in0=ring[0:r, k, :], scalar=1.0, in1=hrow[0:r], op0=ALU.mult,
                                                                 op1=ALU.mult, accum_out=dots[0:r, bass.ds(8 * i + k, 1)])
                            ins.then_inc(s_used, 1)
                    dve.wait_ge(s_used, 256 * b + 128 + NSLOT)
                    dve.sem_inc(s_dots, 1)
                    dve.wait_ge(s_gel, b + 1)
                    nc.vector.tensor_tensor(wts[0:r], dots[0:r], row(gate[0:r, bass.ds(b, 1), :]), ALU.mult).then_inc(s_w, 1)
                    dve.wait_ge(s_w, b + 1)
                    dve.sem_inc(s_vtick, 1)
                    with dve.Fori(0, NEXP // GRP) as i:
                        for k in range(GRP):
                            dve.wait_ge(s_gat[k], 512 * b + 16 * i + 272)
                            dve.wait_ge(s_used, 256 * b + 128 + 8 * i + k + NSLOT)
                            nc.vector.scalar_tensor_tensor(out=xr, in0=ring[0:r, k, :], scalar=wts[0:r, bass.ds(8 * i + k, 1)], in1=xr,
                                                           op0=ALU.mult, op1=ALU.add).then_inc(s_used, 1)
                    dve.wait_ge(s_fa2, 2 * b + 1)
                    nc.vector.tensor_scalar(fin[0:r, 1:2], fin[0:r, 0:1], 1.0 / D, EPS, ALU.mult, ALU.add).then_inc(s_fd, 1)
                    dve.wait_ge(s_fa2, 2 * b + 2)
                    nc.vector.reciprocal(fin[0:r, 2:3], fin[0:r, 1:2]).then_inc(s_fd, 1)
                    dve.wait_ge(s_fd, 3 * b + 2)
                    dve.wait_ge(s_y, 16 * b) if not isinstance(b, int) or b else None
                    nc.vector.scalar_tensor_tensor(out=y[0:r], in0=xr, scalar=fin[0:r, 2:3], in1=g_fin[0:r], op0=ALU.mult,
                                                   op1=ALU.mult).then_inc(s_fd, 1)

                dve.wait_ge(s_gf, 16)
                with dve.Fori(0, 4) as b:
                    block_of(b, P)
                block_of(4, T_S)


_OUTS = {
    "y": (T, D), "z_out": (P, F0 - K0, T), "mem_out": (P, 2 * MEM, N_MEM), "logf_out": (FOX, T), "state_out": (P, 4, DB, STATE),
}


def _half_stripes(w):
    n = w.shape[1] // P
    return np.ascontiguousarray(w.reshape(2, 8, P, n, P).transpose(3, 0, 2, 1, 4)).reshape(n * 2 * P, 1024)


def _constants():
    ident = np.eye(P, dtype=np.float32)
    negsel_p = np.zeros((FOX, FOX, P), np.float32)
    negsel_s = np.zeros((DB, FOX, DB, FOX, DT), np.float32)
    for h in range(FOX):
        negsel_p[h, h, :] = -1.0 / SCALE
        for b in range(DB):
            negsel_s[b, h, b, h, :] = -1.0 / SCALE
    smask = np.full((FOX, DT, DB, DB, DT), NEG, np.float32)
    for b in range(DB):
        for t in range(DT):
            smask[:, t, b, b, 0:t + 1] = 0.0
    causal = np.where(np.arange(P)[None, :] <= np.arange(P)[:, None], 0.0, NEG).astype(np.float32)
    cnt = np.array([[1.0 / min(t + 1, w) for t in range(16)] for w in WINDOWS], np.float32)
    return {
        "ident": ident, "negsel_p": negsel_p, "negsel_s": negsel_s.reshape(DB * FOX, DB, FOX * DT),
        "smask": smask.reshape(FOX * DT, DB, T_S), "causal": causal,
        "cnt_inv": np.ascontiguousarray(np.broadcast_to(cnt, (P, 4, 16))),
        "iota16": np.ascontiguousarray(np.broadcast_to(np.arange(PTOP, dtype=np.float32), (P, PTOP))),
    }


def kernel(**inputs):
    import concourse.bacc as bacc
    from concourse.bass_utils import run_bass_kernel_spmd

    g = {k: np.asarray(v) for k, v in inputs.items()}
    w_in = g["w_in"][0]
    pw, fw, mw = 512, 1024, 512
    cols = {}
    o = 0
    for name, n in (("u", pw), ("q", fw), ("k", fw), ("v", fw), ("f", FOX), ("qm", mw), ("g", 3 * D)):
        cols[name] = w_in[:, o:o + n]
        o += n
    w_z = np.concatenate([cols["q"], cols["qm"], cols["k"], cols["v"], cols["u"], cols["f"], np.zeros((D, P - FOX), np.float32)], axis=1)
    w_gate = cols["g"].reshape(D, 3, KC, P).transpose(0, 2, 1, 3).reshape(D, 3 * D)
    arrays = {
        "x": np.concatenate([g["x_prompt"].reshape(T_P, D), g["x_sample"].reshape(T_S, D)]),
        "mem_prompt": g["mem_prompt"].reshape(N_MEM, D),
        "w_z": _half_stripes(w_z), "w_gate": _half_stripes(w_gate),
        "w_mem": _half_stripes(np.concatenate([g["w_mem_k"][0], g["w_mem_v"][0]], axis=1)),
        "w_up": _half_stripes(np.concatenate([g["w_up_pool"][0], g["w_up_fox"][0], g["w_up_mem"][0]], axis=0)),
        "w_out": _half_stripes(g["w_out"][0]), "w_pq": _half_stripes(g["w_peer_q"][0]),
        "cache_k": np.ascontiguousarray(g["cache_k"][0].transpose(0, 3, 2, 1)).reshape(N_PHYS * HD, FOX * PAGE),
        "cache_v": g["cache_v"][0].reshape(N_PHYS * PAGE, FOX * HD),
        "cache_logf": np.ascontiguousarray(g["cache_logf"][0].transpose(0, 2, 1)).reshape(N_PHYS * FOX, PAGE),
        "mem_cache_k": np.ascontiguousarray(g["cache_mem_k"][0].transpose(0, 3, 2, 1)).reshape(DB * HD, MEM * N_MEM),
        "mem_cache_v": np.ascontiguousarray(g["cache_mem_v"][0].reshape(DB, 2, P, MEM * HD).transpose(0, 2, 1, 3)).reshape(DB * P, 2 * MEM * HD),
        "state_pool": np.ascontiguousarray(g["state_pool"][0].reshape(DB, STATE, 4, P).transpose(3, 2, 0, 1)),
        "page_table": g["page_table"].reshape(1, DB * PAGES),
        "pool_w": np.ascontiguousarray(g["pool_w"][0].transpose(1, 0, 2)),
        "pool_scale": np.ascontiguousarray(g["pool_scale"][0].reshape(4, P).T),
        "b_f": g["b_f"].reshape(FOX, 1),
        "subkeys": np.ascontiguousarray(g["peer_subkeys"][0].transpose(3, 0, 1, 2)).reshape(P, 2 * PH, NKEY),
        "peer_u": g["peer_u"][0], "peer_v": g["peer_v"][0],
        "norm_mix_g": g["norm_mix_g"][0], "mem_norm_g": g["mem_norm_g"][0], "norm_ffn_g": g["norm_ffn_g"][0],
        "norm_final_g": g["norm_final_g"],
        **_constants(),
    }
    nc = bacc.Bacc("TRN2", target_bir_lowering=False, num_devices=1)
    a, given = {}, {}
    for name, x in arrays.items():
        x = np.ascontiguousarray(x)
        given["in_" + name] = x
        a[name] = nc.dram_tensor("in_" + name, x.shape, mybir.dt.from_np(x.dtype), kind="ExternalInput").ap()
    for name, shape in _OUTS.items():
        a[name] = nc.dram_tensor("out_" + name, shape, F32, kind="ExternalOutput").ap()
    build(nc, a)
    r = run_bass_kernel_spmd(nc, [given], core_ids=[0]).results[0]
    y, zo, mo, lf, st = (np.asarray(r["out_" + n]) for n in _OUTS)

    def rows(z_part, t0, t1):
        return np.ascontiguousarray(z_part[:, :, t0:t1].transpose(2, 1, 0)).reshape(t1 - t0, -1)

    k, v, u = zo[:, 0:8], zo[:, 8:16], zo[:, 16:20]
    return (
        y[0:T_P].reshape(1, T_P, D), y[T_P:T].reshape(DB, DT, D),
        rows(k, 0, T_P).reshape(1, 1, T_P, FOX, HD), rows(v, 0, T_P).reshape(1, 1, T_P, FOX, HD),
        np.ascontiguousarray(lf[:, 0:T_P].T).reshape(1, 1, T_P, FOX),
        rows(u, T_P - STATE, T_P).reshape(1, 1, STATE, 512),
        rows(mo[:, 0:MEM], 0, N_MEM).reshape(1, 1, N_MEM, MEM, HD), rows(mo[:, MEM:], 0, N_MEM).reshape(1, 1, N_MEM, MEM, HD),
        rows(k, T_P, T).reshape(1, DB, DT, FOX, HD), rows(v, T_P, T).reshape(1, DB, DT, FOX, HD),
        np.ascontiguousarray(lf[:, T_P:T].T).reshape(1, DB, DT, FOX),
        np.ascontiguousarray(st.transpose(2, 3, 1, 0)).reshape(1, DB, STATE, 512),
    )
```

```python
import numpy as np
from contextlib import ExitStack

import concourse.bass as bass
from concourse import mybir

F32, F32R, I32, U32 = mybir.dt.float32, mybir.dt.float32r, mybir.dt.int32, mybir.dt.uint32
ACT, ALU, AX = mybir.ActivationFunctionType, mybir.AluOpType, mybir.AxisListType

D = 2048
P = 128
KC = D // P
T_P, T_S = 512, 64
T = T_P + T_S
HALF = T // 2
NBLK = 5
ROWS = [128, 128, 128, 128, 64]
DB, DT = 8, 8
FOX, MEM, HD = 8, 4, 128
N_MEM = 256
PAGES, PAGE = 8, 128
N_PHYS = 80
WINDOWS = (2, 4, 8, 16)
STATE = 15
SCALE = float(HD) ** -0.5
EPS = 1e-6
NEG = -1e30
PH, PK, PTOP, NKEY = 8, 16, 16, 128
NEXP = PH * PTOP
N_EXPERTS = NKEY * NKEY
NTILE = N_EXPERTS // P
ND = T - P
GRP = 8
Q0, QM0, K0, V0, U0, F0, NZ = 0, 8, 12, 20, 28, 32, 33
NGATE = 3 * KC
RING = 6

BASE = 16512
O_IDENT, O_SMALL, O_MKT, O_MVTOK, O_GB, O_ATT, O_Z, O_R1 = 0, 512, 1536, 5632, 9728, 17920, 27168, 103200
O_R2, O_W = O_R1 + KC * T * 4, O_R1 + 2 * KC * T * 4


def build(nc, a):
    ctx = ExitStack()

    def at(name, shape, dtype, offset):
        return nc.alloc_sbuf_tensor_at(name, shape, dtype, offset=BASE + offset)

    live = []

    def sem(name):
        live.append(nc.alloc_semaphore(name=name))
        return live[-1]

    def recycle():
        nc.clear_and_free_semaphores(live)
        live.clear()
        nc.all_engine_barrier()

    with ctx:
        gates_dram = nc.dram_tensor("gates_scratch", [NGATE, P, T], F32, kind="Internal").ap()
        acts_dram = nc.dram_tensor("activations_scratch", [NTILE, P, ND], F32, kind="Internal").ap()
        route_dram = nc.dram_tensor("routes_scratch", [N_EXPERTS * ND, 1], F32, kind="Internal").ap()

        ident = at("ident", [P, P], F32, O_IDENT)
        small = at("small", [P, 64], F32, O_SMALL)
        b_f, pool_scale = small[0:FOX, 0:1], small[:, 4:8]
        ss, ms, rstd = small[:, 8:13], small[:, 16:21], small[:, 24:29]
        ss_m, ms_m, rstd_m = small[:, 32:34], small[:, 36:38], small[:, 40:42]
        ss2, ms2, rstd2 = small[:, 44:49], small[:, 50:55], small[:, 56:61]
        mk_t = at("mk_t", [P, MEM, N_MEM], F32, O_MKT)
        mv_tok = at("mv_tok", [P, 2, MEM * HD], F32, O_MVTOK)
        g_row = at("g_row", [P, D], F32, O_GB)

        raw = at("w_raw", [P, 4, 1024], F32, O_W)
        w_hi = at("w_hi", [P, 2, 1024], F32R, O_W + 16384)
        w_lo = at("w_lo", [P, 2, 1024], F32R, O_W + 24576)

        acc = ctx.enter_context(nc.psum_tensor("acc", [P, 2, 2, 512], F32))
        tps = ctx.enter_context(nc.psum_tensor("tps", [P, 4, 512], F32))

        def stream_sems(tag):
            return dict(loaded=[sem(f"{tag}_w_loaded{k}") for k in range(4)], hi=sem(f"{tag}_hi_ready"),
                        lo=sem(f"{tag}_lo_ready"), mm=sem(f"{tag}_half_done"),
                        act=sem(f"{tag}_act_drained"), dve=sem(f"{tag}_dve_drained"))

        def load_stripes(sp, w, n, q):
            nj = 2 * n
            for j in range(4):
                sp.dma_start(raw[:, j, :], w[j * P:(j + 1) * P, :]).then_inc(q["loaded"][j], 16)
            with sp.Fori(1, nj // 4) as i:
                for k in range(4):
                    sp.wait_ge(q["lo"], 4 * i + k - 3)
                    sp.dma_start(raw[:, k, :], w[bass.ds((4 * i + k) * P, P), :]).then_inc(q["loaded"][k], 16)
            for j in range(nj // 4 * 4, nj):
                sp.wait_ge(q["lo"], j - 3)
                sp.dma_start(raw[:, j % 4, :], w[j * P:(j + 1) * P, :]).then_inc(q["loaded"][j % 4], 16)

        def split_hi(act, i, s, q):
            for h in range(2):
                j = 2 * s + h
                act.wait_ge(q["loaded"][j % 4], 16 * (i + j // 4 + 1))
                act.wait_ge(q["mm"], 4 * i + j + 1)
                nc.scalar.activation(w_hi[:, h, :], raw[:, j % 4, :], ACT.Copy).then_inc(q["hi"], 1)

        def split_lo(dve, i, s, q):
            for h in range(2):
                j = 2 * s + h
                dve.wait_ge(q["loaded"][j % 4], 16 * (i + j // 4 + 1))
                dve.wait_ge(q["hi"], 4 * i + j + 1)
                nc.vector.tensor_tensor(w_lo[:, h, :], raw[:, j % 4, :], w_hi[:, h, :].bitcast(F32),
                                        ALU.subtract).then_inc(q["lo"], 1)

        def lagged(eng, n, split, drain):
            split(0, 0)
            pairs = (n - 1) // 2
            with eng.Fori(0, pairs) as i:
                split(i, 1)
                drain(i, 0)
                split(i, 2)
                drain(i, 1)
            if n % 2 == 0:
                split(pairs, 1)
                drain(pairs, 0)
                drain(pairs, 1)
            else:
                drain(pairs, 0)

        def multiply_half(pe, par, h, x_hi, x_lo, cols, q, out=None, before=None):
            for c in range(8):
                cc = 8 * h + c
                if before:
                    before(cc)
                wh, wl = w_hi[:, h, c * P:(c + 1) * P], w_lo[:, h, c * P:(c + 1) * P]
                for (p_, l_, r_) in ((0, wh, x_hi), (1, wh, x_lo), (2, wl, x_hi)):
                    for b, (c0, cn) in enumerate(cols):
                        dst, first, last_c = out(cc, b, cn) if out else (acc[:, par, b, 0:cn], 0, KC - 1)
                        last = nc.tensor.matmul(dst, l_, r_[:, cc, c0:c0 + cn],
                                                start=(cc == first and p_ == 0),
                                                stop=(cc == last_c and p_ == 2))
            last.then_inc(q["mm"], 1)

        HALVES = [(0, HALF), (HALF, HALF)]

        def multiply_stripes(pe, n, x_hi, x_lo, cols, q, use=("act", "dve"), between=None):
            def one(i, s, mid=True):
                for h in range(2):
                    pe.wait_ge(q["lo"], 4 * i + 2 * s + h + 1)
                    if h == 0:
                        for u in use:
                            pe.wait_ge(q[u], 2 * i + s + 1)
                    elif between and mid:
                        between(i, s - 1)
                    multiply_half(pe, s % 2, h, x_hi, x_lo, cols, q)

            pe.sem_inc(q["mm"], 2)
            for u in use:
                pe.sem_inc(q[u], 2)
            one(0, 0, mid=False)
            pairs = (n - 1) // 2
            with pe.Fori(0, pairs) as i:
                one(i, 1)
                one(i, 2)
            if n % 2 == 0:
                one(pairs, 1)
            if between:
                between(pairs, (n - 1) % 2)

        def norm_transposed(tag, n_blk, rows, g_in, x_of, load, x_hi, x_lo, stat, xn):
            ss_, ms_, r_ = stat
            s_g, s_sq, s_ms, s_rt, s_r, s_xn = (sem(f"{tag}_{x}") for x in ("g_loaded", "squared", "mean", "root", "rstd", "normed"))
            s_tp, s_hi, s_lo = (sem(f"{tag}_{x}") for x in ("transposed", "hi_out", "lo_out"))
            s_x = [sem(f"{tag}_x_loaded{k}") for k in range(2)] if load else None
            with nc.Block() as block:
                @block.sync
                def _(sp):
                    sp.dma_start(g_row[:], g_in.rearrange("(o d) -> o d", o=1).to_broadcast([P, D])).then_inc(s_g, 16)
                    if tag == "mem":
                        for dst, name in ((ident[:], "ident"), (pool_scale, "pool_scale"), (b_f, "b_f")):
                            sp.dma_start(dst, a[name]).then_inc(s_g, 16)
                    if load:
                        for b in range(n_blk):
                            if b >= 2:
                                sp.wait_ge(s_xn, b - 1)
                            sp.dma_start(x_of(b), load(b)).then_inc(s_x[b % 2], 16)

                @block.scalar
                def _(act):
                    def squares(b):
                        if load:
                            act.wait_ge(s_x[b % 2], 16 * (b // 2 + 1))
                        if b >= 2:
                            act.wait_ge(s_tp, 4 * (b - 1))
                        nc.scalar.activation(xn[0:rows[b], b % 2, :], x_of(b), ACT.Square,
                                             accum_out=ss_[0:rows[b], b:b + 1]).then_inc(s_sq, 1)
                        act.wait_ge(s_ms, b + 1)
                        nc.scalar.activation(ms_[0:rows[b], b:b + 1], ms_[0:rows[b], b:b + 1], ACT.Sqrt).then_inc(s_rt, 1)

                    squares(0)
                    for b in range(n_blk):
                        if b + 1 < n_blk:
                            squares(b + 1)
                        for g in range(4):
                            act.wait_ge(s_tp, 4 * b + g + 1)
                            nc.scalar.activation(x_hi[:, 4 * g:4 * g + 4, b * P:b * P + rows[b]],
                                                 tps[:, g, 0:4 * rows[b]].rearrange("p (c t) -> p c t", c=4),
                                                 ACT.Copy).then_inc(s_hi, 1)

                @block.vector
                def _(dve):
                    def norm(b):
                        n = rows[b]
                        dve.wait_ge(s_sq, b + 1)
                        nc.vector.tensor_scalar(ms_[0:n, b:b + 1], ss_[0:n, b:b + 1], 1.0 / D, EPS, ALU.mult,
                                                ALU.add).then_inc(s_ms, 1)
                        dve.wait_ge(s_rt, b + 1)
                        nc.vector.reciprocal(r_[0:n, b:b + 1], ms_[0:n, b:b + 1]).then_inc(s_r, 1)
                        dve.wait_ge(s_r, b + 1)
                        nc.vector.scalar_tensor_tensor(out=xn[0:n, b % 2, :], in0=x_of(b), scalar=r_[0:n, b:b + 1],
                                                       in1=g_row[0:n, :], op0=ALU.mult, op1=ALU.mult).then_inc(s_xn, 1)

                    dve.wait_ge(s_g, 64 if tag == "mem" else 16)
                    norm(0)
                    for b in range(n_blk):
                        if b + 1 < n_blk:
                            norm(b + 1)
                        for g in range(4):
                            dve.wait_ge(s_hi, 4 * b + g + 1)
                            nc.vector.tensor_tensor(x_lo[:, 4 * g:4 * g + 4, b * P:b * P + rows[b]],
                                                    tps[:, g, 0:4 * rows[b]].rearrange("p (c t) -> p c t", c=4),
                                                    x_hi[:, 4 * g:4 * g + 4, b * P:b * P + rows[b]].bitcast(F32),
                                                    ALU.subtract).then_inc(s_lo, 1)

                @block.tensor
                def _(pe):
                    pe.wait_ge(s_g, 64 if tag == "mem" else 16)
                    for b in range(n_blk):
                        n = rows[b]
                        pe.wait_ge(s_xn, b + 1)
                        for g in range(4):
                            if b >= 1:
                                pe.wait_ge(s_lo, 4 * (b - 1) + g + 1)
                            for c in range(4):
                                last = nc.tensor.transpose(tps[:, g, c * n:(c + 1) * n],
                                                           xn[0:n, b % 2, (4 * g + c) * P:(4 * g + c + 1) * P],
                                                           ident[0:n, 0:n])
                            last.then_inc(s_tp, 1)

        z = at("z", [P, NZ, T], F32, O_Z)
        xb_m = at("xb_m", [P, 2, D], F32, O_Z)
        xn_m = at("xn_m", [P, 2, D], F32, O_Z + 16384)
        mn_hi = at("mn_hi", [P, KC, N_MEM], F32R, O_R1)
        mn_lo = at("mn_lo", [P, KC, N_MEM], F32R, O_R2)
        norm_transposed("mem", 2, [128, 128], a["mem_norm_g"], lambda b: xb_m[:, b % 2, :],
                        lambda b: a["mem_prompt"][b * P:(b + 1) * P, :], mn_hi, mn_lo, (ss_m, ms_m, rstd_m), xn_m)

        mkv_t = at("mkv_t", [P, 2 * MEM, N_MEM], F32, O_Z)
        q = stream_sems("mem")
        s_vt, s_vo, s_mout = sem("mem_v_transposed"), sem("mem_v_copied"), sem("mem_stored")
        with nc.Block() as block:
            @block.sync
            def _(sp):
                load_stripes(sp, a["w_mem"], 2 * MEM, q)
                sp.wait_ge(q["act"], 2 + 2 * MEM)
                sp.dma_start(a["mem_out"], mkv_t[:]).then_inc(s_mout, 16)
                sp.wait_ge(s_mout, 16)

            def drain_mem(act, i, s):
                act.wait_ge(q["mm"], 4 * i + 2 * s + 4)
                nc.scalar.activation(mkv_t[:, bass.ds(2 * i + s, 1), :], acc[:, s % 2, 0:1, 0:N_MEM], ACT.Copy).then_inc(q["act"], 1)

            @block.scalar
            def _(act):
                lagged(act, 2 * MEM, lambda i, s: split_hi(act, i, s, q), lambda i, s: drain_mem(act, i, s))
                act.wait_ge(q["act"], 2 + MEM)
                nc.scalar.activation(mk_t[:], mkv_t[:, 0:MEM, :], ACT.Copy)

            @block.vector
            def _(dve):
                with dve.Fori(0, MEM) as i:
                    split_lo(dve, i, 0, q)
                    split_lo(dve, i, 1, q)
                for m in range(2):
                    dve.wait_ge(s_vt, m + 1)
                    nc.vector.tensor_copy(mv_tok[:, m, :], tps[:, m, :]).then_inc(s_vo, 1)

            @block.tensor
            def _(pe):
                multiply_stripes(pe, 2 * MEM, mn_hi, mn_lo, [(0, N_MEM)], q, use=("act",))
                pe.wait_ge(q["act"], 2 + 2 * MEM)
                for m in range(2):
                    for h in range(MEM):
                        last = nc.tensor.transpose(tps[:, m, h * P:(h + 1) * P], mkv_t[:, MEM + h, m * P:(m + 1) * P], ident[:])
                    last.then_inc(s_vt, 1)

        recycle()

        x_hi = at("x_hi", [P, KC, T], F32R, O_R1)
        x_lo = at("x_lo", [P, KC, T], F32R, O_R2)
        xb = at("xb", [P, 2, D], F32, O_Z)
        xn = at("xn", [P, 2, D], F32, O_Z + 16384)
        norm_transposed("mix", NBLK, ROWS, a["norm_mix_g"], lambda b: xb[0:ROWS[b], b % 2, :],
                        lambda b: a["x"][b * P:b * P + ROWS[b], :], x_hi, x_lo, (ss, ms, rstd), xn)

        def drain_to(dst_t, q):
            def by_act(act, i, s):
                act.wait_ge(q["mm"], 4 * i + 2 * s + 4)
                nc.scalar.activation(dst_t[:, bass.ds(2 * i + s, 1), 0:HALF], acc[:, s % 2, 0, 0:HALF], ACT.Copy).then_inc(q["act"], 1)

            def by_dve(dve, i, s):
                dve.wait_ge(q["mm"], 4 * i + 2 * s + 4)
                nc.vector.tensor_copy(dst_t[:, bass.ds(2 * i + s, 1), HALF:T], acc[:, s % 2, 1, 0:HALF]).then_inc(q["dve"], 1)
            return by_act, by_dve

        q1 = stream_sems("proj")
        act_z, dve_z = drain_to(z, q1)
        with nc.Block() as block:
            @block.sync
            def _(sp):
                load_stripes(sp, a["w_z"], NZ, q1)

            @block.scalar
            def _(act):
                lagged(act, NZ, lambda i, s: split_hi(act, i, s, q1), lambda i, s: act_z(act, i, s))

            @block.vector
            def _(dve):
                lagged(dve, NZ, lambda i, s: split_lo(dve, i, s, q1), lambda i, s: dve_z(dve, i, s))

            @block.tensor
            def _(pe):
                multiply_stripes(pe, NZ, x_hi, x_lo, HALVES, q1)

        gate_out = at("gate_out", [P, 2, T], F32, O_GB)
        q2 = stream_sems("gate")
        s_gfree, s_gst, s_zst = sem("gate_buffer_free"), sem("gate_stored"), sem("z_stored")
        with nc.Block() as block:
            @block.sync
            def _(sp):
                load_stripes(sp, a["w_gate"], NGATE, q2)

            @block.gpsimd
            def _(pool):
                pool.sem_inc(s_gfree, 2)
                pool.dma_start(a["z_out"], z[:, K0:F0, :]).then_inc(s_zst, 16)
                with pool.Fori(0, NGATE // 2) as i:
                    for s in range(2):
                        pool.wait_ge(q2["act"], 2 * i + s + 3)
                        pool.dma_start(gates_dram[bass.ds(2 * i + s, 1), :, :].rearrange("o p t -> p (o t)"),
                                       gate_out[:, s, :]).then_inc(s_gst, 16)
                        pool.wait_ge(s_gst, 32 * i + 16 * s + 16)
                        pool.sem_inc(s_gfree, 1)
                pool.wait_ge(s_zst, 16)

            def drain_gate(act, i, s):
                act.wait_ge(q2["mm"], 4 * i + 2 * s + 4)
                act.wait_ge(s_gfree, 2 * i + s + 1)
                nc.scalar.activation(gate_out[:, s % 2, :].rearrange("p (b t) -> p b t", b=2), acc[:, s % 2, :, 0:HALF],
                                     ACT.Sigmoid).then_inc(q2["act"], 1)

            @block.scalar
            def _(act):
                lagged(act, NGATE, lambda i, s: split_hi(act, i, s, q2), lambda i, s: drain_gate(act, i, s))

            @block.vector
            def _(dve):
                with dve.Fori(0, NGATE // 2) as i:
                    split_lo(dve, i, 0, q2)
                    split_lo(dve, i, 1, q2)

            @block.tensor
            def _(pe):
                multiply_stripes(pe, NGATE, x_hi, x_lo, HALVES, q2, use=("act",))

        recycle()

        O_CAUS, O_LF, O_CP, O_CS, O_CNT = O_ATT, O_ATT + 512, O_ATT + 2816, O_ATT + 4864, O_ATT + 8992
        negsel_p = at("negsel_p", [FOX, FOX, P], F32, O_GB)
        negsel_s = at("negsel_s", [DB * FOX, DB, FOX * DT], F32, O_GB + 4096)
        smask = at("smask", [FOX * DT, DB, T_S], F32, O_GB + 6144)
        causal = at("causal", [P, P], F32, O_CAUS)
        logf = at("logf", [FOX, T], F32, O_LF)
        c_p = at("c_p", [FOX, T_P], F32, O_CP)
        c_s = at("c_s", [DB * FOX, PAGES * PAGE + DT], F32, O_CS)
        cnt_inv = at("cnt_inv", [P, 4, 16], F32, O_CNT)
        b_t = at("b_t", [P, KC, T], F32, O_R1)
        v_tok = at("v_tok", [P, NBLK, FOX * HD], F32, O_R2)
        O_K = O_R2 + NBLK * FOX * HD * 4
        PW, SW = 16 + T_P, 24
        ua = at("ua", [P, PW + DB * SW], F32, O_K)
        ub = at("ub", [P, PW + DB * SW], F32, O_K + 2880)
        uc = at("uc", [P, PW + DB * SW], F32, O_K + 5760)
        pooled = at("pooled", [P, T], F32, O_K + 8640)
        pool_w = at("pool_w", [P, 4, P], F32, O_K + 11008)
        ones = at("ones", [DB * FOX, PAGES * PAGE + DT], F32, O_K + 13120)
        lf_raw = at("lf_raw", [DB * FOX, PAGES * PAGE + DT], F32, O_K + 17280)
        lt1 = at("lt1", [FOX, T], F32, O_K + 21440)
        lt2 = at("lt2", [FOX, T], F32, O_K + 23808)
        pt = at("pt", [1, DB * PAGES], I32, O_SMALL + 512)
        st_buf = at("state_buf", [P, 4, DB, STATE], F32, O_W + 20000)
        st_new = at("state_new", [P, 4, DB, STATE], F32, O_W + 22016)
        t16 = at("pool_head", [P, 16], F32, O_W + 24000)

        s_pc, s_pt, s_plf, s_pln, s_lfo = (sem(f"prep_{x}") for x in ("consts", "page_table", "past_logf", "new_logf", "logf_stored"))
        s_fa, s_fv, s_init = sem("prep_logf_act"), sem("prep_logf_dve"), sem("prep_cleared")
        s_un, s_st, s_pd, s_ym, s_yo = (sem(f"pool_{x}") for x in ("chain", "state_loaded", "pooled", "mixed", "drained"))
        s_sn = sem("state_assembled")
        s_vtp, s_vtc = sem("v_transposed"), sem("v_copied")
        with nc.Block() as block:
            @block.sync
            def _(sp):
                sp.dma_start(pt[:], a["page_table"]).then_inc(s_pt, 16)
                for dst, name in ((negsel_p[:], "negsel_p"), (negsel_s[:], "negsel_s"), (smask[:], "smask"), (causal[:], "causal"),
                                  (cnt_inv[:], "cnt_inv"), (pool_w[:], "pool_w")):
                    sp.dma_start(dst, a[name]).then_inc(s_pc, 16)
                sp.dma_start(st_buf[:], a["state_pool"]).then_inc(s_st, 16)
                sp.wait_ge(s_pt, 16)
                for b in range(DB):
                    for j in range(PAGES):
                        page = sp.value_load(pt[0:1, b * PAGES + j:b * PAGES + j + 1], min_val=0, max_val=N_PHYS - 1)
                        sp.dma_start(lf_raw[b * FOX:(b + 1) * FOX, j * PAGE:(j + 1) * PAGE],
                                     a["cache_logf"][bass.ds(page * FOX, FOX), :]).then_inc(s_plf, 16)

            @block.gpsimd
            def _(pool):
                nc.gpsimd.memset(ones[:], 1.0).then_inc(s_init, 1)
                pool.wait_ge(s_st, 16)
                for g in range(4):
                    nc.gpsimd.tensor_copy(st_new[:, g, :, 0:STATE - DT], st_buf[:, g, :, DT:STATE])
                    last = nc.gpsimd.tensor_copy(st_new[:, g, :, STATE - DT:STATE],
                                                 z[:, U0 + g, T_P:T].rearrange("p (b t) -> p b t", b=DB))
                last.then_inc(s_sn, 1)
                pool.wait_ge(s_sn, 1)
                pool.dma_start(a["state_out"], st_new[:]).then_inc(s_lfo, 16)
                pool.wait_ge(s_fv, 3)
                pool.dma_start(a["logf_out"], logf[:]).then_inc(s_lfo, 16)
                for b in range(DB):
                    pool.dma_start(lf_raw[b * FOX:(b + 1) * FOX, PAGES * PAGE:],
                                   logf[:, T_P + b * DT:T_P + (b + 1) * DT]).then_inc(s_pln, 16)
                pool.wait_ge(s_lfo, 32)

            @block.scalar
            def _(act):
                act.wait_ge(s_fv, 1)
                nc.scalar.activation(lt2[:], lt1[:], ACT.Abs).then_inc(s_fa, 1)
                act.wait_ge(s_fa, 1)
                nc.scalar.activation(lt2[:], lt2[:], ACT.Exp, scale=-1.0).then_inc(s_fa, 1)
                act.wait_ge(s_fa, 2)
                act.wait_ge(s_fv, 2)
                nc.scalar.activation(lt2[:], lt2[:], ACT.Ln, bias=1.0).then_inc(s_fa, 1)
                for n in range(2 * NBLK):
                    r = ROWS[n // 2]
                    act.wait_ge(s_vtp, n + 1)
                    nc.scalar.activation(v_tok[0:r, n // 2, (n % 2) * 512:(n % 2 + 1) * 512], tps[0:r, n % 2, :],
                                         ACT.Copy).then_inc(s_vtc, 1)

            @block.vector
            def _(dve):
                chain = [0]

                def link(ins):
                    chain[0] += 1
                    ins.then_inc(s_un, 1)
                    dve.wait_ge(s_un, chain[0])

                nc.vector.tensor_scalar(lt1[:], z[0:FOX, F0, :], b_f, None, ALU.add).then_inc(s_fv, 1)
                dve.wait_ge(s_fa, 1)
                nc.vector.tensor_scalar(lt1[:], lt1[:], 0.0, None, ALU.min).then_inc(s_fv, 1)
                dve.wait_ge(s_fa, 3)
                dve.wait_ge(s_fv, 2)
                nc.vector.tensor_tensor(logf[:], lt1[:], lt2[:], ALU.subtract).then_inc(s_fv, 1)
                dve.wait_ge(s_fv, 3)
                dve.wait_ge(s_init, 1)
                nc.vector.tensor_tensor_scan(c_p[:], ones[0:FOX, 0:T_P], logf[:, 0:T_P], 0.0, ALU.mult, ALU.add)
                link(nc.vector.memset(ua[:, 0:16], 0.0))
                dve.wait_ge(s_pc, 96)
                dve.wait_ge(s_st, 16)
                for g, w in enumerate(WINDOWS):
                    u = z[:, U0 + g, :]
                    u_s = u[:, T_P:T].rearrange("p (b t) -> p b t", b=DB)
                    nc.vector.tensor_copy(ua[:, 16:PW], u[:, 0:T_P])
                    nc.vector.tensor_copy(ua[:, PW:].rearrange("p (b c) -> p b c", b=DB)[:, :, 16:SW], u_s)
                    link(nc.vector.tensor_copy(ua[:, PW:].rearrange("p (b c) -> p b c", b=DB)[:, :, 1:16], st_buf[:, g]))
                    src, sh = ua, 1
                    lo = 1
                    while sh < w:
                        dst = ub if src is not ub else uc
                        s3 = src[:, PW:].rearrange("p (b c) -> p b c", b=DB)
                        d3 = dst[:, PW:].rearrange("p (b c) -> p b c", b=DB)
                        nc.vector.tensor_tensor(dst[:, lo + sh - 1:PW], src[:, lo + sh - 1:PW], src[:, lo - 1:PW - sh], ALU.add)
                        link(nc.vector.tensor_tensor(d3[:, :, lo + sh:SW], s3[:, :, lo + sh:SW], s3[:, :, lo:SW - sh], ALU.add))
                        src, lo, sh = dst, lo + sh, 2 * sh
                    if g >= 1:
                        dve.wait_ge(s_ym, g)
                    link(nc.vector.tensor_tensor(t16[:], src[:, 16:32], cnt_inv[:, g, :], ALU.mult))
                    nc.vector.tensor_tensor(pooled[:, 0:16], t16[:], u[:, 0:16], ALU.subtract)
                    nc.vector.scalar_tensor_tensor(out=pooled[:, 16:T_P], in0=src[:, 32:PW], scalar=1.0 / w, in1=u[:, 16:T_P],
                                                   op0=ALU.mult, op1=ALU.subtract)
                    nc.vector.scalar_tensor_tensor(out=pooled[:, T_P:T].rearrange("p (b t) -> p b t", b=DB),
                                                   in0=src[:, PW:].rearrange("p (b c) -> p b c", b=DB)[:, :, 16:SW],
                                                   scalar=1.0 / w, in1=u_s, op0=ALU.mult, op1=ALU.subtract).then_inc(s_pd, 1)
                    dve.wait_ge(s_ym, g + 1)
                    nc.vector.tensor_scalar(b_t[:, g, :].rearrange("p (b t) -> p b t", b=2), acc[:, 0, :, 0:HALF],
                                            pool_scale[:, g:g + 1], None, ALU.mult).then_inc(s_yo, 1)
                dve.wait_ge(s_plf, 16 * DB * PAGES)
                dve.wait_ge(s_pln, 16 * DB)
                nc.vector.tensor_tensor_scan(c_s[:], ones[:], lf_raw[:], 0.0, ALU.mult, ALU.add)

            @block.tensor
            def _(pe):
                for n in range(2 * NBLK):
                    r = ROWS[n // 2]
                    if n >= 2:
                        pe.wait_ge(s_vtc, n - 1)
                    for k in range(4):
                        c0 = (n // 2) * P
                        last = nc.tensor.transpose(tps[0:r, n % 2, k * P:(k + 1) * P], z[:, V0 + 4 * (n % 2) + k, c0:c0 + r], ident[:])
                    last.then_inc(s_vtp, 1)
                pe.wait_ge(s_pc, 96)
                for g in range(4):
                    pe.wait_ge(s_pd, g + 1)
                    if g >= 1:
                        pe.wait_ge(s_yo, g)
                    for b in range(2):
                        last = nc.tensor.matmul(acc[:, 0, b, 0:HALF], pool_w[:, g, :], pooled[:, b * HALF:(b + 1) * HALF],
                                                start=True, stop=True)
                    last.then_inc(s_ym, 1)

        recycle()

        k_ring = at("k_ring", [P, RING, 1024], F32, O_K)
        v_ring = at("v_ring", [P, RING, 1024], F32, O_Z + V0 * T * 4)
        O_P = O_K + RING * 4096
        probs = at("probs", [P, 2, PAGES * PAGE + T_S], F32, O_P)
        p_t = at("p_t", [P, 2, 9, P], F32, O_P + 8704)
        qz = at("qz", [P, 2, FOX * 72], F32, O_P + 17920)
        qzm = at("qzm", [P, 4, MEM * 40], F32, O_P + 22528)
        stat_a = at("stat_a", [P, 2, 4], F32, O_P + 25088)
        rsum = at("rsum", [P, 2, 4], F32, O_P + 25120)
        nmax = at("nmax", [P, 2], F32, O_P + 25152)
        rinv = at("rinv", [P, 2], F32, O_P + 25184)
        prompt = [("fox", h, i) for i in range(4) for h in range(FOX)] + [("mem", h, i) for i in range(4) for h in range(MEM)]
        samples = [("sfox", g, 0) for g in range(DB // 2)] + [("smem", g, 0) for g in range(DB // 4)]
        units = []
        for n, u in enumerate(samples):
            units += prompt[8 * n:8 * n + 8] + [u]
        units += prompt[48:]
        NU = len(units)

        def keys(u):
            kind, _, i = u
            return {"fox": (i + 1) * P, "mem": N_MEM, "sfox": PAGES * PAGE + T_S, "smem": N_MEM}[kind]

        def chunks(u):
            return (keys(u) + P - 1) // P

        def t_groups(u):
            return (chunks(u) + 3) // 4

        groups_before = [sum(t_groups(v) for v in units[:n]) for n in range(NU + 1)]
        n_samp = [sum(v[0] in ("sfox", "smem") for v in units[:n]) for n in range(NU + 1)]
        n_sfox = [sum(v[0] == "sfox" for v in units[:n]) for n in range(NU + 1)]
        n_smem = [sum(v[0] == "smem" for v in units[:n]) for n in range(NU + 1)]
        pages_of = {"sfox": 2 * PAGES, "smem": 4}
        pages_before = [sum(pages_of.get(v[0], 0) for v in units[:n]) for n in range(NU + 1)]

        s_kl = [sem(f"k_page_loaded{k}") for k in range(RING)]
        s_vl = [sem(f"v_page_loaded{k}") for k in range(RING)]
        s_ku, s_vu = sem("k_page_used"), sem("v_page_used")
        s_qz, s_qc = sem("q_rows_placed"), sem("q_rows_cleared")
        s_s, s_m, s_e, s_rs, s_pr = (sem(f"att_{x}") for x in ("logits", "negmax", "exps", "recips", "probs"))
        s_ng = sem("att_max")
        s_t, s_tc, s_pv, s_o = (sem(f"att_{x}") for x in ("transposed", "transposed_copied", "weighted", "drained"))

        def logits(n):
            return [acc[:, 0, 0, :], acc[:, 0, 1, :], acc[:, 1, 0, :]] if n % 2 == 0 else [acc[:, 1, 1, :], tps[:, 0, :], tps[:, 1, :]]

        tbank, obank = tps[:, 2, :], tps[:, 3, :]

        with nc.Block() as block:
            @block.sync
            def _(sp):
                n = 0
                for u in units:
                    if u[0] not in pages_of:
                        continue
                    m = pages_of[u[0]]
                    for which, ring, used, loaded in (("k", k_ring, s_ku, s_kl), ("v", v_ring, s_vu, s_vl)):
                        for k in range(m):
                            j = n + k
                            if j >= RING:
                                sp.wait_ge(used, j - RING + 1)
                            if u[0] == "sfox":
                                row = 2 * u[1] * PAGES + k
                                page = sp.value_load(pt[0:1, row:row + 1], min_val=0, max_val=N_PHYS - 1)
                                src = a["cache_" + which][bass.ds(page * P, P), :]
                            else:
                                row = 4 * u[1] + k
                                src = a["mem_cache_" + which][row * P:(row + 1) * P, :]
                            sp.dma_start(ring[:, j % RING, :], src).then_inc(loaded[j % RING], 16)
                    n += m

            @block.gpsimd
            def _(pool):
                nc.gpsimd.memset(qz[:], 0.0).then_inc(s_qc, 1)
                nc.gpsimd.memset(qzm[:], 0.0).then_inc(s_qc, 1)
                pool.wait_ge(s_qc, 2)
                for n, u in enumerate(units):
                    if u[0] == "sfox":
                        if n_sfox[n]:
                            m = max(k for k in range(n) if units[k][0] == "sfox")
                            pool.wait_ge(s_s, m + 1)
                        for b in range(2):
                            c0 = T_P + (2 * u[1] + b) * DT
                            last = nc.gpsimd.tensor_copy(qz[:, b, :].rearrange("p (h c) -> p h c", h=FOX)[:, :, 0:DT],
                                                         z[:, Q0:Q0 + FOX, c0:c0 + DT])
                        last.then_inc(s_qz, 1)
                    elif u[0] == "smem":
                        if n_smem[n]:
                            m = max(k for k in range(n) if units[k][0] == "smem")
                            pool.wait_ge(s_s, m + 1)
                        for b in range(4):
                            c0 = T_P + (4 * u[1] + b) * DT
                            last = nc.gpsimd.tensor_copy(qzm[:, b, :].rearrange("p (h c) -> p h c", h=MEM)[:, :, 0:DT],
                                                         z[:, QM0:QM0 + MEM, c0:c0 + DT])
                        last.then_inc(s_qz, 1)

            def softmax_parts(n):
                k = keys(units[n])
                return [(bank[:, 0:min(512, k - 512 * j)], 512 * j) for j, bank in enumerate(logits(n)) if k > 512 * j]

            @block.vector
            def _(dve):
                def negmax(n):
                    dve.wait_ge(s_s, n + 1)
                    if n >= 2:
                        dve.wait_ge(s_e, n - 1)
                    parts = softmax_parts(n)
                    for j, (src, _) in enumerate(parts):
                        last = nc.vector.reduce_max(stat_a[:, n % 2, j:j + 1], src, AX.X)
                    last.then_inc(s_ng, 1)
                    dve.wait_ge(s_ng, 2 * n + 1)
                    if len(parts) > 1:
                        nc.vector.reduce_max(stat_a[:, n % 2, 3:4], stat_a[:, n % 2, 0:3], AX.X).then_inc(s_ng, 1)
                    else:
                        nc.vector.tensor_copy(stat_a[:, n % 2, 3:4], stat_a[:, n % 2, 0:1]).then_inc(s_ng, 1)
                    dve.wait_ge(s_ng, 2 * n + 2)
                    nc.vector.tensor_scalar(nmax[:, n % 2:n % 2 + 1], stat_a[:, n % 2, 3:4], -SCALE, None, ALU.mult).then_inc(s_m, 1)

                def normalise(n):
                    dve.wait_ge(s_e, n + 1)
                    parts = len(softmax_parts(n))
                    if parts > 1:
                        nc.vector.reduce_sum(rsum[:, n % 2, 3:4], rsum[:, n % 2, 0:parts], AX.X).then_inc(s_rs, 1)
                    else:
                        nc.vector.tensor_copy(rsum[:, n % 2, 3:4], rsum[:, n % 2, 0:1]).then_inc(s_rs, 1)
                    dve.wait_ge(s_rs, 2 * n + 1)
                    nc.vector.reciprocal(rinv[:, n % 2:n % 2 + 1], rsum[:, n % 2, 3:4]).then_inc(s_rs, 1)
                    dve.wait_ge(s_rs, 2 * n + 2)
                    nk = keys(units[n])
                    nc.vector.tensor_scalar(probs[:, n % 2, 0:nk], probs[:, n % 2, 0:nk], rinv[:, n % 2:n % 2 + 1], None,
                                            ALU.mult).then_inc(s_pr, 1)

                def drain(n):
                    kind, h, i = units[n]
                    dve.wait_ge(s_pv, n + 1)
                    if kind in ("fox", "mem"):
                        c = (4 if kind == "fox" else 12) + h
                        nc.vector.tensor_copy(b_t[:, c, i * P:(i + 1) * P], obank[:, 0:P]).then_inc(s_o, 1)
                    else:
                        nb, nh, c = (2, FOX, 4) if kind == "sfox" else (4, MEM, 12)
                        t0 = T_P + h * nb * DT
                        for b in range(nb):
                            last = nc.vector.tensor_copy(b_t[:, c:c + nh, t0 + b * DT:t0 + (b + 1) * DT],
                                                         obank[:, b * nh * DT:(b + 1) * nh * DT].rearrange("p (h t) -> p h t", h=nh))
                        last.then_inc(s_o, 1)

                for n in range(NU + 2):
                    if n < NU:
                        negmax(n)
                    if 1 <= n <= NU:
                        normalise(n - 1)
                    if n >= 2:
                        drain(n - 2)

            @block.scalar
            def _(act):
                for n in range(NU + 1):
                    if n < NU:
                        act.wait_ge(s_m, n + 1)
                        if n >= 2:
                            act.wait_ge(s_t, groups_before[n - 1])
                            act.wait_ge(s_rs, 2 * (n - 1))
                        parts = softmax_parts(n)
                        for j, (src, k0) in enumerate(parts):
                            ins = nc.scalar.activation(probs[:, n % 2, k0:k0 + src.shape[1]], src, ACT.Exp,
                                                       bias=nmax[:, n % 2:n % 2 + 1], scale=SCALE,
                                                       accum_out=rsum[:, n % 2, j:j + 1])
                        ins.then_inc(s_e, 1)
                    if n >= 1:
                        m = n - 1
                        r = P
                        for g in range(t_groups(units[m])):
                            act.wait_ge(s_t, groups_before[m] + g + 1)
                            if m >= 2 and g == 0:
                                act.wait_ge(s_pv, m - 1)
                            nch = min(4, chunks(units[m]) - 4 * g)
                            rows = min(P, keys(units[m]) - 4 * g * P)
                            nc.scalar.activation(p_t[0:rows, m % 2, 4 * g:4 * g + nch, :],
                                                 tbank[0:rows, 0:nch * P].rearrange("p (c t) -> p c t", c=nch),
                                                 ACT.Copy).then_inc(s_tc, 1)

            @block.tensor
            def _(pe):
                def make_logits(n):
                    kind, h, i = units[n]
                    banks = logits(n)
                    if n >= 2:
                        pe.wait_ge(s_e, n - 1)
                    if kind == "fox":
                        nk = keys(units[n])
                        nc.tensor.matmul(banks[0][:, 0:nk], z[:, Q0 + h, i * P:(i + 1) * P], z[:, K0 + h, 0:nk], start=True, stop=False)
                        nc.tensor.matmul(banks[0][:, 0:nk], negsel_p[:, h, :], c_p[:, 0:nk], start=False, stop=False)
                        last = nc.tensor.matmul(banks[0][:, i * P:nk], ident[:], causal[:], start=False, stop=True)
                    elif kind == "mem":
                        last = nc.tensor.matmul(banks[0][:, 0:N_MEM], z[:, QM0 + h, i * P:(i + 1) * P], mk_t[:, h, :], start=True, stop=True)
                    elif kind == "sfox":
                        pe.wait_ge(s_qz, n_samp[n] + 1)
                        for b in range(2):
                            r0 = b * 64
                            for k in range(PAGES):
                                j = pages_before[n] + b * PAGES + k
                                pe.wait_ge(s_kl[j % RING], 16 * (j // RING + 1))
                                dst = banks[k // 4][r0:r0 + 64, (k % 4) * P:(k % 4 + 1) * P]
                                nc.tensor.matmul(dst, negsel_s[:, 2 * h + b, :], c_s[:, k * PAGE:(k + 1) * PAGE], start=True, stop=False)
                                for hh in range(FOX):
                                    last = nc.tensor.matmul(dst, qz[:, b, hh * 64:(hh + 1) * 64], k_ring[:, j % RING, hh * P:(hh + 1) * P],
                                                            start=False, stop=(hh == FOX - 1))
                                last.then_inc(s_ku, 1)
                            dst = banks[2][r0:r0 + 64, 0:T_S]
                            nc.tensor.matmul(dst, ident[0:64, 0:64], smask[:, 2 * h + b, :], start=True, stop=False)
                            nc.tensor.matmul(dst, negsel_s[:, 2 * h + b, :],
                                             c_s[:, PAGES * PAGE:].rearrange("p (o t) -> p o t", o=1).to_broadcast([64, DB, DT]),
                                             start=False, stop=False)
                            for hh in range(FOX):
                                last = nc.tensor.matmul(dst, qz[:, b, hh * 64:(hh + 1) * 64], z[:, K0 + hh, T_P:T],
                                                        start=False, stop=(hh == FOX - 1))
                    else:
                        pe.wait_ge(s_qz, n_samp[n] + 1)
                        for b in range(4):
                            j = pages_before[n] + b
                            pe.wait_ge(s_kl[j % RING], 16 * (j // RING + 1))
                            for hh in range(MEM):
                                last = nc.tensor.matmul(banks[0][b * 32:(b + 1) * 32, 0:N_MEM], qzm[:, b, hh * 32:(hh + 1) * 32],
                                                        k_ring[:, j % RING, hh * N_MEM:(hh + 1) * N_MEM],
                                                        start=(hh == 0), stop=(hh == MEM - 1), tile_position=(0, b * 32))
                            if b < 3:
                                last.then_inc(s_ku, 1)
                    last.then_inc(s_s, 1)
                    if kind == "smem":
                        pe.wait_ge(s_s, n + 1)
                        pe.sem_inc(s_ku, 1)

                def transpose_probs(n):
                    u = units[n]
                    pe.wait_ge(s_pr, n + 1)
                    for g in range(t_groups(u)):
                        if groups_before[n] + g >= 1:
                            pe.wait_ge(s_tc, groups_before[n] + g)
                        for c in range(4 * g, min(4 * g + 4, chunks(u))):
                            w = min(P, keys(u) - c * P)
                            last = nc.tensor.transpose(tbank[0:w, (c % 4) * P:(c % 4 + 1) * P], probs[:, n % 2, c * P:c * P + w], ident[:])
                        last.then_inc(s_t, 1)

                def weigh(n):
                    kind, h, i = units[n]
                    pe.wait_ge(s_tc, groups_before[n + 1])
                    if n >= 1:
                        pe.wait_ge(s_o, n)
                    nch = chunks(units[n])
                    if kind in ("fox", "mem"):
                        v = v_tok if kind == "fox" else mv_tok
                        for c in range(nch):
                            last = nc.tensor.matmul(obank[:, 0:P], v[:, c, h * HD:(h + 1) * HD], p_t[:, n % 2, c, :],
                                                    start=(c == 0), stop=(c == nch - 1))
                    elif kind == "sfox":
                        for b in range(2):
                            for k in range(PAGES + 1):
                                j = pages_before[n] + b * PAGES + k
                                if k < PAGES:
                                    pe.wait_ge(s_vl[j % RING], 16 * (j // RING + 1))
                                for hh in range(FOX):
                                    r0 = b * 64 + hh * DT
                                    if k < PAGES:
                                        l_, r_ = v_ring[:, j % RING, hh * HD:(hh + 1) * HD], p_t[:, n % 2, k, r0:r0 + DT]
                                    else:
                                        l_, r_ = v_tok[0:64, 4, hh * HD:(hh + 1) * HD], p_t[0:64, n % 2, k, r0:r0 + DT]
                                    last = nc.tensor.matmul(obank[:, r0:r0 + DT], l_, r_, start=(b == 0 and k == 0 and hh == 0),
                                                            stop=(b == 1 and k == PAGES and hh == FOX - 1), skip_group_check=True)
                                if k < PAGES:
                                    last.then_inc(s_vu, 1)
                    else:
                        for b in range(4):
                            j = pages_before[n] + b
                            pe.wait_ge(s_vl[j % RING], 16 * (j // RING + 1))
                            for hh in range(MEM):
                                for c in range(2):
                                    r0 = b * 32 + hh * DT
                                    last = nc.tensor.matmul(obank[:, r0:r0 + DT], v_ring[:, j % RING, c * 512 + hh * HD:c * 512 + (hh + 1) * HD],
                                                            p_t[:, n % 2, c, r0:r0 + DT], start=(c == 0), stop=(c == 1))
                            if b < 3:
                                last.then_inc(s_vu, 1)
                    last.then_inc(s_pv, 1)
                    if kind == "smem":
                        pe.wait_ge(s_pv, n + 1)
                        pe.sem_inc(s_vu, 1)

                for n in range(NU + 1):
                    if n < NU:
                        make_logits(n)
                    if n >= 1:
                        transpose_probs(n - 1)
                        weigh(n - 1)

        recycle()

        bt_hi = at("bt_hi", [P, KC, T], F32R, O_Z)
        bt_lo = at("bt_lo", [P, KC, T], F32R, O_Z + KC * T * 4)
        m_hi = at("m_hi", [P, KC, T], F32R, O_R1)
        m_lo = at("m_lo", [P, KC, T], F32R, O_R2)
        g_in = at("g_in", [P, 2, 3, T], F32, O_GB)
        tmp = at("merge_tmp", [P, T], F32, O_GB + 13824)
        merged = at("merged", [P, T], F32, O_Z + 2 * KC * T * 4)
        s_bh = sem("branches_split")
        with nc.Block() as block:
            @block.scalar
            def _(act):
                for g in range(4):
                    nc.scalar.activation(bt_hi[:, 4 * g:4 * g + 4, :], b_t[:, 4 * g:4 * g + 4, :], ACT.Copy).then_inc(s_bh, 1)

            @block.vector
            def _(dve):
                for g in range(4):
                    dve.wait_ge(s_bh, g + 1)
                    nc.vector.tensor_tensor(bt_lo[:, 4 * g:4 * g + 4, :], b_t[:, 4 * g:4 * g + 4, :],
                                            bt_hi[:, 4 * g:4 * g + 4, :].bitcast(F32), ALU.subtract)

        q3 = stream_sems("merge")
        s_gl = [sem(f"gates_loaded{k}") for k in range(2)]
        s_m0, s_m1, s_m2 = sem("pool_branch_taken"), sem("fox_branch_taken"), sem("mem_branch_taken")
        s_mch, s_mrd, s_mh, s_ml = sem("merge_chain"), sem("merged_ready"), sem("merged_hi"), sem("merged_lo")
        with nc.Block() as block:
            @block.sync
            def _(sp):
                load_stripes(sp, a["w_up"], KC, q3)

            @block.gpsimd
            def _(pool):
                for s in range(KC):
                    if s >= 2:
                        pool.wait_ge(s_m2, s)
                    pool.dma_start(g_in[:, s % 2, :, :], gates_dram[3 * s:3 * s + 3, :, :].rearrange("g p t -> p g t")).then_inc(s_gl[s % 2], 16)

            @block.scalar
            def _(act):
                def drain(i, s):
                    act.wait_ge(s_mrd, 2 * i + s + 1)
                    nc.scalar.activation(m_hi[:, bass.ds(2 * i + s, 1), :], merged[:].rearrange("p (o t) -> p o t", o=1), ACT.Copy).then_inc(s_mh, 1)
                lagged(act, KC, lambda i, s: split_hi(act, i, s, q3), drain)

            @block.vector
            def _(dve):
                def two(t_):
                    return t_.rearrange("p (b t) -> p b t", b=2)

                def drain(i, s):
                    n = 2 * i + s
                    par = s % 2
                    dve.wait_ge(q3["mm"], 4 * i + 2 * s + 4)
                    dve.wait_ge(s_gl[par], 16 * (i + s // 2 + 1))
                    dve.wait_ge(s_ml, n + 1)
                    nc.vector.tensor_tensor(two(merged[:]), acc[:, par, :, 0:HALF], two(g_in[:, par, 0, :]), ALU.mult).then_inc(s_m0, 1)
                    nc.vector.tensor_tensor(two(tmp[:]), tps[:, 0:2, 0:HALF], two(g_in[:, par, 1, :]), ALU.mult).then_inc(s_m1, 1)
                    dve.wait_ge(s_m1, n + 2)
                    nc.vector.tensor_tensor(merged[:], merged[:], tmp[:], ALU.add).then_inc(s_mch, 1)
                    dve.wait_ge(s_mch, n + 1)
                    nc.vector.tensor_tensor(two(tmp[:]), tps[:, 2:4, 0:HALF], two(g_in[:, par, 2, :]), ALU.mult).then_inc(s_m2, 1)
                    dve.wait_ge(s_m2, n + 2)
                    nc.vector.tensor_tensor(merged[:], merged[:], tmp[:], ALU.add).then_inc(s_mrd, 1)
                    dve.wait_ge(s_mh, n + 1)
                    nc.vector.tensor_tensor(m_lo[:, bass.ds(n, 1), :], merged[:].rearrange("p (o t) -> p o t", o=1),
                                            m_hi[:, bass.ds(n, 1), :].bitcast(F32), ALU.subtract).then_inc(s_ml, 1)
                lagged(dve, KC, lambda i, s: split_lo(dve, i, s, q3), drain)

            @block.tensor
            def _(pe):
                pe.sem_inc(q3["mm"], 2)
                pe.sem_inc(s_m0, 2)
                pe.sem_inc(s_m1, 1)
                pe.sem_inc(s_m2, 1)
                pe.sem_inc(s_ml, 1)

                def one(i, s):
                    par = s % 2

                    def out(cc, b, cn):
                        if cc < 4:
                            return acc[:, par, b, 0:cn], 0, 3
                        if cc < 12:
                            return tps[:, b, 0:cn], 4, 11
                        return tps[:, 2 + b, 0:cn], 12, KC - 1

                    def before(cc):
                        if cc in (0, 4, 12):
                            pe.wait_ge({0: s_m0, 4: s_m1, 12: s_m2}[cc], 2 * i + s + 1)

                    for h in range(2):
                        pe.wait_ge(q3["lo"], 4 * i + 2 * s + h + 1)
                        multiply_half(pe, par, h, bt_hi, bt_lo, HALVES, q3, out=out, before=before)

                with pe.Fori(0, KC // 2) as i:
                    one(i, 0)
                    one(i, 1)

        recycle()

        O_X1 = O_ATT
        O_T = O_X1 + NBLK * D * 4
        x1 = at("x1", [P, NBLK, D], F32, O_X1)
        mo = at("mo", [P, 2, T], F32, O_T)
        q4 = stream_sems("out")
        s_xl, s_ot, s_oa = sem("x_reloaded"), sem("out_transposed"), sem("out_added")
        with nc.Block() as block:
            @block.sync
            def _(sp):
                load_stripes(sp, a["w_out"], KC, q4)

            @block.gpsimd
            def _(pool):
                pool.dma_start(x1[:, 0:4, :], a["x"][0:T_P, :].rearrange("(b p) d -> p b d", p=P)).then_inc(s_xl, 16)
                pool.dma_start(x1[0:T_S, 4, :], a["x"][T_P:T, :]).then_inc(s_xl, 16)

            @block.scalar
            def _(act):
                def drain(i, s):
                    act.wait_ge(q4["mm"], 4 * i + 2 * s + 4)
                    act.wait_ge(s_ot, 2 * i + s + 1)
                    nc.scalar.activation(mo[:, s % 2, :].rearrange("p (b t) -> p b t", b=2), acc[:, s % 2, :, 0:HALF], ACT.Copy).then_inc(q4["act"], 1)
                lagged(act, KC, lambda i, s: split_hi(act, i, s, q4), drain)

            @block.vector
            def _(dve):
                def drain(i, s):
                    n, par = 2 * i + s, s % 2
                    dve.wait_ge(s_ot, n + 3)
                    dst = x1[:, 0:4, bass.ds(n * P, P)]
                    nc.vector.tensor_tensor(dst, tps[:, 2 * par, :].rearrange("p (b t) -> p b t", b=4), dst, ALU.add)
                    dst = x1[0:T_S, 4, bass.ds(n * P, P)]
                    nc.vector.tensor_tensor(dst, tps[0:T_S, 2 * par + 1, 0:P], dst, ALU.add).then_inc(s_oa, 1)
                dve.wait_ge(s_xl, 32)
                lagged(dve, KC, lambda i, s: split_lo(dve, i, s, q4), drain)

            @block.tensor
            def _(pe):
                def between(i, s):
                    n, par = 2 * i + s, s % 2
                    pe.wait_ge(q4["act"], n + 3)
                    pe.wait_ge(s_oa, n + 1)
                    for b in range(NBLK):
                        dst = tps[:, 2 * par, b * P:(b + 1) * P] if b < 4 else tps[0:T_S, 2 * par + 1, 0:P]
                        last = nc.tensor.transpose(dst, mo[:, par, b * P:b * P + ROWS[b]], ident[:])
                    last.then_inc(s_ot, 1)
                pe.sem_inc(s_ot, 2)
                pe.sem_inc(s_oa, 2)
                multiply_stripes(pe, KC, m_hi, m_lo, HALVES, q4, use=("act",), between=between)

        recycle()

        h_hi = at("h_hi", [P, KC, T], F32R, O_R1)
        h_lo = at("h_lo", [P, KC, T], F32R, O_R2)
        hn = at("hn", [P, 2, D], F32, O_T)
        norm_transposed("ffn", NBLK, ROWS, a["norm_ffn_g"], lambda b: x1[0:ROWS[b], b, :], None, h_hi, h_lo, (ss2, ms2, rstd2), hn)

        qp = at("qp", [P, 2 * PH, T], F32, O_T)
        q5 = stream_sems("peerq")
        act_q, dve_q = drain_to(qp, q5)
        with nc.Block() as block:
            @block.sync
            def _(sp):
                load_stripes(sp, a["w_pq"], 2 * PH, q5)

            @block.scalar
            def _(act):
                lagged(act, 2 * PH, lambda i, s: split_hi(act, i, s, q5), lambda i, s: act_q(act, i, s))

            @block.vector
            def _(dve):
                lagged(dve, 2 * PH, lambda i, s: split_lo(dve, i, s, q5), lambda i, s: dve_q(dve, i, s))

            @block.tensor
            def _(pe):
                multiply_stripes(pe, 2 * PH, h_hi, h_lo, HALVES, q5)

        recycle()

        place = [O_T + 2 * PH * T * 4]

        def then(name, shape, dtype):
            size = int(np.prod(shape[1:])) * 4
            t_ = at(name, shape, dtype, place[0])
            place[0] += (size + 31) // 32 * 32
            return t_

        eidx = at("eidx", [P, NEXP, NBLK], I32, O_MKT)
        route = at("route", [P, NEXP, NBLK], I32, O_MKT + NBLK * NEXP * 4)
        gate = at("gate", [P, NEXP, NBLK], F32, O_MKT + 2 * NBLK * NEXP * 4)
        onehot = at("onehot", [P, NEXP, PTOP], F32, O_GB)
        sc = at("sc", [P, 2, 2 * PH, NKEY], F32, O_W)
        sc_b = at("sc_b", [P, 2 * PH, NKEY], F32, O_W + 16384)
        cand2 = at("cand", [P, 2, PH, PTOP * PTOP], F32, O_W)
        cand_b = at("cand_b", [P, PH, PTOP * PTOP], F32, O_W + 16384)
        sk = at("sk", [P, 2 * PH, NKEY], F32, O_W + 24576)
        part = at("part", [P, 2, NEXP], F32, O_W + 32768)
        zero = at("zero", [P, 512], F32, O_W + 32768 + 1024)
        top = then("top", [P, 2 * PH, PTOP], F32)
        tidx = then("tidx", [P, 2 * PH, PTOP], U32)
        tidx_f = then("tidx_f", [P, 2 * PH, PTOP], F32)
        best = then("best", [P, PH, PTOP], F32)
        sel = then("sel", [P, PH, PTOP], U32)
        sel_a = then("sel_a", [P, 2, NEXP], U32)
        sel_f = then("sel_f", [P, 2, NEXP], F32)
        iota = then("iota16", [P, PTOP], F32)
        tok = then("token", [P, 8], F32)
        ebest = then("ebest", [P, PH, PTOP], F32)
        esum = then("esum", [P, 2, PH], F32)
        assert place[0] <= O_R1
        s_skl, s_qk, s_qkc, s_dd, s_tk, s_ex = (sem(f"topk_{x}") for x in ("keys_loaded", "scores", "copied", "block_done", "chain", "exps"))
        s_tick = sem("topk_tick")
        s_z0, s_z1 = sem("zero_written"), sem("routes_cleared")
        LINKS = 22
        with nc.Block() as block:
            @block.sync
            def _(sp):
                sp.dma_start(sk[:], a["subkeys"]).then_inc(s_skl, 16)
                sp.dma_start(iota[:], a["iota16"]).then_inc(s_skl, 16)
                sp.dma_start(tok[:], a["token"]).then_inc(s_skl, 16)

            @block.gpsimd
            def _(pool):
                nc.gpsimd.memset(zero[:], 0.0).then_inc(s_z0, 1)
                nc.gpsimd.memset(route[:], 0).then_inc(s_z0, 1)
                nc.gpsimd.memset(gate[:], 0.0).then_inc(s_z0, 1)
                pool.wait_ge(s_z0, 1)
                cells = route_dram.rearrange("(q p j c) o -> q p j (c o)", q=8, p=P, c=512)
                for k in range(8):
                    pool.dma_start(cells[k], zero[:].unsqueeze(1).to_broadcast([P, N_EXPERTS * ND // (8 * P * 512), 512])).then_inc(s_z1, 16)
                pool.wait_ge(s_z1, 16 * 8)

            @block.tensor
            def _(pe):
                pe.wait_ge(s_skl, 48)
                for b in range(NBLK):
                    r = ROWS[b]
                    for g in range(4):
                        n = 4 * b + g
                        bank = acc[:, n % 4 // 2, n % 2, :]
                        if n >= 4:
                            pe.wait_ge(s_qkc, n - 3)
                        for k in range(4):
                            last = nc.tensor.matmul(bank[0:r, k * P:(k + 1) * P], qp[:, 4 * g + k, b * P:b * P + r], sk[:, 4 * g + k, :],
                                                    start=True, stop=True)
                        last.then_inc(s_qk, 1)

            @block.scalar
            def _(act):
                for b in range(NBLK + 1):
                    if b < NBLK:
                        if b >= 2:
                            act.wait_ge(s_dd, b - 1)
                        for g in range(4):
                            n = 4 * b + g
                            r = ROWS[b]
                            act.wait_ge(s_qk, n + 1)
                            nc.scalar.activation(sc[0:r, b % 2, 4 * g:4 * g + 4, :],
                                                 acc[0:r, n % 4 // 2, n % 2, :].rearrange("p (k c) -> p k c", k=4), ACT.Copy).then_inc(s_qkc, 1)
                    if b >= 1:
                        r = ROWS[b - 1]
                        act.wait_ge(s_tk, LINKS * (b - 1) + 10)
                        nc.scalar.activation(ebest[0:r], ebest[0:r], ACT.Exp).then_inc(s_ex, 1)

            @block.vector
            def _(dve):
                def topk(b, par, r):
                    count = [0]

                    def link(ins):
                        count[0] += 1
                        ins.then_inc(s_tk, 1)
                        dve.wait_ge(s_tk, LINKS * b + count[0])
                        dve.sem_inc(s_tick, 1)

                    dve.wait_ge(s_qkc, 4 * b + 4)
                    dve.sem_inc(s_tick, 1)
                    cand = cand2[:, par]
                    for src, src_b, vals, idx, m in ((sc[0:r, par], sc_b[0:r], top[0:r], tidx[0:r], 2 * PH), (cand[0:r], cand_b[0:r], best[0:r], sel[0:r], PH)):
                        if m == PH:
                            tv = top[0:r].rearrange("p (h two) k -> p h two k", two=2)
                            link(nc.vector.tensor_tensor(
                                cand[0:r].rearrange("p h (x y) -> p h x y", x=PTOP),
                                tv[:, :, 0, :].unsqueeze(3).to_broadcast([r, PH, PTOP, PTOP]),
                                tv[:, :, 1, :].unsqueeze(2).to_broadcast([r, PH, PTOP, PTOP]), ALU.add))
                        for h in range(m):
                            last = nc.vector.max(out=vals[:, h, 0:8], in_=src[:, h, :])
                        link(last)
                        for h in range(m):
                            nc.vector.max_index(out=idx[:, h, 0:8], in_max=vals[:, h, 0:8], in_values=src[:, h, :])
                            last = nc.vector.match_replace(out=src_b[:, h, :], in_to_replace=vals[:, h, 0:8], in_values=src[:, h, :], imm_value=-3.0e38)
                        link(last)
                        for h in range(m):
                            last = nc.vector.max(out=vals[:, h, 8:16], in_=src_b[:, h, :])
                        link(last)
                        for h in range(m):
                            last = nc.vector.max_index(out=idx[:, h, 8:16], in_max=vals[:, h, 8:16], in_values=src_b[:, h, :])
                        link(last)
                    link(nc.vector.tensor_tensor(ebest[0:r], best[0:r], best[0:r, :, 0:1].to_broadcast([r, PH, PTOP]), ALU.subtract))
                    sf = sel[0:r].rearrange("p h k -> p (h k)")
                    nc.vector.tensor_scalar(sel_a[0:r, 0], sf, 4, None, ALU.logical_shift_right)
                    link(nc.vector.tensor_scalar(sel_a[0:r, 1], sf, PTOP - 1, None, ALU.bitwise_and))
                    nc.vector.tensor_copy(tidx_f[0:r], tidx[0:r])
                    link(nc.vector.tensor_copy(sel_f[0:r], sel_a[0:r]))
                    for side in range(2):
                        link(nc.vector.tensor_tensor(onehot[0:r], sel_f[0:r, side, :].unsqueeze(2).to_broadcast([r, NEXP, PTOP]),
                                                     iota[0:r].unsqueeze(1).to_broadcast([r, NEXP, PTOP]), ALU.is_equal))
                        oh4 = onehot[0:r].rearrange("p (h k) x -> p h k x", h=PH)
                        lists = tidx_f[0:r].rearrange("p (h two) k -> p h two k", two=2)[:, :, side, :]
                        link(nc.vector.tensor_tensor(oh4, oh4, lists.unsqueeze(2).to_broadcast([r, PH, PTOP, PTOP]), ALU.mult))
                        link(nc.vector.reduce_sum(part[0:r, side, :], onehot[0:r], AX.X))
                    link(nc.vector.scalar_tensor_tensor(out=eidx[0:r, :, bass.ds(b, 1)], in0=part[0:r, 0, :].unsqueeze(2), scalar=float(NKEY),
                                                        in1=part[0:r, 1, :].unsqueeze(2), op0=ALU.mult, op1=ALU.add))
                    nc.vector.tensor_scalar(route[0:r, :, bass.ds(b, 1)], eidx[0:r, :, bass.ds(b, 1)], float(ND), tok[0:r, bass.ds(b, 1)],
                                            ALU.mult, ALU.add)
                    dve.wait_ge(s_ex, b + 1)
                    link(nc.vector.reduce_sum(esum[0:r, 0, :], ebest[0:r], AX.X))
                    link(nc.vector.reciprocal(esum[0:r, 1, :], esum[0:r, 0, :]))
                    link(nc.vector.tensor_tensor(gate[0:r, :, bass.ds(b, 1)].rearrange("p (h k) o -> p h (k o)", h=PH), ebest[0:r],
                                                 esum[0:r, 1, :].unsqueeze(2).to_broadcast([r, PH, PTOP]), ALU.mult))
                    assert count[0] == LINKS
                    dve.sem_inc(s_dd, 1)

                dve.wait_ge(s_skl, 48)
                dve.wait_ge(s_z0, 3)
                with dve.Fori(0, 2) as i:
                    topk(2 * i, 0, P)
                    topk(2 * i + 1, 1, P)
                topk(4, 0, T_S)

        recycle()

        ring = at("ring", [P, 2, D], F32, O_T)
        hrow = at("h_row", [P, D], F32, O_T + 16384)
        a_out = at("a_out", [P, 2, ND], F32, O_T + 24576)
        dots = at("dots", [P, NEXP], F32, O_T + 28672)
        O_WTS = O_R1 - 1024
        wts = at("weights", [P, NEXP], F32, O_WTS)
        stage_e = at("expert_stage", [P, 2, 8], I32, O_WTS + 512)
        stage_r = at("route_stage", [P, 2, 8], I32, O_WTS + 576)
        stage_g = at("gate_stage", [P, 2, 8], F32, O_WTS + 640)
        q6 = stream_sems("peeru")
        s_gl2, s_hr = sem("ffn_g_reloaded"), sem("h_row_ready")
        s_st = [sem(f"activations_stored{k}") for k in range(2)]
        s_gat = [sem(f"u_row_gathered{k}") for k in range(2)]
        s_used, s_stg, s_sct, s_ptick = sem("u_row_used"), sem("indices_staged"), sem("gates_scattered"), sem("route_tick")
        s_dots, s_gel = sem("dots_done"), sem("gelu_done")
        with nc.Block() as block:
            @block.sync
            def _(sp):
                sp.dma_start(g_row[:], a["norm_ffn_g"].rearrange("(o d) -> o d", o=1).to_broadcast([P, D])).then_inc(s_gl2, 16)
                load_stripes(sp, a["w_peer_u"], NTILE, q6)

            @block.gpsimd
            def _(pool):
                pool.sem_inc(s_used, 2)
                with pool.Fori(0, NEXP // 2) as i:
                    for s in range(2):
                        n = 2 * i + s
                        pool.wait_ge(s_sct, 64 * n)
                        pool.wait_ge(s_used, n + 1)
                        nc.gpsimd.tensor_copy(stage_e[:, s, 0:1], eidx[:, bass.ds(n, 1), 0]).then_inc(s_stg, 1)
                        nc.gpsimd.tensor_copy(stage_r[:, s, 0:NBLK], route[:, bass.ds(n, 1), :].rearrange("p o b -> p (o b)")).then_inc(s_stg, 1)
                        nc.gpsimd.tensor_copy(stage_g[:, s, 0:NBLK], gate[:, bass.ds(n, 1), :].rearrange("p o b -> p (o b)")).then_inc(s_stg, 1)
                        pool.wait_ge(s_stg, 3 * n + 3)
                        pool.sem_inc(s_ptick, 1)
                        for b in range(1, NBLK):
                            r = ROWS[b]
                            pool.indirect_dma_start(route_dram, bass.IndirectOffsetOnAxis(ap=stage_r[0:r, s, b:b + 1], axis=0),
                                                    stage_g[0:r, s, b:b + 1], None, compute_op=ALU.add).then_inc(s_sct, 16)
                        pool.indirect_dma_start(ring[:, s, :], None, a["peer_u"],
                                                bass.IndirectOffsetOnAxis(ap=stage_e[:, s, 0:1], axis=0)).then_inc(s_gat[s], 16)
                pool.wait_ge(s_sct, 64 * NEXP)

            def drain_u(act, i, s):
                act.wait_ge(q6["mm"], 4 * i + 2 * s + 4)
                act.wait_ge(s_st[s], 16 * i)
                nc.scalar.activation(a_out[:, s, :], acc[:, s, 0, 0:ND], ACT.Gelu).then_inc(q6["act"], 1)
                act.wait_ge(q6["act"], 2 * i + s + 3)
                act.dma_start(acts_dram[bass.ds(2 * i + s, 1), :, :].rearrange("o p t -> p (o t)"), a_out[:, s, :]).then_inc(s_st[s], 16)

            @block.scalar
            def _(act):
                lagged(act, NTILE, lambda i, s: split_hi(act, i, s, q6), lambda i, s: drain_u(act, i, s))
                act.wait_ge(s_dots, NEXP)
                nc.scalar.activation(dots[:], dots[:], ACT.Gelu).then_inc(s_gel, 1)
                for s in range(2):
                    act.wait_ge(s_st[s], 16 * NTILE // 2)

            @block.vector
            def _(dve):
                def dot(i, s):
                    dve.wait_ge(s_gat[s], 16 * i + 16)
                    nc.vector.scalar_tensor_tensor(out=ring[:, s, :], in0=ring[:, s, :], scalar=1.0, in1=hrow[:], op0=ALU.mult,
                                                   op1=ALU.mult, accum_out=dots[:, bass.ds(2 * i + s, 1)]).then_inc(s_used, 1)

                dve.wait_ge(s_gl2, 16)
                nc.vector.scalar_tensor_tensor(out=hrow[:], in0=x1[:, 0, :], scalar=rstd2[:, 0:1], in1=g_row[:],
                                               op0=ALU.mult, op1=ALU.mult).then_inc(s_hr, 1)
                dve.wait_ge(s_hr, 1)
                lagged(dve, NTILE, lambda i, s: split_lo(dve, i, s, q6), dot)
                dve.wait_ge(s_used, 2 + NEXP)
                dve.sem_inc(s_dots, NEXP)
                dve.wait_ge(s_gel, 1)
                nc.vector.tensor_tensor(wts[:], dots[:], gate[:, :, 0], ALU.mult)

            @block.tensor
            def _(pe):
                multiply_stripes(pe, NTILE, h_hi, h_lo, [(P, ND)], q6, use=("act",))

        recycle()

        NG = NTILE // GRP
        t_hi = at("tile_hi", [P, 2 * GRP, ND], F32R, O_R1)
        t_lo = at("tile_lo", [P, 2 * GRP, ND], F32R, O_R1 + 2 * GRP * ND * 4)
        ring_v = at("ring_v", [P, 2, D], F32, O_R1 + 4 * GRP * ND * 4)
        out_t = at("out_t", [P, KC, ND], F32, O_T)
        O_AG = O_T + KC * ND * 4
        ag = at("act_and_gate", [P, 2, 2, ND], F32, O_AG)
        hf = at("tile_full", [P, 2, ND], F32, O_AG + 4 * ND * 4)
        assert O_AG + 6 * ND * 4 <= O_WTS
        q7 = stream_sems("peerv")
        s_ag = [sem(f"act_and_gate_loaded{k}") for k in range(2)]
        s_hm, s_hh, s_hl = sem("tile_product"), sem("tile_hi_ready"), sem("tile_lo_ready")
        s_clr = sem("out_cleared")
        s_gat = [sem(f"v_row_gathered{k}") for k in range(2)]
        s_used, s_stg, s_ptick, s_vt2 = sem("v_row_used"), sem("v_index_staged"), sem("v_tick"), sem("v_add_tick")
        with nc.Block() as block:
            @block.sync
            def _(sp):
                w = a["w_peer_v"]

                def load_tile(tile, par):
                    sp.dma_start(ag[:, par, 0, :], acts_dram[bass.ds(tile, 1), :, :].rearrange("o p t -> p (o t)")).then_inc(s_ag[par], 16)
                    sp.dma_start(ag[:, par, 1, :], route_dram.rearrange("(n t) o -> n (t o)", t=ND)[bass.ds(tile * P, P), :]).then_inc(s_ag[par], 16)

                for t_ in range(GRP):
                    if t_ >= 2:
                        sp.wait_ge(s_hm, t_ - 1)
                    load_tile(t_, t_ % 2)
                    if t_ < 4:
                        sp.dma_start(raw[:, t_, :], w[t_ * P:(t_ + 1) * P, :]).then_inc(q7["loaded"][t_], 16)

                def tile_of(i, k):
                    sp.wait_ge(s_hm, 2 * i + k + GRP - 1)
                    load_tile(2 * i + k + GRP, k)

                def halves(i, k):
                    sp.wait_ge(q7["lo"], 4 * i + k - 3)
                    sp.dma_start(raw[:, k, :], w[bass.ds((4 * i + k) * P, P), :]).then_inc(q7["loaded"][k], 16)

                tile_of(0, 0)
                tile_of(0, 1)
                with sp.Fori(1, (NTILE - GRP) // 2) as i:
                    for k in range(4):
                        halves(i, k)
                        if k % 2:
                            tile_of(i, k // 2)
                with sp.Fori((NTILE - GRP) // 2, NTILE // 2) as i:
                    for k in range(4):
                        halves(i, k)

            @block.gpsimd
            def _(pool):
                for k in range(4):
                    nc.gpsimd.memset(out_t[:, 4 * k:4 * k + 4, :], 0.0).then_inc(s_clr, 1)
                pool.sem_inc(s_used, 2)
                with pool.Fori(0, NEXP // 2) as i:
                    for s in range(2):
                        n = 2 * i + s
                        pool.wait_ge(s_used, n + 1)
                        nc.gpsimd.tensor_copy(stage_e[:, s, 0:1], eidx[:, bass.ds(n, 1), 0]).then_inc(s_stg, 1)
                        pool.wait_ge(s_stg, n + 1)
                        pool.sem_inc(s_ptick, 1)
                        pool.indirect_dma_start(ring_v[:, s, :], None, a["peer_v"],
                                                bass.IndirectOffsetOnAxis(ap=stage_e[:, s, 0:1], axis=0)).then_inc(s_gat[s], 16)

            def sweep(eng, before, split, after):
                def body(i, par, j, build=True, ahead=True):
                    for s in range(2):
                        before(i, s, par, j, build)
                        if s == 0 or ahead:
                            split(i, s + 1)
                        after(i, s, par, j, build)

                split(0, 0)
                with eng.Fori(0, NG // 2 - 1) as gg:
                    for par in range(2):
                        with eng.Fori(0, GRP // 2) as j:
                            body(GRP * gg + GRP // 2 * par + j, par, j)
                last = GRP * (NG // 2 - 1)
                with eng.Fori(0, GRP // 2) as j:
                    body(last + j, 0, j)
                with eng.Fori(0, GRP // 2 - 1) as j:
                    body(last + GRP // 2 + j, 1, j, build=False)
                body(last + GRP - 1, 1, GRP // 2 - 1, build=False, ahead=False)

            def slot_of(s, par, j):
                return bass.ds(GRP * (1 - par) + 2 * j + s, 1)

            def round_tile(act, tile, par, dst):
                act.wait_ge(s_hm, tile + 1)
                nc.scalar.activation(dst, hf[:, par:par + 1, :], ACT.Copy).then_inc(s_hh, 1)

            @block.scalar
            def _(act):
                for t_ in range(GRP):
                    round_tile(act, t_, t_ % 2, t_hi[:, t_:t_ + 1, :])

                def before(i, s, par, j, build):
                    if build:
                        round_tile(act, 2 * i + s + GRP, s, t_hi[:, slot_of(s, par, j), :])
                sweep(act, before, lambda i, s: split_hi(act, i, s, q7), lambda *_: None)

            @block.vector
            def _(dve):
                def product(tile, par, loads):
                    dve.wait_ge(s_ag[par], 32 * loads)
                    dve.wait_ge(s_hl, tile + 1)
                    nc.vector.tensor_tensor(hf[:, par, :], ag[:, par, 0, :], ag[:, par, 1, :], ALU.mult).then_inc(s_hm, 1)

                def rest(tile, par, dst, hi):
                    dve.wait_ge(s_hh, tile + 1)
                    nc.vector.tensor_tensor(dst, hf[:, par:par + 1, :], hi.bitcast(F32), ALU.subtract).then_inc(s_hl, 1)

                dve.sem_inc(s_hl, 2)
                for t_ in range(GRP):
                    product(t_, t_ % 2, t_ // 2 + 1)
                    rest(t_, t_ % 2, t_lo[:, t_:t_ + 1, :], t_hi[:, t_:t_ + 1, :])
                dve.wait_ge(s_clr, 4)

                def before(i, s, par, j, build):
                    if build:
                        product(2 * i + s + GRP, s, i + 1 + GRP // 2)

                def after(i, s, par, j, build):
                    for h in range(2):
                        dve.wait_ge(q7["mm"], 4 * i + 2 * s + h + 3)
                        dst = out_t[:, bass.ds(4 * j + 2 * s + h, 1), :] if not isinstance(j, int) else out_t[:, 4 * j + 2 * s + h:4 * j + 2 * s + h + 1, :]
                        nc.vector.tensor_tensor(dst, acc[:, s, h:h + 1, 0:ND], dst, ALU.add).then_inc(q7["dve"], 1)
                    if build:
                        sl = slot_of(s, par, j)
                        rest(2 * i + s + GRP, s, t_lo[:, sl, :], t_hi[:, sl, :])
                    dve.wait_ge(s_gat[s], 16 * i + 16)
                    dve.wait_ge(s_used, 2 * i + s + 2)
                    w = wts[:, bass.ds(2 * i + s, 1)] if not isinstance(i, int) else wts[:, 2 * i + s:2 * i + s + 1]
                    nc.vector.scalar_tensor_tensor(out=x1[:, 0, :], in0=ring_v[:, s, :], scalar=w, in1=x1[:, 0, :],
                                                   op0=ALU.mult, op1=ALU.add).then_inc(s_used, 1)

                sweep(dve, before, lambda i, s: split_lo(dve, i, s, q7), after)

            @block.tensor
            def _(pe):
                pe.sem_inc(q7["mm"], 2)
                pe.sem_inc(q7["dve"], 4)

                with pe.Fori(0, NG // 2) as gg:
                    for par in range(2):
                        with pe.Fori(0, GRP // 2) as j:
                            for s, h in ((0, 0), (0, 1), (1, 0), (1, 1)):
                                n = 2 * KC * gg + KC * par + 4 * j + 2 * s + h
                                pe.wait_ge(q7["lo"], n + 1)
                                pe.wait_ge(q7["dve"], n + 1)
                                pe.wait_ge(s_hl, 2 * GRP * gg + GRP * par + GRP + 1)
                                for c in range(GRP):
                                    if c == GRP - 1:
                                        pe.wait_ge(s_hl, 2 * GRP * gg + GRP * par + GRP + 2)
                                    wh, wl = w_hi[:, h, c * P:(c + 1) * P], w_lo[:, h, c * P:(c + 1) * P]
                                    t_ = GRP * par + c
                                    for p_, (l_, r_) in enumerate(((wh, t_hi), (wh, t_lo), (wl, t_hi))):
                                        last = nc.tensor.matmul(acc[:, s, h, 0:ND], l_, r_[:, t_, :], start=(c == 0 and p_ == 0),
                                                                stop=(c == GRP - 1 and p_ == 2))
                                last.then_inc(q7["mm"], 1)

        recycle()

        g_fin = at("g_final", [P, D], F32, O_W)
        y = at("y", [P, 2, D], F32, O_R1)
        sq = at("squares", [P, D], F32, O_R1 + 16384)
        fin = at("fin", [P, 3, 8], F32, O_WTS)
        s_gf, s_ft, s_fadd, s_fsq, s_fms, s_frt, s_frs, s_fy = (sem(f"final_{x}") for x in (
            "g_loaded", "transposed", "added", "squared", "mean", "root", "rstd", "normed"))
        s_ys = [sem(f"y_stored{k}") for k in range(2)]
        with nc.Block() as block:
            @block.sync
            def _(sp):
                sp.dma_start(g_fin[:], a["norm_final_g"].rearrange("(o d) -> o d", o=1).to_broadcast([P, D])).then_inc(s_gf, 16)
                for b, r in enumerate(ROWS):
                    sp.wait_ge(s_fy, b + 1)
                    sp.dma_start(a["y"][b * P:b * P + r, :], y[0:r, b % 2, :]).then_inc(s_ys[b % 2], 16)
                sp.wait_ge(s_ys[0], 48)
                sp.wait_ge(s_ys[1], 32)

            @block.tensor
            def _(pe):
                for b in range(1, NBLK):
                    for g in range(4):
                        n = 4 * (b - 1) + g
                        if n >= 4:
                            pe.wait_ge(s_fadd, n - 3)
                        for c in range(4):
                            last = nc.tensor.transpose(tps[0:ROWS[b], g, c * P:(c + 1) * P],
                                                       out_t[:, 4 * g + c, (b - 1) * P:(b - 1) * P + ROWS[b]], ident[:])
                        last.then_inc(s_ft, 1)

            @block.scalar
            def _(act):
                for b, r in enumerate(ROWS):
                    if b:
                        act.wait_ge(s_fadd, 4 * b)
                        act.wait_ge(s_fsq, b)
                    nc.scalar.activation(sq[0:r], x1[0:r, b, :], ACT.Square, accum_out=fin[0:r, 0, b:b + 1]).then_inc(s_fsq, 1)
                    act.wait_ge(s_fms, b + 1)
                    nc.scalar.activation(fin[0:r, 1, b:b + 1], fin[0:r, 1, b:b + 1], ACT.Sqrt).then_inc(s_frt, 1)

            @block.vector
            def _(dve):
                def add(b):
                    r = ROWS[b]
                    for g in range(4):
                        dve.wait_ge(s_ft, 4 * (b - 1) + g + 1)
                        dst = x1[0:r, b, g * 512:(g + 1) * 512]
                        nc.vector.tensor_tensor(dst, tps[0:r, g, :], dst, ALU.add).then_inc(s_fadd, 1)

                def mean(b):
                    r = ROWS[b]
                    dve.wait_ge(s_fsq, b + 1)
                    nc.vector.tensor_scalar(fin[0:r, 1, b:b + 1], fin[0:r, 0, b:b + 1], 1.0 / D, EPS, ALU.mult, ALU.add).then_inc(s_fms, 1)

                def norm(b):
                    r = ROWS[b]
                    dve.wait_ge(s_frt, b + 1)
                    nc.vector.reciprocal(fin[0:r, 2, b:b + 1], fin[0:r, 1, b:b + 1]).then_inc(s_frs, 1)
                    dve.wait_ge(s_frs, b + 1)
                    if b >= 2:
                        dve.wait_ge(s_ys[b % 2], 16 * (b // 2))
                    nc.vector.scalar_tensor_tensor(out=y[0:r, b % 2, :], in0=x1[0:r, b, :], scalar=fin[0:r, 2, b:b + 1], in1=g_fin[0:r],
                                                   op0=ALU.mult, op1=ALU.mult).then_inc(s_fy, 1)

                dve.wait_ge(s_gf, 16)
                mean(0)
                for b in range(NBLK):
                    if b + 1 < NBLK:
                        add(b + 1)
                    norm(b)
                    if b + 1 < NBLK:
                        mean(b + 1)


_OUTS = {
    "y": (T, D), "z_out": (P, F0 - K0, T), "mem_out": (P, 2 * MEM, N_MEM), "logf_out": (FOX, T), "state_out": (P, 4, DB, STATE),
}


def _half_stripes(w):
    n = w.shape[1] // P
    return np.ascontiguousarray(w.reshape(2, 8, P, n, P).transpose(3, 0, 2, 1, 4)).reshape(n * 2 * P, 1024)


def _expert_stripes(v):
    return np.ascontiguousarray(v.reshape(NTILE // GRP, GRP, P, KC, P).transpose(0, 3, 2, 1, 4)).reshape(NTILE // GRP * KC * P, GRP * P)


def _constants():
    ident = np.eye(P, dtype=np.float32)
    negsel_p = np.zeros((FOX, FOX, P), np.float32)
    negsel_s = np.zeros((DB, FOX, DB, FOX, DT), np.float32)
    for h in range(FOX):
        negsel_p[h, h, :] = -1.0 / SCALE
        for b in range(DB):
            negsel_s[b, h, b, h, :] = -1.0 / SCALE
    smask = np.full((FOX, DT, DB, DB, DT), NEG, np.float32)
    for b in range(DB):
        for t in range(DT):
            smask[:, t, b, b, 0:t + 1] = 0.0
    causal = np.where(np.arange(P)[None, :] <= np.arange(P)[:, None], 0.0, NEG).astype(np.float32)
    cnt = np.array([[1.0 / min(t + 1, w) for t in range(16)] for w in WINDOWS], np.float32)
    return {
        "ident": ident, "negsel_p": negsel_p, "negsel_s": negsel_s.reshape(DB * FOX, DB, FOX * DT),
        "smask": smask.reshape(FOX * DT, DB, T_S), "causal": causal,
        "cnt_inv": np.ascontiguousarray(np.broadcast_to(cnt, (P, 4, 16))),
        "token": np.ascontiguousarray((np.arange(P)[:, None] + (np.arange(8)[None, :] - 1) * P).astype(np.float32)),
        "iota16": np.ascontiguousarray(np.broadcast_to(np.arange(PTOP, dtype=np.float32), (P, PTOP))),
    }


def kernel(**inputs):
    import concourse.bacc as bacc
    from concourse.bass_utils import run_bass_kernel_spmd

    g = {k: np.asarray(v) for k, v in inputs.items()}
    w_in = g["w_in"][0]
    pw, fw, mw = 512, 1024, 512
    cols = {}
    o = 0
    for name, n in (("u", pw), ("q", fw), ("k", fw), ("v", fw), ("f", FOX), ("qm", mw), ("g", 3 * D)):
        cols[name] = w_in[:, o:o + n]
        o += n
    w_z = np.concatenate([cols["q"], cols["qm"], cols["k"], cols["v"], cols["u"], cols["f"], np.zeros((D, P - FOX), np.float32)], axis=1)
    w_gate = cols["g"].reshape(D, 3, KC, P).transpose(0, 2, 1, 3).reshape(D, 3 * D)
    arrays = {
        "x": np.concatenate([g["x_prompt"].reshape(T_P, D), g["x_sample"].reshape(T_S, D)]),
        "mem_prompt": g["mem_prompt"].reshape(N_MEM, D),
        "w_z": _half_stripes(w_z), "w_gate": _half_stripes(w_gate),
        "w_mem": _half_stripes(np.concatenate([g["w_mem_k"][0], g["w_mem_v"][0]], axis=1)),
        "w_up": _half_stripes(np.concatenate([g["w_up_pool"][0], g["w_up_fox"][0], g["w_up_mem"][0]], axis=0)),
        "w_out": _half_stripes(g["w_out"][0]), "w_pq": _half_stripes(g["w_peer_q"][0]),
        "cache_k": np.ascontiguousarray(g["cache_k"][0].transpose(0, 3, 2, 1)).reshape(N_PHYS * HD, FOX * PAGE),
        "cache_v": g["cache_v"][0].reshape(N_PHYS * PAGE, FOX * HD),
        "cache_logf": np.ascontiguousarray(g["cache_logf"][0].transpose(0, 2, 1)).reshape(N_PHYS * FOX, PAGE),
        "mem_cache_k": np.ascontiguousarray(g["cache_mem_k"][0].transpose(0, 3, 2, 1)).reshape(DB * HD, MEM * N_MEM),
        "mem_cache_v": np.ascontiguousarray(g["cache_mem_v"][0].reshape(DB, 2, P, MEM * HD).transpose(0, 2, 1, 3)).reshape(DB * P, 2 * MEM * HD),
        "state_pool": np.ascontiguousarray(g["state_pool"][0].reshape(DB, STATE, 4, P).transpose(3, 2, 0, 1)),
        "page_table": g["page_table"].reshape(1, DB * PAGES),
        "pool_w": np.ascontiguousarray(g["pool_w"][0].transpose(1, 0, 2)),
        "pool_scale": np.ascontiguousarray(g["pool_scale"][0].reshape(4, P).T),
        "b_f": g["b_f"].reshape(FOX, 1),
        "subkeys": np.ascontiguousarray(g["peer_subkeys"][0].transpose(3, 0, 1, 2)).reshape(P, 2 * PH, NKEY),
        "peer_u": g["peer_u"][0], "peer_v": g["peer_v"][0],
        "w_peer_u": _half_stripes(g["peer_u"][0].T), "w_peer_v": _expert_stripes(g["peer_v"][0]),
        "norm_mix_g": g["norm_mix_g"][0], "mem_norm_g": g["mem_norm_g"][0], "norm_ffn_g": g["norm_ffn_g"][0],
        "norm_final_g": g["norm_final_g"],
        **_constants(),
    }
    nc = bacc.Bacc("TRN2", target_bir_lowering=False, num_devices=1)
    a, given = {}, {}
    for name, x in arrays.items():
        x = np.ascontiguousarray(x)
        given["in_" + name] = x
        a[name] = nc.dram_tensor("in_" + name, x.shape, mybir.dt.from_np(x.dtype), kind="ExternalInput").ap()
    for name, shape in _OUTS.items():
        a[name] = nc.dram_tensor("out_" + name, shape, F32, kind="ExternalOutput").ap()
    build(nc, a)
    r = run_bass_kernel_spmd(nc, [given], core_ids=[0]).results[0]
    y, zo, mo, lf, st = (np.asarray(r["out_" + n]) for n in _OUTS)

    def rows(z_part, t0, t1):
        return np.ascontiguousarray(z_part[:, :, t0:t1].transpose(2, 1, 0)).reshape(t1 - t0, -1)

    k, v, u = zo[:, 0:8], zo[:, 8:16], zo[:, 16:20]
    return (
        y[0:T_P].reshape(1, T_P, D), y[T_P:T].reshape(DB, DT, D),
        rows(k, 0, T_P).reshape(1, 1, T_P, FOX, HD), rows(v, 0, T_P).reshape(1, 1, T_P, FOX, HD),
        np.ascontiguousarray(lf[:, 0:T_P].T).reshape(1, 1, T_P, FOX),
        rows(u, T_P - STATE, T_P).reshape(1, 1, STATE, 512),
        rows(mo[:, 0:MEM], 0, N_MEM).reshape(1, 1, N_MEM, MEM, HD), rows(mo[:, MEM:], 0, N_MEM).reshape(1, 1, N_MEM, MEM, HD),
        rows(k, T_P, T).reshape(1, DB, DT, FOX, HD), rows(v, T_P, T).reshape(1, DB, DT, FOX, HD),
        np.ascontiguousarray(lf[:, T_P:T].T).reshape(1, DB, DT, FOX),
        np.ascontiguousarray(st.transpose(2, 3, 1, 0)).reshape(1, DB, STATE, 512),
    )
```

```python
import numpy as np
from contextlib import ExitStack

import concourse.bass as bass
from concourse import mybir

F32, F32R, I32, U32 = mybir.dt.float32, mybir.dt.float32r, mybir.dt.int32, mybir.dt.uint32
ACT, ALU, AX = mybir.ActivationFunctionType, mybir.AluOpType, mybir.AxisListType

D = 2048
P = 128
KC = D // P
T_P, T_S = 512, 64
T = T_P + T_S
HALF = T // 2
NBLK = 5
ROWS = [128, 128, 128, 128, 64]
DB, DT = 8, 8
FOX, MEM, HD = 8, 4, 128
N_MEM = 256
PAGES, PAGE = 8, 128
N_PHYS = 80
WINDOWS = (2, 4, 8, 16)
STATE = 15
SCALE = float(HD) ** -0.5
EPS = 1e-6
NEG = -1e30
PH, PK, PTOP, NKEY = 8, 16, 16, 128
NEXP = PH * PTOP
N_EXPERTS = NKEY * NKEY
NTILE = N_EXPERTS // P
ND = T_P - P
GRP = 8
Q0, QM0, K0, V0, U0, F0, NZ = 0, 8, 12, 20, 28, 32, 33
NGATE = 3 * KC
RING = 6

BASE = 16512
O_IDENT, O_SMALL, O_MKT, O_MVTOK, O_GB, O_ATT, O_Z, O_R1 = 0, 512, 1536, 5632, 9728, 17920, 27168, 103200
O_X1 = O_ATT
O_CAUS, O_LF, O_CP, O_CS, O_CNT = O_ATT, O_ATT + 512, O_ATT + 2816, O_ATT + 4864, O_ATT + 8992
O_R2, O_W = O_R1 + KC * T * 4, O_R1 + 2 * KC * T * 4


def build(nc, a):
    ctx = ExitStack()

    def at(name, shape, dtype, offset):
        return nc.alloc_sbuf_tensor_at(name, shape, dtype, offset=BASE + offset)

    live = []

    def sem(name):
        live.append(nc.alloc_semaphore(name=name))
        return live[-1]

    def recycle():
        nc.clear_and_free_semaphores(live)
        live.clear()
        nc.all_engine_barrier()

    with ctx:
        gates_dram = nc.dram_tensor("gates_scratch", [NGATE, P, T], F32, kind="Internal").ap()
        acts_dram = nc.dram_tensor("activations_scratch", [NTILE, P, ND], F32, kind="Internal").ap()
        x1_dram = nc.dram_tensor("x1_scratch", [3 * P, D], F32, kind="Internal").ap()
        route_dram = nc.dram_tensor("routes_scratch", [N_EXPERTS * ND, 1], F32, kind="Internal").ap()

        ident = at("ident", [P, P], F32, O_IDENT)
        small = at("small", [P, 64], F32, O_SMALL)
        b_f, pool_scale = small[0:FOX, 0:1], small[:, 4:8]
        ss, ms, rstd = small[:, 8:13], small[:, 16:21], small[:, 24:29]
        ss_m, ms_m, rstd_m = small[:, 32:34], small[:, 36:38], small[:, 40:42]
        ss2, ms2, rstd2 = small[:, 44:49], small[:, 50:55], small[:, 56:61]
        mk_t = at("mk_t", [P, MEM, N_MEM], F32, O_MKT)
        mv_tok = at("mv_tok", [P, 2, MEM * HD], F32, O_MVTOK)
        g_row = at("g_row", [P, D], F32, O_GB)

        raw = at("w_raw", [P, 4, 1024], F32, O_W)
        w_hi = at("w_hi", [P, 2, 1024], F32R, O_W + 16384)
        w_lo = at("w_lo", [P, 2, 1024], F32R, O_W + 24576)

        def more_slots(tag, hi_at, lo_at):
            return at(f"w_hi_{tag}", [P, 2, 1024], F32R, hi_at), at(f"w_lo_{tag}", [P, 2, 1024], F32R, lo_at)

        acc = ctx.enter_context(nc.psum_tensor("acc", [P, 2, 2, 512], F32))
        tps = ctx.enter_context(nc.psum_tensor("tps", [P, 4, 512], F32))

        def stream_sems(tag, more=None):
            return dict(loaded=[sem(f"{tag}_w_loaded{k}") for k in range(4)], hi=sem(f"{tag}_hi_ready"),
                        lo=sem(f"{tag}_lo_ready"), mm=sem(f"{tag}_half_done"),
                        act=sem(f"{tag}_act_drained"), dve=sem(f"{tag}_dve_drained"), more=more, slots=4 if more else 2)

        def slot(q, j):
            k = j % q["slots"]
            return (w_hi[:, k, :], w_lo[:, k, :]) if k < 2 else tuple(t_[:, k - 2, :] for t_ in q["more"])

        def load_stripes(sp, w, n, q):
            nj = 2 * n
            for j in range(4):
                sp.dma_start(raw[:, j, :], w[j * P:(j + 1) * P, :]).then_inc(q["loaded"][j], 16)
            with sp.Fori(1, nj // 4) as i:
                for k in range(4):
                    sp.wait_ge(q["lo"], 4 * i + k - 3)
                    sp.dma_start(raw[:, k, :], w[bass.ds((4 * i + k) * P, P), :]).then_inc(q["loaded"][k], 16)
            for j in range(nj // 4 * 4, nj):
                sp.wait_ge(q["lo"], j - 3)
                sp.dma_start(raw[:, j % 4, :], w[j * P:(j + 1) * P, :]).then_inc(q["loaded"][j % 4], 16)

        def split_hi(act, i, s, q):
            for h in range(2):
                j = 2 * s + h
                act.wait_ge(q["loaded"][j % 4], 16 * (i + j // 4 + 1))
                act.wait_ge(q["mm"], 4 * i + j + 1)
                nc.scalar.activation(slot(q, j)[0], raw[:, j % 4, :], ACT.Copy).then_inc(q["hi"], 1)

        def split_lo(dve, i, s, q):
            for h in range(2):
                j = 2 * s + h
                dve.wait_ge(q["loaded"][j % 4], 16 * (i + j // 4 + 1))
                dve.wait_ge(q["hi"], 4 * i + j + 1)
                hi, lo = slot(q, j)
                nc.vector.tensor_tensor(lo, raw[:, j % 4, :], hi.bitcast(F32), ALU.subtract).then_inc(q["lo"], 1)

        def lagged(eng, n, split, drain):
            split(0, 0)
            pairs = (n - 1) // 2
            with eng.Fori(0, pairs) as i:
                split(i, 1)
                drain(i, 0)
                split(i, 2)
                drain(i, 1)
            if n % 2 == 0:
                split(pairs, 1)
                drain(pairs, 0)
                drain(pairs, 1)
            else:
                drain(pairs, 0)

        def multiply_half(pe, par, h, x_hi, x_lo, cols, q, out=None, before=None):
            for c in range(8):
                cc = 8 * h + c
                if before:
                    before(cc)
                wh, wl = (w[:, c * P:(c + 1) * P] for w in slot(q, 2 * par + h))
                for (p_, l_, r_) in ((0, wh, x_hi), (1, wh, x_lo), (2, wl, x_hi)):
                    for b, (c0, cn) in enumerate(cols):
                        dst, first, last_c = out(cc, b, cn) if out else (acc[:, par, b, 0:cn], 0, KC - 1)
                        last = nc.tensor.matmul(dst, l_, r_[:, cc, c0:c0 + cn],
                                                start=(cc == first and p_ == 0),
                                                stop=(cc == last_c and p_ == 2))
            last.then_inc(q["mm"], 1)

        HALVES = [(0, HALF), (HALF, HALF)]

        def multiply_stripes(pe, n, x_hi, x_lo, cols, q, use=("act", "dve"), between=None):
            def one(i, s, mid=True):
                for h in range(2):
                    pe.wait_ge(q["lo"], 4 * i + 2 * s + h + 1)
                    if h == 0:
                        for u in use:
                            pe.wait_ge(q[u], 2 * i + s + 1)
                    elif between and mid:
                        between(i, s - 1)
                    multiply_half(pe, s % 2, h, x_hi, x_lo, cols, q)

            pe.sem_inc(q["mm"], q["slots"])
            for u in use:
                pe.sem_inc(q[u], 2)
            one(0, 0, mid=False)
            pairs = (n - 1) // 2
            with pe.Fori(0, pairs) as i:
                one(i, 1)
                one(i, 2)
            if n % 2 == 0:
                one(pairs, 1)
            if between:
                between(pairs, (n - 1) % 2)

        def norm_transposed(tag, n_blk, rows, g_in, x_of, load, x_hi, x_lo, stat, xn):
            ss_, ms_, r_ = stat
            s_g, s_sq, s_ms, s_rt, s_r, s_xn = (sem(f"{tag}_{x}") for x in ("g_loaded", "squared", "mean", "root", "rstd", "normed"))
            s_tp, s_hi, s_lo = (sem(f"{tag}_{x}") for x in ("transposed", "hi_out", "lo_out"))
            s_x = [sem(f"{tag}_x_loaded{k}") for k in range(2)] if load else None
            with nc.Block() as block:
                @block.sync
                def _(sp):
                    sp.dma_start(g_row[:], g_in.rearrange("(o d) -> o d", o=1).to_broadcast([P, D])).then_inc(s_g, 16)
                    if tag == "mem":
                        for dst, name in ((ident[:], "ident"), (pool_scale, "pool_scale"), (b_f, "b_f")):
                            sp.dma_start(dst, a[name]).then_inc(s_g, 16)
                    if load:
                        for b in range(n_blk):
                            if b >= 2:
                                sp.wait_ge(s_xn, b - 1)
                            sp.dma_start(x_of(b), load(b)).then_inc(s_x[b % 2], 16)

                @block.scalar
                def _(act):
                    def squares(b):
                        if load:
                            act.wait_ge(s_x[b % 2], 16 * (b // 2 + 1))
                        if b >= 2:
                            act.wait_ge(s_tp, 4 * (b - 1))
                        nc.scalar.activation(xn[0:rows[b], b % 2, :], x_of(b), ACT.Square,
                                             accum_out=ss_[0:rows[b], b:b + 1]).then_inc(s_sq, 1)
                        act.wait_ge(s_ms, b + 1)
                        nc.scalar.activation(ms_[0:rows[b], b:b + 1], ms_[0:rows[b], b:b + 1], ACT.Sqrt).then_inc(s_rt, 1)

                    squares(0)
                    for b in range(n_blk):
                        if b + 1 < n_blk:
                            squares(b + 1)
                        for g in range(4):
                            act.wait_ge(s_tp, 4 * b + g + 1)
                            nc.scalar.activation(x_hi[:, 4 * g:4 * g + 4, b * P:b * P + rows[b]],
                                                 tps[:, g, 0:4 * rows[b]].rearrange("p (c t) -> p c t", c=4),
                                                 ACT.Copy).then_inc(s_hi, 1)

                @block.vector
                def _(dve):
                    def norm(b):
                        n = rows[b]
                        dve.wait_ge(s_sq, b + 1)
                        nc.vector.tensor_scalar(ms_[0:n, b:b + 1], ss_[0:n, b:b + 1], 1.0 / D, EPS, ALU.mult,
                                                ALU.add).then_inc(s_ms, 1)
                        dve.wait_ge(s_rt, b + 1)
                        nc.vector.reciprocal(r_[0:n, b:b + 1], ms_[0:n, b:b + 1]).then_inc(s_r, 1)
                        dve.wait_ge(s_r, b + 1)
                        nc.vector.scalar_tensor_tensor(out=xn[0:n, b % 2, :], in0=x_of(b), scalar=r_[0:n, b:b + 1],
                                                       in1=g_row[0:n, :], op0=ALU.mult, op1=ALU.mult).then_inc(s_xn, 1)

                    dve.wait_ge(s_g, 64 if tag == "mem" else 16)
                    norm(0)
                    for b in range(n_blk):
                        if b + 1 < n_blk:
                            norm(b + 1)
                        for g in range(4):
                            dve.wait_ge(s_hi, 4 * b + g + 1)
                            nc.vector.tensor_tensor(x_lo[:, 4 * g:4 * g + 4, b * P:b * P + rows[b]],
                                                    tps[:, g, 0:4 * rows[b]].rearrange("p (c t) -> p c t", c=4),
                                                    x_hi[:, 4 * g:4 * g + 4, b * P:b * P + rows[b]].bitcast(F32),
                                                    ALU.subtract).then_inc(s_lo, 1)

                @block.tensor
                def _(pe):
                    pe.wait_ge(s_g, 64 if tag == "mem" else 16)
                    for b in range(n_blk):
                        n = rows[b]
                        pe.wait_ge(s_xn, b + 1)
                        for g in range(4):
                            if b >= 1:
                                pe.wait_ge(s_lo, 4 * (b - 1) + g + 1)
                            for c in range(4):
                                last = nc.tensor.transpose(tps[:, g, c * n:(c + 1) * n],
                                                           xn[0:n, b % 2, (4 * g + c) * P:(4 * g + c + 1) * P],
                                                           ident[0:n, 0:n])
                            last.then_inc(s_tp, 1)

        z = at("z", [P, NZ, T], F32, O_Z)
        xb_m = at("xb_m", [P, 2, D], F32, O_Z)
        xn_m = at("xn_m", [P, 2, D], F32, O_Z + 16384)
        mn_hi = at("mn_hi", [P, KC, N_MEM], F32R, O_R1)
        mn_lo = at("mn_lo", [P, KC, N_MEM], F32R, O_R2)
        norm_transposed("mem", 2, [128, 128], a["mem_norm_g"], lambda b: xb_m[:, b % 2, :],
                        lambda b: a["mem_prompt"][b * P:(b + 1) * P, :], mn_hi, mn_lo, (ss_m, ms_m, rstd_m), xn_m)

        mkv_t = at("mkv_t", [P, 2 * MEM, N_MEM], F32, O_Z)
        q = stream_sems("mem")
        s_vt, s_vo, s_mout = sem("mem_v_transposed"), sem("mem_v_copied"), sem("mem_stored")
        with nc.Block() as block:
            @block.sync
            def _(sp):
                load_stripes(sp, a["w_mem"], 2 * MEM, q)
                sp.wait_ge(q["act"], 2 + 2 * MEM)
                sp.dma_start(a["mem_out"], mkv_t[:]).then_inc(s_mout, 16)
                sp.wait_ge(s_mout, 16)

            def drain_mem(act, i, s):
                act.wait_ge(q["mm"], 4 * i + 2 * s + 4)
                nc.scalar.activation(mkv_t[:, bass.ds(2 * i + s, 1), :], acc[:, s % 2, 0:1, 0:N_MEM], ACT.Copy).then_inc(q["act"], 1)

            @block.scalar
            def _(act):
                lagged(act, 2 * MEM, lambda i, s: split_hi(act, i, s, q), lambda i, s: drain_mem(act, i, s))
                act.wait_ge(q["act"], 2 + MEM)
                nc.scalar.activation(mk_t[:], mkv_t[:, 0:MEM, :], ACT.Copy)

            @block.vector
            def _(dve):
                with dve.Fori(0, MEM) as i:
                    split_lo(dve, i, 0, q)
                    split_lo(dve, i, 1, q)
                for m in range(2):
                    dve.wait_ge(s_vt, m + 1)
                    nc.vector.tensor_copy(mv_tok[:, m, :], tps[:, m, :]).then_inc(s_vo, 1)

            @block.tensor
            def _(pe):
                multiply_stripes(pe, 2 * MEM, mn_hi, mn_lo, [(0, N_MEM)], q, use=("act",))
                pe.wait_ge(q["act"], 2 + 2 * MEM)
                for m in range(2):
                    for h in range(MEM):
                        last = nc.tensor.transpose(tps[:, m, h * P:(h + 1) * P], mkv_t[:, MEM + h, m * P:(m + 1) * P], ident[:])
                    last.then_inc(s_vt, 1)

        recycle()

        x_hi = at("x_hi", [P, KC, T], F32R, O_R1)
        x_lo = at("x_lo", [P, KC, T], F32R, O_R2)
        xb = at("xb", [P, 2, D], F32, O_Z)
        xn = at("xn", [P, 2, D], F32, O_Z + 16384)
        norm_transposed("mix", NBLK, ROWS, a["norm_mix_g"], lambda b: xb[0:ROWS[b], b % 2, :],
                        lambda b: a["x"][b * P:b * P + ROWS[b], :], x_hi, x_lo, (ss, ms, rstd), xn)

        def drain_to(dst_t, q):
            def by_act(act, i, s):
                act.wait_ge(q["mm"], 4 * i + 2 * s + 2 + q["slots"])
                nc.scalar.activation(dst_t[:, bass.ds(2 * i + s, 1), 0:HALF], acc[:, s % 2, 0, 0:HALF], ACT.Copy).then_inc(q["act"], 1)

            def by_dve(dve, i, s):
                dve.wait_ge(q["mm"], 4 * i + 2 * s + 2 + q["slots"])
                nc.vector.tensor_copy(dst_t[:, bass.ds(2 * i + s, 1), HALF:T], acc[:, s % 2, 1, 0:HALF]).then_inc(q["dve"], 1)
            return by_act, by_dve

        q1 = stream_sems("proj")
        act_z, dve_z = drain_to(z, q1)
        with nc.Block() as block:
            @block.sync
            def _(sp):
                load_stripes(sp, a["w_z"], NZ, q1)

            @block.scalar
            def _(act):
                lagged(act, NZ, lambda i, s: split_hi(act, i, s, q1), lambda i, s: act_z(act, i, s))

            @block.vector
            def _(dve):
                lagged(dve, NZ, lambda i, s: split_lo(dve, i, s, q1), lambda i, s: dve_z(dve, i, s))

            @block.tensor
            def _(pe):
                multiply_stripes(pe, NZ, x_hi, x_lo, HALVES, q1)

        gate_out = at("gate_out", [P, 2, T], F32, O_GB)
        q2 = stream_sems("gate")
        c_s = at("c_s", [DB * FOX, PAGES * PAGE + DT], F32, O_CS)
        pages = at("pages", [DB * FOX, PAGES], I32, O_SMALL + 768)
        head_row = at("head_of_row", [DB * FOX, 8], F32, O_SMALL + 800)
        s_gfree, s_gst, s_zst = sem("gate_buffer_free"), sem("gate_stored"), sem("z_stored")
        s_pgl, s_pgi, s_lfg = sem("pages_loaded"), sem("page_rows"), sem("past_logf_gathered")
        with nc.Block() as block:
            @block.sync
            def _(sp):
                load_stripes(sp, a["w_gate"], NGATE, q2)

            @block.gpsimd
            def _(pool):
                pool.sem_inc(s_gfree, 2)
                pool.dma_start(a["z_out"], z[:, K0:F0, :]).then_inc(s_zst, 16)
                by_sample = a["page_table"].rearrange("o (b j) -> b (o j)", b=DB)
                for b in range(DB):
                    pool.dma_start(pages[b * FOX:(b + 1) * FOX, :], by_sample[b:b + 1, :].to_broadcast([FOX, PAGES])).then_inc(s_pgl, 16)
                pool.dma_start(head_row[:], a["head_row"]).then_inc(s_pgl, 16)
                pool.wait_ge(s_pgl, 16 * (DB + 1))
                nc.gpsimd.tensor_scalar(pages[:], pages[:], float(FOX), head_row[:, 0:1], ALU.mult, ALU.add).then_inc(s_pgi, 1)
                pool.wait_ge(s_pgi, 1)
                for j in range(PAGES):
                    pool.indirect_dma_start(c_s[:, j * PAGE:(j + 1) * PAGE], None, a["cache_logf"],
                                            bass.IndirectOffsetOnAxis(ap=pages[:, j:j + 1], axis=0)).then_inc(s_lfg, 16)
                with pool.Fori(0, NGATE // 2) as i:
                    for s in range(2):
                        pool.wait_ge(q2["act"], 2 * i + s + 3)
                        pool.dma_start(gates_dram[bass.ds(2 * i + s, 1), :, :].rearrange("o p t -> p (o t)"),
                                       gate_out[:, s, :]).then_inc(s_gst, 16)
                        pool.wait_ge(s_gst, 32 * i + 16 * s + 16)
                        pool.sem_inc(s_gfree, 1)
                pool.wait_ge(s_zst, 16)
                pool.wait_ge(s_lfg, 16 * PAGES)

            def drain_gate(act, i, s):
                act.wait_ge(q2["mm"], 4 * i + 2 * s + 4)
                act.wait_ge(s_gfree, 2 * i + s + 1)
                nc.scalar.activation(gate_out[:, s % 2, :].rearrange("p (b t) -> p b t", b=2), acc[:, s % 2, :, 0:HALF],
                                     ACT.Sigmoid).then_inc(q2["act"], 1)

            @block.scalar
            def _(act):
                lagged(act, NGATE, lambda i, s: split_hi(act, i, s, q2), lambda i, s: drain_gate(act, i, s))

            @block.vector
            def _(dve):
                with dve.Fori(0, NGATE // 2) as i:
                    split_lo(dve, i, 0, q2)
                    split_lo(dve, i, 1, q2)

            @block.tensor
            def _(pe):
                multiply_stripes(pe, NGATE, x_hi, x_lo, HALVES, q2, use=("act",))

        recycle()

        negsel_p = at("negsel_p", [FOX, FOX, P], F32, O_GB)
        negsel_s = at("negsel_s", [DB * FOX, DB, FOX * DT], F32, O_GB + 4096)
        smask = at("smask", [FOX * DT, DB, T_S], F32, O_GB + 6144)
        causal = at("causal", [P, P], F32, O_CAUS)
        logf = at("logf", [FOX, T], F32, O_LF)
        c_p = at("c_p", [FOX, T_P], F32, O_CP)
        cnt_inv = at("cnt_inv", [P, 4, 16], F32, O_CNT)
        b_t = at("b_t", [P, KC, T], F32, O_R1)
        v_tok = at("v_tok", [P, NBLK, FOX * HD], F32, O_R2)
        O_K = O_R2 + NBLK * FOX * HD * 4
        PW, SW = 16 + T_P, 24
        ua = at("ua", [P, PW + DB * SW], F32, O_K)
        ub = at("ub", [P, PW + DB * SW], F32, O_K + 2880)
        uc = at("uc", [P, PW + DB * SW], F32, O_K + 5760)
        pooled = at("pooled", [P, T], F32, O_K + 8640)
        pool_w = at("pool_w", [P, 4, P], F32, O_K + 11008)
        ones = at("ones", [DB * FOX, PAGES * PAGE + DT], F32, O_K + 13120)
        lt1 = at("lt1", [FOX, T], F32, O_K + 21440)
        lt2 = at("lt2", [FOX, T], F32, O_K + 23808)
        pt = at("pt", [1, DB * PAGES], I32, O_SMALL + 512)
        st_buf = at("state_buf", [P, 4, DB, STATE], F32, O_W + 20000)
        st_new = at("state_new", [P, 4, DB, STATE], F32, O_W + 22016)
        t16 = at("pool_head", [P, 16], F32, O_W + 24000)

        s_pc, s_pt, s_pln, s_lfo = (sem(f"prep_{x}") for x in ("consts", "page_table", "new_logf", "logf_stored"))
        s_fa, s_fv, s_init = sem("prep_logf_act"), sem("prep_logf_dve"), sem("prep_cleared")
        s_un, s_st, s_pd, s_ym, s_yo = (sem(f"pool_{x}") for x in ("chain", "state_loaded", "pooled", "mixed", "drained"))
        s_sn = sem("state_assembled")
        s_vtp, s_vtc = sem("v_transposed"), sem("v_copied")
        with nc.Block() as block:
            @block.sync
            def _(sp):
                sp.dma_start(pt[:], a["page_table"]).then_inc(s_pt, 16)
                for dst, name in ((negsel_p[:], "negsel_p"), (negsel_s[:], "negsel_s"), (smask[:], "smask"), (causal[:], "causal"),
                                  (cnt_inv[:], "cnt_inv"), (pool_w[:], "pool_w")):
                    sp.dma_start(dst, a[name]).then_inc(s_pc, 16)
                sp.dma_start(st_buf[:], a["state_pool"]).then_inc(s_st, 16)
                sp.wait_ge(s_pt, 16)

            @block.gpsimd
            def _(pool):
                nc.gpsimd.memset(ones[:], 1.0).then_inc(s_init, 1)
                pool.wait_ge(s_st, 16)
                for g in range(4):
                    nc.gpsimd.tensor_copy(st_new[:, g, :, 0:STATE - DT], st_buf[:, g, :, DT:STATE])
                    last = nc.gpsimd.tensor_copy(st_new[:, g, :, STATE - DT:STATE],
                                                 z[:, U0 + g, T_P:T].rearrange("p (b t) -> p b t", b=DB))
                last.then_inc(s_sn, 1)
                pool.wait_ge(s_sn, 1)
                pool.dma_start(a["state_out"], st_new[:]).then_inc(s_lfo, 16)
                pool.wait_ge(s_fv, 3)
                pool.dma_start(a["logf_out"], logf[:]).then_inc(s_lfo, 16)
                for b in range(DB):
                    pool.dma_start(c_s[b * FOX:(b + 1) * FOX, PAGES * PAGE:],
                                   logf[:, T_P + b * DT:T_P + (b + 1) * DT]).then_inc(s_pln, 16)
                pool.wait_ge(s_lfo, 32)

            @block.scalar
            def _(act):
                act.wait_ge(s_fv, 1)
                nc.scalar.activation(lt2[:], lt1[:], ACT.Abs).then_inc(s_fa, 1)
                act.wait_ge(s_fa, 1)
                nc.scalar.activation(lt2[:], lt2[:], ACT.Exp, scale=-1.0).then_inc(s_fa, 1)
                act.wait_ge(s_fa, 2)
                act.wait_ge(s_fv, 2)
                nc.scalar.activation(lt2[:], lt2[:], ACT.Ln, bias=1.0).then_inc(s_fa, 1)
                for n in range(2 * NBLK):
                    r = ROWS[n // 2]
                    act.wait_ge(s_vtp, n + 1)
                    nc.scalar.activation(v_tok[0:r, n // 2, (n % 2) * 512:(n % 2 + 1) * 512], tps[0:r, n % 2, :],
                                         ACT.Copy).then_inc(s_vtc, 1)

            @block.vector
            def _(dve):
                chain = [0]

                def link(ins):
                    chain[0] += 1
                    ins.then_inc(s_un, 1)
                    dve.wait_ge(s_un, chain[0])

                nc.vector.tensor_scalar(lt1[:], z[0:FOX, F0, :], b_f, None, ALU.add).then_inc(s_fv, 1)
                dve.wait_ge(s_fa, 1)
                nc.vector.tensor_scalar(lt1[:], lt1[:], 0.0, None, ALU.min).then_inc(s_fv, 1)
                dve.wait_ge(s_fa, 3)
                dve.wait_ge(s_fv, 2)
                nc.vector.tensor_tensor(logf[:], lt1[:], lt2[:], ALU.subtract).then_inc(s_fv, 1)
                dve.wait_ge(s_fv, 3)
                dve.wait_ge(s_init, 1)
                nc.vector.tensor_tensor_scan(c_p[:], ones[0:FOX, 0:T_P], logf[:, 0:T_P], 0.0, ALU.mult, ALU.add)
                link(nc.vector.memset(ua[:, 0:16], 0.0))
                dve.wait_ge(s_pc, 96)
                dve.wait_ge(s_st, 16)
                for g, w in enumerate(WINDOWS):
                    u = z[:, U0 + g, :]
                    u_s = u[:, T_P:T].rearrange("p (b t) -> p b t", b=DB)
                    nc.vector.tensor_copy(ua[:, 16:PW], u[:, 0:T_P])
                    nc.vector.tensor_copy(ua[:, PW:].rearrange("p (b c) -> p b c", b=DB)[:, :, 16:SW], u_s)
                    link(nc.vector.tensor_copy(ua[:, PW:].rearrange("p (b c) -> p b c", b=DB)[:, :, 1:16], st_buf[:, g]))
                    src, sh = ua, 1
                    lo = 1
                    while sh < w:
                        dst = ub if src is not ub else uc
                        s3 = src[:, PW:].rearrange("p (b c) -> p b c", b=DB)
                        d3 = dst[:, PW:].rearrange("p (b c) -> p b c", b=DB)
                        nc.vector.tensor_tensor(dst[:, lo + sh - 1:PW], src[:, lo + sh - 1:PW], src[:, lo - 1:PW - sh], ALU.add)
                        link(nc.vector.tensor_tensor(d3[:, :, lo + sh:SW], s3[:, :, lo + sh:SW], s3[:, :, lo:SW - sh], ALU.add))
                        src, lo, sh = dst, lo + sh, 2 * sh
                    if g >= 1:
                        dve.wait_ge(s_ym, g)
                    link(nc.vector.tensor_tensor(t16[:], src[:, 16:32], cnt_inv[:, g, :], ALU.mult))
                    nc.vector.tensor_tensor(pooled[:, 0:16], t16[:], u[:, 0:16], ALU.subtract)
                    nc.vector.scalar_tensor_tensor(out=pooled[:, 16:T_P], in0=src[:, 32:PW], scalar=1.0 / w, in1=u[:, 16:T_P],
                                                   op0=ALU.mult, op1=ALU.subtract)
                    nc.vector.scalar_tensor_tensor(out=pooled[:, T_P:T].rearrange("p (b t) -> p b t", b=DB),
                                                   in0=src[:, PW:].rearrange("p (b c) -> p b c", b=DB)[:, :, 16:SW],
                                                   scalar=1.0 / w, in1=u_s, op0=ALU.mult, op1=ALU.subtract).then_inc(s_pd, 1)
                    dve.wait_ge(s_ym, g + 1)
                    nc.vector.tensor_scalar(b_t[:, g, :].rearrange("p (b t) -> p b t", b=2), acc[:, 0, :, 0:HALF],
                                            pool_scale[:, g:g + 1], None, ALU.mult).then_inc(s_yo, 1)
                dve.wait_ge(s_pln, 16 * DB)
                nc.vector.tensor_tensor_scan(c_s[:], ones[:], c_s[:], 0.0, ALU.mult, ALU.add)

            @block.tensor
            def _(pe):
                for n in range(2 * NBLK):
                    r = ROWS[n // 2]
                    if n >= 2:
                        pe.wait_ge(s_vtc, n - 1)
                    for k in range(4):
                        c0 = (n // 2) * P
                        last = nc.tensor.transpose(tps[0:r, n % 2, k * P:(k + 1) * P], z[:, V0 + 4 * (n % 2) + k, c0:c0 + r], ident[:])
                    last.then_inc(s_vtp, 1)
                pe.wait_ge(s_pc, 96)
                for g in range(4):
                    pe.wait_ge(s_pd, g + 1)
                    if g >= 1:
                        pe.wait_ge(s_yo, g)
                    for b in range(2):
                        last = nc.tensor.matmul(acc[:, 0, b, 0:HALF], pool_w[:, g, :], pooled[:, b * HALF:(b + 1) * HALF],
                                                start=True, stop=True)
                    last.then_inc(s_ym, 1)

        recycle()

        k_ring = at("k_ring", [P, RING, 1024], F32, O_K)
        v_ring = at("v_ring", [P, RING, 1024], F32, O_Z + V0 * T * 4)
        place = [O_K + RING * 4096]

        def then(name, shape, dtype):
            size = int(np.prod(shape[1:])) * 4
            t_ = at(name, shape, dtype, place[0])
            place[0] += (size + 31) // 32 * 32
            return t_

        probs_p = then("probs_prompt", [P, 3, T_P], F32)
        probs_s = then("probs_sample", [P, PAGES * PAGE + T_S], F32)
        pt_p = then("probs_t_prompt", [P, 2, 4, P], F32)
        pt_s = then("probs_t_sample", [P, 9, P + 32], F32)
        qz = then("qz", [P, 2, FOX * 72], F32)
        stat = {c: then(f"stat_{c}", [P, 2, 4], F32) for c in "ps"}
        rsum = {c: then(f"rsum_{c}", [P, 2, 4], F32) for c in "ps"}
        nmax = {c: then(f"nmax_{c}", [P, 2], F32) for c in "ps"}
        rinv = {c: then(f"rinv_{c}", [P, 2], F32) for c in "ps"}
        O_V = O_Z + V0 * T * 4 + RING * 4096
        o_s = at("sample_result", [P, 512], F32, O_V)
        qzm = at("qzm", [P, 4, MEM * 40], F32, O_V + 2048)
        assert place[0] <= O_W + 35904

        PAIRS, QUADS = DB // 2, DB // 4
        units = {"p": [("fox", h, i) for i in range(4) for h in range(FOX)] + [("mem", h, i) for i in range(4) for h in range(MEM)],
                 "s": [("sfox", g, 0) for g in range(PAIRS)] + [("smem", g, 0) for g in range(QUADS)]}
        NP, NS = len(units["p"]), len(units["s"])

        def keys(c, n):
            kind, _, i = units[c][n]
            return {"fox": (i + 1) * P, "mem": N_MEM, "sfox": PAGES * PAGE + T_S, "smem": N_MEM}[kind]

        def chunks(c, n):
            return (keys(c, n) + P - 1) // P

        def t_groups(c, n):
            return (chunks(c, n) + 3) // 4

        k_items = {u: [(u, b, k) for b in range(2) for k in (*range(PAGES), -1)] if u < PAIRS else [(u, b, 0) for b in range(4)] for u in range(NS)}
        STEPS = NP + 3
        k_at, v_at = {p: [] for p in range(STEPS)}, {p: [] for p in range(STEPS)}
        soft_at, turn_at, out_at = {}, {}, {}
        for u, k0, kn, s0, v0, vn in ((0, 0, 2, 9, 10, 2), (1, 10, 2, 19, 20, 2), (2, 20, 2, 29, 30, 2), (3, 30, 2, 39, 40, 4),
                                      (4, 40, 2, 42, 45, 2), (5, 43, 2, 46, 47, 2)):
            for j, item in enumerate(k_items[u]):
                k_at[k0 + j // kn].append(item)
                v_at[v0 + j // vn].append(item)
            soft_at[s0], turn_at[v0] = u, u
            out_at[v0 + (len(k_items[u]) - 1) // vn + 2] = u
        turns = []
        for p in range(STEPS):
            turns += [("p", p - 2, 0)] if 0 <= p - 2 < NP else []
            turns += [("s", turn_at[p], g) for g in range(t_groups("s", turn_at[p]))] if p in turn_at else []
            turns += [("o", out_at[p], 0)] if p in out_at else []
        place_of = {t_: n for n, t_ in enumerate(turns)}
        page_no = {}
        for u in range(NS):
            for item in k_items[u]:
                if item[2] >= 0:
                    page_no[item] = len(page_no)

        s_kl = [sem(f"k_page_loaded{k}") for k in range(RING)]
        s_vl = [sem(f"v_page_loaded{k}") for k in range(RING)]
        s_ku, s_vu = sem("k_page_used"), sem("v_page_used")
        s_qz, s_qc = sem("q_rows_placed"), sem("q_rows_cleared")
        S = {c: {x: sem(f"att_{w}_{x}") for x in ("logits", "max", "negmax", "exps", "recips", "probs", "weighted", "drained")}
             for c, w in (("p", "prompt"), ("s", "sample"))}
        s_t, s_tc = sem("att_transposed"), sem("att_transposed_copied")

        s_logits = [acc[:, 0, 0, :], acc[:, 0, 1, :], acc[:, 1, 0, :]]
        p_logits = [acc[:, 1, 1, :], tps[:, 0, :]]
        tbank, p_out, s_out = tps[:, 1, :], tps[:, 2, :], tps[:, 3, :]

        def parts_of(c, n):
            nk = keys(c, n)
            return [(bank[:, 0:min(512, nk - 512 * j)], 512 * j) for j, bank in
                    enumerate([p_logits[n % 2]] if c == "p" else s_logits) if nk > 512 * j]

        def probs_of(c, n):
            return probs_p[:, n % 3, :] if c == "p" else probs_s[:]

        def source(item, which, eng):
            u, b, k = item
            if u < PAIRS:
                row = (2 * u + b) * PAGES + k
                page = eng.value_load(pt[0:1, row:row + 1], min_val=0, max_val=N_PHYS - 1)
                return a["cache_" + which][bass.ds(page * P, P), :]
            row = 4 * (u - PAIRS) + b
            return a["mem_cache_" + which][row * P:(row + 1) * P, :]

        with nc.Block() as block:
            @block.sync
            def _(sp):
                for item, j in page_no.items():
                    if j >= RING:
                        sp.wait_ge(s_ku, j - RING + 1)
                    sp.dma_start(k_ring[:, j % RING, :], source(item, "k", sp)).then_inc(s_kl[j % RING], 16)

            @block.gpsimd
            def _(pool):
                def place_q(u):
                    nb, nh, q0, dst = (2, FOX, Q0, qz) if u < PAIRS else (4, MEM, QM0, qzm)
                    if u not in (0, PAIRS):
                        pool.wait_ge(S["s"]["logits"], u)
                    for b in range(nb):
                        c0 = T_P + ((u if u < PAIRS else u - PAIRS) * nb + b) * DT
                        last = nc.gpsimd.tensor_copy(dst[:, b, :].rearrange("p (h c) -> p h c", h=nh)[:, :, 0:DT], z[:, q0:q0 + nh, c0:c0 + DT])
                    last.then_inc(s_qz, 1)

                nc.gpsimd.memset(qz[:], 0.0).then_inc(s_qc, 1)
                nc.gpsimd.memset(qzm[:], 0.0).then_inc(s_qc, 1)
                nc.gpsimd.memset(pt_s[:, :, P:], 0.0).then_inc(s_qc, 1)
                pool.wait_ge(s_qc, 2)
                place_q(0)
                for u in range(NS):
                    first = True
                    for item in k_items[u]:
                        if item[2] < 0:
                            continue
                        j = page_no[item]
                        if first:
                            first = False
                            if u + 1 < NS:
                                place_q(u + 1)
                        if j >= RING:
                            pool.wait_ge(s_vu, j - RING + 1)
                        pool.dma_start(v_ring[:, j % RING, :], source(item, "v", pool)).then_inc(s_vl[j % RING], 16)

            @block.vector
            def _(dve):
                def negmax(c, n):
                    q = S[c]
                    dve.wait_ge(q["logits"], n + 1)
                    if n >= 2:
                        dve.wait_ge(q["exps"], n - 1)
                    parts = parts_of(c, n)
                    for j, (src, _) in enumerate(parts):
                        last = nc.vector.reduce_max(stat[c][:, n % 2, j:j + 1], src, AX.X)
                    last.then_inc(q["max"], 1)
                    dve.wait_ge(q["max"], 2 * n + 1)
                    if len(parts) > 1:
                        nc.vector.reduce_max(stat[c][:, n % 2, 3:4], stat[c][:, n % 2, 0:3], AX.X).then_inc(q["max"], 1)
                        dve.wait_ge(q["max"], 2 * n + 2)
                    else:
                        dve.sem_inc(q["max"], 1)
                    m = 3 if len(parts) > 1 else 0
                    nc.vector.tensor_scalar(nmax[c][:, n % 2:n % 2 + 1], stat[c][:, n % 2, m:m + 1], -SCALE, None, ALU.mult).then_inc(q["negmax"], 1)

                def normalise(c, n):
                    q = S[c]
                    dve.wait_ge(q["exps"], n + 1)
                    parts = len(parts_of(c, n))
                    m = 3 if parts > 1 else 0
                    if parts > 1:
                        nc.vector.reduce_sum(rsum[c][:, n % 2, 3:4], rsum[c][:, n % 2, 0:parts], AX.X).then_inc(q["recips"], 1)
                        dve.wait_ge(q["recips"], 2 * n + 1)
                    else:
                        dve.sem_inc(q["recips"], 1)
                    nc.vector.reciprocal(rinv[c][:, n % 2:n % 2 + 1], rsum[c][:, n % 2, m:m + 1]).then_inc(q["recips"], 1)
                    dve.wait_ge(q["recips"], 2 * n + 2)
                    w = probs_of(c, n)[:, 0:keys(c, n)]
                    nc.vector.tensor_scalar(w, w, rinv[c][:, n % 2:n % 2 + 1], None, ALU.mult).then_inc(q["probs"], 1)

                def drain(n):
                    kind, h, i = units["p"][n]
                    dve.wait_ge(S["p"]["weighted"], n + 1)
                    c = (4 if kind == "fox" else 12) + h
                    nc.vector.tensor_copy(b_t[:, c, i * P:(i + 1) * P], p_out[:, 0:P]).then_inc(S["p"]["drained"], 1)

                def drain_sample(u):
                    dve.wait_ge(S["s"]["weighted"], u + 1)
                    if u:
                        dve.wait_ge(s_t, place_of[("o", u - 1, 0)] + 1)
                    nc.vector.tensor_copy(o_s[:], s_out[:]).then_inc(S["s"]["drained"], 1)

                for p in range(STEPS):
                    if 1 <= p <= NP:
                        normalise("p", p - 1)
                    if p >= 1 and v_at[p - 1] and v_at[p - 1][-1] == k_items[v_at[p - 1][-1][0]][-1]:
                        drain_sample(v_at[p - 1][-1][0])
                    if p < NP:
                        negmax("p", p)
                    if p in soft_at:
                        negmax("s", soft_at[p])
                    if p >= 3:
                        drain(p - 3)
                    if p in soft_at:
                        normalise("s", soft_at[p])

            @block.scalar
            def _(act):
                def exps(c, n):
                    q = S[c]
                    act.wait_ge(q["negmax"], n + 1)
                    old = n - (3 if c == "p" else 1)
                    if old >= 0:
                        act.wait_ge(s_t, place_of[(c, old, t_groups(c, old) - 1)] + 1)
                    if n >= 2:
                        act.wait_ge(q["recips"], 2 * (n - 1))
                    for j, (src, k0) in enumerate(parts_of(c, n)):
                        ins = nc.scalar.activation(probs_of(c, n)[:, k0:k0 + src.shape[1]], src, ACT.Exp,
                                                   bias=nmax[c][:, n % 2:n % 2 + 1], scale=SCALE,
                                                   accum_out=rsum[c][:, n % 2, j:j + 1])
                    ins.then_inc(q["exps"], 1)

                def copy_turned(c, n, g):
                    act.wait_ge(s_t, place_of[(c, n, g)] + 1)
                    depth = 2 if c == "p" else 1
                    if c == "s":
                        act.wait_ge(s_qc, 3)
                    if g == 0 and n >= depth:
                        act.wait_ge(S[c]["weighted"], n - depth + 1)
                    dst = pt_p[:, n % 2] if c == "p" else pt_s[:]
                    nch = min(4, chunks(c, n) - 4 * g)
                    rows = min(P, keys(c, n) - 4 * g * P)
                    nc.scalar.activation(dst[0:rows, 4 * g:4 * g + nch, 0:P], tbank[0:rows, 0:nch * P].rearrange("p (c t) -> p c t", c=nch),
                                         ACT.Copy).then_inc(s_tc, 1)

                def place_result(u):
                    kind, g, _ = units["s"][u]
                    act.wait_ge(s_t, place_of[("o", u, 0)] + 1)
                    nb, nh, c = (2, FOX, 4) if kind == "sfox" else (4, MEM, 12)
                    t0 = T_P + g * nb * DT
                    for b in range(nb):
                        if kind == "sfox":
                            src = tbank[:, b * 256:(b + 1) * 256].rearrange("p (h x) -> p h x", h=FOX)[:, :, 0:DT]
                            last = nc.scalar.activation(b_t[:, c:c + nh, t0 + b * DT:t0 + (b + 1) * DT], src, ACT.Copy)
                        else:
                            for h in range(MEM):
                                r0 = h * P + b * 32 + h * DT
                                last = nc.scalar.activation(b_t[:, c + h, t0 + b * DT:t0 + (b + 1) * DT], tbank[:, r0:r0 + DT], ACT.Copy)
                    last.then_inc(s_tc, 1)

                for p in range(STEPS):
                    if 0 <= p - 2 < NP:
                        copy_turned("p", p - 2, 0)
                    if p < NP:
                        exps("p", p)
                    if p in turn_at:
                        for g in range(t_groups("s", turn_at[p])):
                            copy_turned("s", turn_at[p], g)
                    if p in out_at:
                        place_result(out_at[p])
                    if p in soft_at:
                        exps("s", soft_at[p])

            @block.tensor
            def _(pe):
                def make_logits(n):
                    kind, h, i = units["p"][n]
                    bank = p_logits[n % 2]
                    if n >= 2:
                        pe.wait_ge(S["p"]["exps"], n - 1)
                    if kind == "fox":
                        nk = keys("p", n)
                        nc.tensor.matmul(bank[:, 0:nk], z[:, Q0 + h, i * P:(i + 1) * P], z[:, K0 + h, 0:nk], start=True, stop=False)
                        nc.tensor.matmul(bank[:, 0:nk], negsel_p[:, h, :], c_p[:, 0:nk], start=False, stop=False)
                        last = nc.tensor.matmul(bank[:, i * P:nk], ident[:], causal[:], start=False, stop=True)
                    else:
                        last = nc.tensor.matmul(bank[:, 0:N_MEM], z[:, QM0 + h, i * P:(i + 1) * P], mk_t[:, h, :], start=True, stop=True)
                    last.then_inc(S["p"]["logits"], 1)

                def keys_item(item):
                    u, b, k = item
                    if item == k_items[u][0]:
                        pe.wait_ge(s_qz, u + 1)
                        if u:
                            pe.wait_ge(S["s"]["exps"], u)
                    j = page_no.get(item)
                    if j is not None:
                        pe.wait_ge(s_kl[j % RING], 16 * (j // RING + 1))
                    done = item == k_items[u][-1]
                    if u >= PAIRS:
                        for hh in range(MEM):
                            last = nc.tensor.matmul(s_logits[0][b * 32:(b + 1) * 32, 0:N_MEM], qzm[:, b, hh * 32:(hh + 1) * 32],
                                                    k_ring[:, j % RING, hh * N_MEM:(hh + 1) * N_MEM],
                                                    start=(hh == 0), stop=(hh == MEM - 1), tile_position=(0, b * 32))
                        last.then_inc(s_ku, 1)
                        if done:
                            pe.wait_ge(s_ku, j + 1)
                            pe.sem_inc(S["s"]["logits"], 1)
                        return
                    r0 = b * 64
                    if k >= 0:
                        dst = s_logits[k // 4][r0:r0 + 64, (k % 4) * P:(k % 4 + 1) * P]
                        nc.tensor.matmul(dst, negsel_s[:, 2 * u + b, :], c_s[:, k * PAGE:(k + 1) * PAGE], start=True, stop=False)
                        for hh in range(FOX):
                            last = nc.tensor.matmul(dst, qz[:, b, hh * 64:(hh + 1) * 64], k_ring[:, j % RING, hh * P:(hh + 1) * P],
                                                    start=False, stop=(hh == FOX - 1))
                        last.then_inc(s_ku, 1)
                        return
                    dst = s_logits[2][r0:r0 + 64, 0:T_S]
                    nc.tensor.matmul(dst, ident[0:64, 0:64], smask[:, 2 * u + b, :], start=True, stop=False)
                    nc.tensor.matmul(dst, negsel_s[:, 2 * u + b, :],
                                     c_s[:, PAGES * PAGE:].rearrange("p (o t) -> p o t", o=1).to_broadcast([64, DB, DT]),
                                     start=False, stop=False)
                    for hh in range(FOX):
                        last = nc.tensor.matmul(dst, qz[:, b, hh * 64:(hh + 1) * 64], z[:, K0 + hh, T_P:T],
                                                start=False, stop=(hh == FOX - 1))
                    if done:
                        last.then_inc(S["s"]["logits"], 1)

                def turn(c, n, g):
                    pe.wait_ge(S[c]["probs"], n + 1)
                    if place_of[(c, n, g)]:
                        pe.wait_ge(s_tc, place_of[(c, n, g)])
                    for k in range(4 * g, min(4 * g + 4, chunks(c, n))):
                        w = min(P, keys(c, n) - k * P)
                        last = nc.tensor.transpose(tbank[0:w, (k % 4) * P:(k % 4 + 1) * P], probs_of(c, n)[:, k * P:k * P + w], ident[:])
                    last.then_inc(s_t, 1)

                def weigh(n):
                    kind, h, i = units["p"][n]
                    pe.wait_ge(s_tc, place_of[("p", n, 0)] + 1)
                    if n >= 1:
                        pe.wait_ge(S["p"]["drained"], n)
                    nch = chunks("p", n)
                    v = v_tok if kind == "fox" else mv_tok
                    for k in range(nch):
                        last = nc.tensor.matmul(p_out[:, 0:P], v[:, k, h * HD:(h + 1) * HD], pt_p[:, n % 2, k, :],
                                                start=(k == 0), stop=(k == nch - 1))
                    last.then_inc(S["p"]["weighted"], 1)

                def values_item(item):
                    u, b, k = item
                    if item == k_items[u][0]:
                        pe.wait_ge(s_tc, place_of[("s", u, t_groups("s", u) - 1)] + 1)
                        pe.wait_ge(s_qc, 3)
                        if u:
                            pe.wait_ge(S["s"]["drained"], u)
                    j = page_no.get(item)
                    if j is not None:
                        pe.wait_ge(s_vl[j % RING], 16 * (j // RING + 1))
                    done = item == k_items[u][-1]
                    if u >= PAIRS:
                        for c in range(2):
                            last = nc.tensor.matmul(s_out[b * 32:(b + 1) * 32, :], pt_s[:, c, b * 32:(b + 1) * 32],
                                                    v_ring[:, j % RING, c * 512:(c + 1) * 512], start=(c == 0), stop=(c == 1),
                                                    tile_position=(0, b * 32))
                        last.then_inc(s_vu, 1)
                        if done:
                            pe.wait_ge(s_vu, j + 1)
                            pe.sem_inc(S["s"]["weighted"], 1)
                        return
                    for hh in range(FOX):
                        r0, q0, c0 = b * 64 + hh * DT, 32 * (hh % 4), (2 * b + hh // 4) * HD
                        if k >= 0:
                            l_, r_ = pt_s[:, k, r0:r0 + 32], v_ring[:, j % RING, hh * HD:(hh + 1) * HD]
                        else:
                            l_, r_ = pt_s[0:64, PAGES, r0:r0 + 32], v_tok[0:64, 4, hh * HD:(hh + 1) * HD]
                        last = nc.tensor.matmul(s_out[q0:q0 + 32, c0:c0 + HD], l_, r_, start=(b == 0 and k == 0 and hh < 4),
                                                stop=(done and hh == FOX - 1), tile_position=(0, q0), skip_group_check=True)
                    if k >= 0:
                        last.then_inc(s_vu, 1)
                    elif done:
                        last.then_inc(S["s"]["weighted"], 1)

                def turn_result(u):
                    pe.wait_ge(S["s"]["drained"], u + 1)
                    pe.wait_ge(s_tc, place_of[("o", u, 0)])
                    for k in range(4):
                        last = nc.tensor.transpose(tbank[:, k * P:(k + 1) * P], o_s[:, k * P:(k + 1) * P], ident[:])
                    last.then_inc(s_t, 1)

                for p in range(STEPS):
                    if 0 <= p - 2 < NP:
                        turn("p", p - 2, 0)
                    if p < NP:
                        make_logits(p)
                    if p in turn_at:
                        for g in range(t_groups("s", turn_at[p])):
                            turn("s", turn_at[p], g)
                    if p in out_at:
                        turn_result(out_at[p])
                    for item in k_at[p]:
                        keys_item(item)
                    for item in v_at[p]:
                        values_item(item)
                    if 0 <= p - 2 < NP:
                        weigh(p - 2)

        recycle()

        bt_hi = at("bt_hi", [P, KC, T], F32R, O_Z)
        bt_lo = at("bt_lo", [P, KC, T], F32R, O_Z + KC * T * 4)
        m_hi = at("m_hi", [P, KC, T], F32R, O_R1)
        m_lo = at("m_lo", [P, KC, T], F32R, O_R2)
        g_in = at("g_in", [P, 2, 3, T], F32, O_GB)
        tmp = at("merge_tmp", [P, T], F32, O_GB + 13824)
        merged = at("merged", [P, T], F32, O_Z + 2 * KC * T * 4)
        s_bh, s_bl = sem("branches_hi"), sem("branches_split")
        q3 = stream_sems("merge")
        s_gl = [sem(f"gates_loaded{k}") for k in range(2)]
        s_m0, s_m1, s_m2 = sem("pool_branch_taken"), sem("fox_branch_taken"), sem("mem_branch_taken")
        s_mch, s_mrd, s_mh, s_ml = sem("merge_chain"), sem("merged_ready"), sem("merged_hi"), sem("merged_lo")
        with nc.Block() as block:
            @block.sync
            def _(sp):
                load_stripes(sp, a["w_up"], KC, q3)

            @block.gpsimd
            def _(pool):
                for s in range(KC):
                    if s >= 2:
                        pool.wait_ge(s_m2, s)
                    pool.dma_start(g_in[:, s % 2, :, :], gates_dram[3 * s:3 * s + 3, :, :].rearrange("g p t -> p g t")).then_inc(s_gl[s % 2], 16)

            @block.scalar
            def _(act):
                def drain(i, s):
                    act.wait_ge(s_bl, 4)
                    act.wait_ge(s_mrd, 2 * i + s + 1)
                    nc.scalar.activation(m_hi[:, bass.ds(2 * i + s, 1), :], merged[:].rearrange("p (o t) -> p o t", o=1), ACT.Copy).then_inc(s_mh, 1)
                for g in range(4):
                    nc.scalar.activation(bt_hi[:, 4 * g:4 * g + 4, :], b_t[:, 4 * g:4 * g + 4, :], ACT.Copy).then_inc(s_bh, 1)
                lagged(act, KC, lambda i, s: split_hi(act, i, s, q3), drain)

            @block.vector
            def _(dve):
                def two(t_):
                    return t_.rearrange("p (b t) -> p b t", b=2)

                def drain(i, s):
                    n = 2 * i + s
                    par = s % 2
                    dve.wait_ge(q3["mm"], 4 * i + 2 * s + 4)
                    dve.wait_ge(s_gl[par], 16 * (i + s // 2 + 1))
                    dve.wait_ge(s_ml, n + 1)
                    nc.vector.tensor_tensor(two(merged[:]), acc[:, par, :, 0:HALF], two(g_in[:, par, 0, :]), ALU.mult).then_inc(s_m0, 1)
                    nc.vector.tensor_tensor(two(tmp[:]), tps[:, 0:2, 0:HALF], two(g_in[:, par, 1, :]), ALU.mult).then_inc(s_m1, 1)
                    dve.wait_ge(s_m1, n + 2)
                    nc.vector.tensor_tensor(merged[:], merged[:], tmp[:], ALU.add).then_inc(s_mch, 1)
                    dve.wait_ge(s_mch, n + 1)
                    nc.vector.tensor_tensor(two(tmp[:]), tps[:, 2:4, 0:HALF], two(g_in[:, par, 2, :]), ALU.mult).then_inc(s_m2, 1)
                    dve.wait_ge(s_m2, n + 2)
                    nc.vector.tensor_tensor(merged[:], merged[:], tmp[:], ALU.add).then_inc(s_mrd, 1)
                    dve.wait_ge(s_mh, n + 1)
                    nc.vector.tensor_tensor(m_lo[:, bass.ds(n, 1), :], merged[:].rearrange("p (o t) -> p o t", o=1),
                                            m_hi[:, bass.ds(n, 1), :].bitcast(F32), ALU.subtract).then_inc(s_ml, 1)
                for g in range(4):
                    dve.wait_ge(s_bh, g + 1)
                    nc.vector.tensor_tensor(bt_lo[:, 4 * g:4 * g + 4, :], b_t[:, 4 * g:4 * g + 4, :],
                                            bt_hi[:, 4 * g:4 * g + 4, :].bitcast(F32), ALU.subtract).then_inc(s_bl, 1)
                lagged(dve, KC, lambda i, s: split_lo(dve, i, s, q3), drain)

            @block.tensor
            def _(pe):
                pe.sem_inc(q3["mm"], 2)
                pe.sem_inc(s_m0, 2)
                pe.sem_inc(s_m1, 1)
                pe.sem_inc(s_m2, 1)
                pe.sem_inc(s_ml, 1)

                def one(i, s):
                    par = s % 2

                    def out(cc, b, cn):
                        if cc < 4:
                            return acc[:, par, b, 0:cn], 0, 3
                        if cc < 12:
                            return tps[:, b, 0:cn], 4, 11
                        return tps[:, 2 + b, 0:cn], 12, KC - 1

                    def before(cc):
                        if cc in (0, 4, 12):
                            pe.wait_ge({0: s_m0, 4: s_m1, 12: s_m2}[cc], 2 * i + s + 1)

                    for h in range(2):
                        pe.wait_ge(q3["lo"], 4 * i + 2 * s + h + 1)
                        multiply_half(pe, par, h, bt_hi, bt_lo, HALVES, q3, out=out, before=before)

                pe.wait_ge(s_bl, 4)
                with pe.Fori(0, KC // 2) as i:
                    one(i, 0)
                    one(i, 1)

        recycle()

        O_T = O_X1 + NBLK * D * 4
        x1 = at("x1", [P, NBLK, D], F32, O_X1)
        mo = at("mo", [P, 2, T], F32, O_T)
        q4 = stream_sems("out", more_slots("out", O_MKT, O_GB))
        s_xl, s_ot, s_oa = sem("x_reloaded"), sem("out_transposed"), sem("out_added")
        with nc.Block() as block:
            @block.sync
            def _(sp):
                load_stripes(sp, a["w_out"], KC, q4)

            @block.gpsimd
            def _(pool):
                pool.wait_ge(q4["loaded"][3], 16)
                pool.dma_start(x1[:, 0:4, :], a["x"][0:T_P, :].rearrange("(b p) d -> p b d", p=P)).then_inc(s_xl, 16)
                pool.dma_start(x1[0:T_S, 4, :], a["x"][T_P:T, :]).then_inc(s_xl, 16)

            @block.scalar
            def _(act):
                def drain(i, s):
                    act.wait_ge(q4["mm"], 4 * i + 2 * s + 6)
                    act.wait_ge(s_ot, 2 * i + s + 1)
                    nc.scalar.activation(mo[:, s % 2, :].rearrange("p (b t) -> p b t", b=2), acc[:, s % 2, :, 0:HALF], ACT.Copy).then_inc(q4["act"], 1)
                lagged(act, KC, lambda i, s: split_hi(act, i, s, q4), drain)

            @block.vector
            def _(dve):
                def drain(i, s):
                    n, par = 2 * i + s, s % 2
                    dve.wait_ge(s_xl, 32)
                    dve.wait_ge(s_ot, n + 3)
                    dst = x1[:, 0:4, bass.ds(n * P, P)]
                    nc.vector.tensor_tensor(dst, tps[:, 2 * par, :].rearrange("p (b t) -> p b t", b=4), dst, ALU.add)
                    dst = x1[0:T_S, 4, bass.ds(n * P, P)]
                    nc.vector.tensor_tensor(dst, tps[0:T_S, 2 * par + 1, 0:P], dst, ALU.add).then_inc(s_oa, 1)
                lagged(dve, KC, lambda i, s: split_lo(dve, i, s, q4), drain)

            @block.tensor
            def _(pe):
                def between(i, s):
                    n, par = 2 * i + s, s % 2
                    pe.wait_ge(q4["act"], n + 3)
                    pe.wait_ge(s_oa, n + 1)
                    for b in range(NBLK):
                        dst = tps[:, 2 * par, b * P:(b + 1) * P] if b < 4 else tps[0:T_S, 2 * par + 1, 0:P]
                        last = nc.tensor.transpose(dst, mo[:, par, b * P:b * P + ROWS[b]], ident[:])
                    last.then_inc(s_ot, 1)
                pe.sem_inc(s_ot, 2)
                pe.sem_inc(s_oa, 2)
                multiply_stripes(pe, KC, m_hi, m_lo, HALVES, q4, use=("act",), between=between)

        recycle()

        h_hi = at("h_hi", [P, KC, T], F32R, O_R1)
        h_lo = at("h_lo", [P, KC, T], F32R, O_R2)
        hn = at("hn", [P, 2, D], F32, O_T)
        norm_transposed("ffn", NBLK, ROWS, a["norm_ffn_g"], lambda b: x1[0:ROWS[b], b, :], None, h_hi, h_lo, (ss2, ms2, rstd2), hn)

        qp = at("qp", [P, 2 * PH, T], F32, O_T)
        q5 = stream_sems("peerq", q4["more"])
        act_q, dve_q = drain_to(qp, q5)
        with nc.Block() as block:
            @block.sync
            def _(sp):
                load_stripes(sp, a["w_pq"], 2 * PH, q5)

            @block.scalar
            def _(act):
                lagged(act, 2 * PH, lambda i, s: split_hi(act, i, s, q5), lambda i, s: act_q(act, i, s))

            @block.vector
            def _(dve):
                lagged(dve, 2 * PH, lambda i, s: split_lo(dve, i, s, q5), lambda i, s: dve_q(dve, i, s))

            @block.tensor
            def _(pe):
                multiply_stripes(pe, 2 * PH, h_hi, h_lo, HALVES, q5)

        recycle()

        place = [O_T + 2 * PH * T * 4]

        eidx = at("eidx", [P, NEXP, NBLK], I32, O_MKT)
        route = at("route", [P, NEXP, NBLK], I32, O_MKT + NBLK * NEXP * 4)
        gate = at("gate", [P, NEXP, NBLK], F32, O_MKT + 2 * NBLK * NEXP * 4)
        onehot = at("onehot", [P, NEXP, PTOP], F32, O_GB)
        sc = at("sc", [P, 2, 2 * PH, NKEY], F32, O_W)
        sc_b = at("sc_b", [P, 2 * PH, NKEY], F32, O_W + 16384)
        cand2 = at("cand", [P, 2, PH, PTOP * PTOP], F32, O_W)
        cand_b = at("cand_b", [P, PH, PTOP * PTOP], F32, O_W + 16384)
        sk = at("sk", [P, 2 * PH, NKEY], F32, O_W + 24576)
        part = at("part", [P, 2, NEXP], F32, O_W + 32768)
        zero = at("zero", [P, 512], F32, O_W + 32768 + 1024)
        top = then("top", [P, 2 * PH, PTOP], F32)
        tidx = then("tidx", [P, 2 * PH, PTOP], U32)
        tidx_f = then("tidx_f", [P, 2 * PH, PTOP], F32)
        best = then("best", [P, PH, PTOP], F32)
        sel = then("sel", [P, PH, PTOP], U32)
        sel_a = then("sel_a", [P, 2, NEXP], U32)
        sel_f = then("sel_f", [P, 2, NEXP], F32)
        iota = then("iota16", [P, PTOP], F32)
        tok = then("token", [P, 8], F32)
        ebest = then("ebest", [P, PH, PTOP], F32)
        esum = then("esum", [P, 2, PH], F32)
        assert place[0] <= O_R1
        s_skl, s_qk, s_qkc, s_dd, s_tk, s_ex = (sem(f"topk_{x}") for x in ("keys_loaded", "scores", "copied", "block_done", "chain", "exps"))
        s_tick = sem("topk_tick")
        s_z0, s_z1 = sem("zero_written"), sem("routes_cleared")
        LINKS = 22
        with nc.Block() as block:
            @block.sync
            def _(sp):
                sp.dma_start(sk[:], a["subkeys"]).then_inc(s_skl, 16)
                sp.dma_start(iota[:], a["iota16"]).then_inc(s_skl, 16)
                sp.dma_start(tok[:], a["token"]).then_inc(s_skl, 16)

            @block.gpsimd
            def _(pool):
                pool.dma_start(x1_dram.rearrange("(b p) d -> p b d", p=P), x1[:, 1:4, :]).then_inc(s_z1, 16)
                nc.gpsimd.memset(zero[:], 0.0).then_inc(s_z0, 1)
                nc.gpsimd.memset(route[:], 0).then_inc(s_z0, 1)
                nc.gpsimd.memset(gate[:], 0.0).then_inc(s_z0, 1)
                pool.wait_ge(s_z0, 1)
                cells = route_dram.rearrange("(q p j c) o -> q p j (c o)", q=8, p=P, c=512)
                for k in range(8):
                    pool.dma_start(cells[k], zero[:].unsqueeze(1).to_broadcast([P, N_EXPERTS * ND // (8 * P * 512), 512])).then_inc(s_z1, 16)
                pool.wait_ge(s_z1, 16 * 9)

            @block.tensor
            def _(pe):
                pe.wait_ge(s_skl, 48)
                for b in range(NBLK):
                    r = ROWS[b]
                    for g in range(4):
                        n = 4 * b + g
                        bank = acc[:, n % 4 // 2, n % 2, :]
                        if n >= 4:
                            pe.wait_ge(s_qkc, n - 3)
                        for k in range(4):
                            last = nc.tensor.matmul(bank[0:r, k * P:(k + 1) * P], qp[:, 4 * g + k, b * P:b * P + r], sk[:, 4 * g + k, :],
                                                    start=True, stop=True)
                        last.then_inc(s_qk, 1)

            @block.scalar
            def _(act):
                for b in range(NBLK + 1):
                    if b < NBLK:
                        if b >= 2:
                            act.wait_ge(s_dd, b - 1)
                        for g in range(4):
                            n = 4 * b + g
                            r = ROWS[b]
                            act.wait_ge(s_qk, n + 1)
                            nc.scalar.activation(sc[0:r, b % 2, 4 * g:4 * g + 4, :],
                                                 acc[0:r, n % 4 // 2, n % 2, :].rearrange("p (k c) -> p k c", k=4), ACT.Copy).then_inc(s_qkc, 1)
                    if b >= 1:
                        r = ROWS[b - 1]
                        act.wait_ge(s_tk, LINKS * (b - 1) + 10)
                        nc.scalar.activation(ebest[0:r], ebest[0:r], ACT.Exp).then_inc(s_ex, 1)

            @block.vector
            def _(dve):
                def topk(b, par, r):
                    count = [0]

                    def link(ins):
                        count[0] += 1
                        ins.then_inc(s_tk, 1)
                        dve.wait_ge(s_tk, LINKS * b + count[0])
                        dve.sem_inc(s_tick, 1)

                    dve.wait_ge(s_qkc, 4 * b + 4)
                    dve.sem_inc(s_tick, 1)
                    cand = cand2[:, par]
                    for src, src_b, vals, idx, m in ((sc[0:r, par], sc_b[0:r], top[0:r], tidx[0:r], 2 * PH), (cand[0:r], cand_b[0:r], best[0:r], sel[0:r], PH)):
                        if m == PH:
                            tv = top[0:r].rearrange("p (h two) k -> p h two k", two=2)
                            link(nc.vector.tensor_tensor(
                                cand[0:r].rearrange("p h (x y) -> p h x y", x=PTOP),
                                tv[:, :, 0, :].unsqueeze(3).to_broadcast([r, PH, PTOP, PTOP]),
                                tv[:, :, 1, :].unsqueeze(2).to_broadcast([r, PH, PTOP, PTOP]), ALU.add))
                        for h in range(m):
                            last = nc.vector.max(out=vals[:, h, 0:8], in_=src[:, h, :])
                        link(last)
                        for h in range(m):
                            nc.vector.max_index(out=idx[:, h, 0:8], in_max=vals[:, h, 0:8], in_values=src[:, h, :])
                            last = nc.vector.match_replace(out=src_b[:, h, :], in_to_replace=vals[:, h, 0:8], in_values=src[:, h, :], imm_value=-3.0e38)
                        link(last)
                        for h in range(m):
                            last = nc.vector.max(out=vals[:, h, 8:16], in_=src_b[:, h, :])
                        link(last)
                        for h in range(m):
                            last = nc.vector.max_index(out=idx[:, h, 8:16], in_max=vals[:, h, 8:16], in_values=src_b[:, h, :])
                        link(last)
                    link(nc.vector.tensor_tensor(ebest[0:r], best[0:r], best[0:r, :, 0:1].to_broadcast([r, PH, PTOP]), ALU.subtract))
                    sf = sel[0:r].rearrange("p h k -> p (h k)")
                    nc.vector.tensor_scalar(sel_a[0:r, 0], sf, 4, None, ALU.logical_shift_right)
                    link(nc.vector.tensor_scalar(sel_a[0:r, 1], sf, PTOP - 1, None, ALU.bitwise_and))
                    nc.vector.tensor_copy(tidx_f[0:r], tidx[0:r])
                    link(nc.vector.tensor_copy(sel_f[0:r], sel_a[0:r]))
                    for side in range(2):
                        link(nc.vector.tensor_tensor(onehot[0:r], sel_f[0:r, side, :].unsqueeze(2).to_broadcast([r, NEXP, PTOP]),
                                                     iota[0:r].unsqueeze(1).to_broadcast([r, NEXP, PTOP]), ALU.is_equal))
                        oh4 = onehot[0:r].rearrange("p (h k) x -> p h k x", h=PH)
                        lists = tidx_f[0:r].rearrange("p (h two) k -> p h two k", two=2)[:, :, side, :]
                        link(nc.vector.tensor_tensor(oh4, oh4, lists.unsqueeze(2).to_broadcast([r, PH, PTOP, PTOP]), ALU.mult))
                        link(nc.vector.reduce_sum(part[0:r, side, :], onehot[0:r], AX.X))
                    link(nc.vector.scalar_tensor_tensor(out=eidx[0:r, :, bass.ds(b, 1)], in0=part[0:r, 0, :].unsqueeze(2), scalar=float(NKEY),
                                                        in1=part[0:r, 1, :].unsqueeze(2), op0=ALU.mult, op1=ALU.add))
                    nc.vector.tensor_scalar(route[0:r, :, bass.ds(b, 1)], eidx[0:r, :, bass.ds(b, 1)], float(ND), tok[0:r, bass.ds(b, 1)],
                                            ALU.mult, ALU.add)
                    dve.wait_ge(s_ex, b + 1)
                    link(nc.vector.reduce_sum(esum[0:r, 0, :], ebest[0:r], AX.X))
                    link(nc.vector.reciprocal(esum[0:r, 1, :], esum[0:r, 0, :]))
                    link(nc.vector.tensor_tensor(gate[0:r, :, bass.ds(b, 1)].rearrange("p (h k) o -> p h (k o)", h=PH), ebest[0:r],
                                                 esum[0:r, 1, :].unsqueeze(2).to_broadcast([r, PH, PTOP]), ALU.mult))
                    assert count[0] == LINKS
                    dve.sem_inc(s_dd, 1)

                dve.wait_ge(s_skl, 48)
                dve.wait_ge(s_z0, 3)
                with dve.Fori(0, 2) as i:
                    topk(2 * i, 0, P)
                    topk(2 * i + 1, 1, P)
                topk(4, 0, T_S)

        recycle()

        HC = NEXP // 2
        ring = at("ring", [P, 3, D], F32, O_T)
        hrow = at("h_row", [P, D], F32, O_T + 24576)
        hrow_s = g_row
        a_out = at("a_out", [P, 2, ND], F32, O_T + 32768)
        dots = at("dots", [P, NEXP + HC], F32, O_T + 32768 + 8 * ND)
        tail = at("sample_second_choices", [T_S, 2, HC], F32, O_T + 34048 + 8 * ND)
        O_WTS = O_R1 - 2048
        wts = at("weights", [P, NEXP + HC], F32, O_WTS)
        eidx_s = at("expert_sample", [P, HC], I32, O_WTS + 768)
        gate_s = at("gate_sample", [P, HC], F32, O_WTS + 1024)
        stage_e = at("expert_stage", [P, 3, 8], I32, O_WTS + 1280)
        stage_r = at("route_stage", [P, 2, 8], I32, O_WTS + 1376)
        stage_g = at("gate_stage", [P, 2, 8], F32, O_WTS + 1440)
        tail_i = at("sample_second_experts", [T_S, HC], I32, O_T + 34048 + 8 * ND + 512)
        assert O_T + 34048 + 8 * ND + 768 <= O_WTS
        q6 = stream_sems("peeru", more_slots("peeru", O_X1 + D * 4, O_X1 + 2 * D * 4))
        s_gl2, s_hr = sem("ffn_g_reloaded"), sem("h_row_ready")
        s_st = [sem(f"activations_stored{k}") for k in range(2)]
        s_gat = [sem(f"u_row_gathered{k}") for k in range(3)]
        s_prep, s_moved, s_hrs, s_hmv, s_used_s = (sem(x) for x in (
            "sample_tables_copied", "sample_tables_moved", "sample_rows_ready", "sample_rows_moved", "u_sample_row_used"))
        s_used, s_stg, s_sct, s_ptick = sem("u_row_used"), sem("indices_staged"), sem("gates_scattered"), sem("route_tick")
        s_dots, s_gel = sem("dots_done"), sem("gelu_done")
        with nc.Block() as block:
            @block.sync
            def _(sp):
                sp.dma_start(g_row[:], a["norm_ffn_g"].rearrange("(o d) -> o d", o=1).to_broadcast([P, D])).then_inc(s_gl2, 16)
                load_stripes(sp, a["w_peer_u"], NTILE, q6)

            @block.gpsimd
            def _(pool):
                pool.sem_inc(s_used, 2)
                pool.sem_inc(s_used_s, 1)
                nc.gpsimd.tensor_copy(eidx_s[0:T_S], eidx[0:T_S, 0:HC, 4]).then_inc(s_prep, 1)
                nc.gpsimd.tensor_copy(gate_s[0:T_S], gate[0:T_S, 0:HC, 4]).then_inc(s_prep, 1)
                nc.gpsimd.tensor_copy(tail_i[:], eidx[0:T_S, HC:, 4]).then_inc(s_prep, 1)
                nc.gpsimd.tensor_copy(tail[:, 0], gate[0:T_S, HC:, 4]).then_inc(s_prep, 1)
                nc.gpsimd.memset(x1[T_S:P, 4, :], 0.0).then_inc(s_prep, 1)
                pool.wait_ge(s_prep, 5)
                pool.dma_start(eidx_s[T_S:P], tail_i[:]).then_inc(s_moved, 16)
                pool.dma_start(gate_s[T_S:P], tail[:, 0]).then_inc(s_moved, 16)
                pool.wait_ge(s_hrs, 1)
                pool.dma_start(hrow_s[T_S:P], hrow_s[0:T_S]).then_inc(s_hmv, 16)
                pool.wait_ge(s_moved, 32)
                with pool.Fori(0, NEXP // 2) as i:
                    for s in range(2):
                        n = 2 * i + s
                        pool.wait_ge(s_sct, 48 * n)
                        pool.wait_ge(s_used, n + 1)
                        nc.gpsimd.tensor_copy(stage_e[:, s, 0:1], eidx[:, bass.ds(n, 1), 0]).then_inc(s_stg, 1)
                        nc.gpsimd.tensor_copy(stage_r[:, s, 0:NBLK], route[:, bass.ds(n, 1), :].rearrange("p o b -> p (o b)")).then_inc(s_stg, 1)
                        nc.gpsimd.tensor_copy(stage_g[:, s, 0:NBLK], gate[:, bass.ds(n, 1), :].rearrange("p o b -> p (o b)")).then_inc(s_stg, 1)
                        pool.wait_ge(s_stg, 7 * i + 3 * s + 3)
                        pool.sem_inc(s_ptick, 1)
                        for b in range(1, 4):
                            r = ROWS[b]
                            pool.indirect_dma_start(route_dram, bass.IndirectOffsetOnAxis(ap=stage_r[0:r, s, b:b + 1], axis=0),
                                                    stage_g[0:r, s, b:b + 1], None, compute_op=ALU.add).then_inc(s_sct, 16)
                        pool.indirect_dma_start(ring[:, s, :], None, a["peer_u"],
                                                bass.IndirectOffsetOnAxis(ap=stage_e[:, s, 0:1], axis=0)).then_inc(s_gat[s], 16)
                    pool.wait_ge(s_used_s, i + 1)
                    nc.gpsimd.tensor_copy(stage_e[:, 2, 0:1], eidx_s[:, bass.ds(i, 1)]).then_inc(s_stg, 1)
                    pool.wait_ge(s_stg, 7 * i + 7)
                    pool.sem_inc(s_ptick, 1)
                    pool.indirect_dma_start(ring[:, 2, :], None, a["peer_u"],
                                            bass.IndirectOffsetOnAxis(ap=stage_e[:, 2, 0:1], axis=0)).then_inc(s_gat[2], 16)
                pool.wait_ge(s_sct, 48 * NEXP)

            def drain_u(act, i, s):
                act.wait_ge(q6["mm"], 4 * i + 2 * s + 6)
                act.wait_ge(s_st[s], 16 * i)
                nc.scalar.activation(a_out[:, s, :], acc[:, s, 0, 0:ND], ACT.Gelu).then_inc(q6["act"], 1)
                act.wait_ge(q6["act"], 2 * i + s + 3)
                act.dma_start(acts_dram[bass.ds(2 * i + s, 1), :, :].rearrange("o p t -> p (o t)"), a_out[:, s, :]).then_inc(s_st[s], 16)

            @block.scalar
            def _(act):
                lagged(act, NTILE, lambda i, s: split_hi(act, i, s, q6), lambda i, s: drain_u(act, i, s))
                act.wait_ge(s_dots, NEXP)
                nc.scalar.activation(dots[:], dots[:], ACT.Gelu).then_inc(s_gel, 1)
                for s in range(2):
                    act.wait_ge(s_st[s], 16 * NTILE // 2)

            @block.vector
            def _(dve):
                def dot(i, s):
                    dve.wait_ge(s_gat[s], 16 * i + 16)
                    nc.vector.scalar_tensor_tensor(out=ring[:, s, :], in0=ring[:, s, :], scalar=1.0, in1=hrow[:], op0=ALU.mult,
                                                   op1=ALU.mult, accum_out=dots[:, bass.ds(2 * i + s, 1)]).then_inc(s_used, 1)
                    if s == 1:
                        dve.wait_ge(s_gat[2], 16 * i + 16)
                        nc.vector.scalar_tensor_tensor(out=ring[:, 2, :], in0=ring[:, 2, :], scalar=1.0, in1=hrow_s[:], op0=ALU.mult,
                                                       op1=ALU.mult, accum_out=dots[:, bass.ds(i + NEXP, 1)]).then_inc(s_used_s, 1)

                dve.wait_ge(s_gl2, 16)
                nc.vector.scalar_tensor_tensor(out=hrow[:], in0=x1[:, 0, :], scalar=rstd2[:, 0:1], in1=g_row[:],
                                               op0=ALU.mult, op1=ALU.mult).then_inc(s_hr, 1)
                dve.wait_ge(s_hr, 1)
                nc.vector.scalar_tensor_tensor(out=hrow_s[0:T_S], in0=x1[0:T_S, 4, :], scalar=rstd2[0:T_S, 4:5], in1=g_row[0:T_S],
                                               op0=ALU.mult, op1=ALU.mult).then_inc(s_hrs, 1)
                dve.wait_ge(s_hmv, 16)
                lagged(dve, NTILE, lambda i, s: split_lo(dve, i, s, q6), dot)
                dve.wait_ge(s_used, 2 + NEXP)
                dve.wait_ge(s_used_s, 1 + HC)
                dve.sem_inc(s_dots, NEXP)
                dve.wait_ge(s_gel, 1)
                nc.vector.tensor_tensor(wts[:, 0:NEXP], dots[:, 0:NEXP], gate[:, :, 0], ALU.mult)
                nc.vector.tensor_tensor(wts[:, NEXP:], dots[:, NEXP:], gate_s[:], ALU.mult)

            @block.tensor
            def _(pe):
                multiply_stripes(pe, NTILE, h_hi, h_lo, [(P, ND)], q6, use=("act",))

        recycle()

        NG = NTILE // GRP
        t_hi = at("tile_hi", [P, 2 * GRP, ND], F32R, O_R1)
        t_lo = at("tile_lo", [P, 2 * GRP, ND], F32R, O_R1 + 2 * GRP * ND * 4)
        ring_v = at("ring_v", [P, 3, D], F32, O_R1 + 4 * GRP * ND * 4)
        out_t = at("out_t", [P, KC, ND], F32, O_T)
        O_AG = O_T + KC * ND * 4
        ag = at("act_and_gate", [P, 2, 2, ND], F32, O_AG)
        hf = at("tile_full", [P, 2, ND], F32, O_AG + 4 * ND * 4)
        assert O_AG + 6 * ND * 4 <= O_WTS
        q7 = stream_sems("peerv", q6["more"])
        s_ag = [sem(f"act_and_gate_loaded{k}") for k in range(2)]
        s_hm, s_hh, s_hl = sem("tile_product"), sem("tile_hi_ready"), sem("tile_lo_ready")
        s_first, s_clr = sem("first_tiles_loaded"), sem("out_cleared")
        s_gat = [sem(f"v_row_gathered{k}") for k in range(3)]
        s_used_s = sem("v_sample_row_used")
        s_used, s_stg, s_ptick = sem("v_row_used"), sem("v_index_staged"), sem("v_tick")
        with nc.Block() as block:
            @block.sync
            def _(sp):
                w = a["w_peer_v"]

                def load_tile(tile, par):
                    sp.dma_start(ag[:, par, 0, :], acts_dram[bass.ds(tile, 1), :, :].rearrange("o p t -> p (o t)")).then_inc(s_ag[par], 16)
                    sp.dma_start(ag[:, par, 1, :], route_dram.rearrange("(n t) o -> n (t o)", t=ND)[bass.ds(tile * P, P), :]).then_inc(s_ag[par], 16)

                sp.dma_start(out_t[:, 0:GRP, :], acts_dram[0:GRP].rearrange("n p t -> p n t")).then_inc(s_first, 16)
                sp.dma_start(out_t[:, GRP:, :], route_dram.rearrange("(n p t) o -> n p (t o)", p=P, t=ND)[0:GRP]
                             .rearrange("n p t -> p n t")).then_inc(s_first, 16)
                for j in range(4):
                    sp.dma_start(raw[:, j, :], w[j * P:(j + 1) * P, :]).then_inc(q7["loaded"][j], 16)

                def tile_of(i, k):
                    sp.wait_ge(s_hm, 2 * i + k + GRP - 1)
                    load_tile(2 * i + k + GRP, k)

                def halves(i, k):
                    sp.wait_ge(q7["lo"], 4 * i + k - 3)
                    sp.dma_start(raw[:, k, :], w[bass.ds((4 * i + k) * P, P), :]).then_inc(q7["loaded"][k], 16)

                tile_of(0, 0)
                tile_of(0, 1)
                with sp.Fori(1, (NTILE - GRP) // 2) as i:
                    for k in range(4):
                        halves(i, k)
                        if k % 2:
                            tile_of(i, k // 2)
                with sp.Fori((NTILE - GRP) // 2, NTILE // 2) as i:
                    for k in range(4):
                        halves(i, k)

            @block.gpsimd
            def _(pool):
                pool.sem_inc(s_used, 2)
                pool.sem_inc(s_used_s, 1)
                pool.sem_inc(s_hl, 2)

                def product(tile, par, loads):
                    pool.wait_ge(s_ag[par], 32 * loads)
                    pool.wait_ge(s_hl, tile + 1)
                    nc.gpsimd.tensor_tensor(hf[:, par, :], ag[:, par, 0, :], ag[:, par, 1, :], ALU.mult).then_inc(s_hm, 1)

                pool.wait_ge(s_first, 32)
                for t_ in range(GRP):
                    pool.wait_ge(s_hl, t_ + 1)
                    nc.gpsimd.tensor_tensor(hf[:, t_ % 2, :], out_t[:, t_, :], out_t[:, GRP + t_, :], ALU.mult).then_inc(s_hm, 1)
                pool.wait_ge(s_hm, GRP)
                for k in range(4):
                    nc.gpsimd.memset(out_t[:, 4 * k:4 * k + 4, :], 0.0).then_inc(s_clr, 1)

                def rows(i, build):
                    for s in range(2):
                        n = 2 * i + s
                        if build:
                            product(2 * i + s + GRP, s, i + 1)
                        pool.wait_ge(s_used, n + 1)
                        nc.gpsimd.tensor_copy(stage_e[:, s, 0:1], eidx[:, bass.ds(n, 1), 0]).then_inc(s_stg, 1)
                        pool.wait_ge(s_stg, 3 * i + s + 1)
                        pool.sem_inc(s_ptick, 1)
                        pool.indirect_dma_start(ring_v[:, s, :], None, a["peer_v"],
                                                bass.IndirectOffsetOnAxis(ap=stage_e[:, s, 0:1], axis=0)).then_inc(s_gat[s], 16)
                    pool.wait_ge(s_used_s, i + 1)
                    nc.gpsimd.tensor_copy(stage_e[:, 2, 0:1], eidx_s[:, bass.ds(i, 1)]).then_inc(s_stg, 1)
                    pool.wait_ge(s_stg, 3 * i + 3)
                    pool.sem_inc(s_ptick, 1)
                    pool.indirect_dma_start(ring_v[:, 2, :], None, a["peer_v"],
                                            bass.IndirectOffsetOnAxis(ap=stage_e[:, 2, 0:1], axis=0)).then_inc(s_gat[2], 16)

                with pool.Fori(0, (NTILE - GRP) // 2) as i:
                    rows(i, True)
                with pool.Fori((NTILE - GRP) // 2, NEXP // 2) as i:
                    rows(i, False)

            def sweep(eng, before, split, after):
                def body(first, par, j, build=True, ahead=True):
                    i = first + j
                    for s in range(2):
                        before(i, s, par, j, build, first)
                        if s == 0 or ahead:
                            split(i, s + 1)
                        after(i, s, par, j, build)

                split(0, 0)
                with eng.Fori(0, NG // 2 - 1) as gg:
                    for par in range(2):
                        with eng.Fori(0, GRP // 2) as j:
                            body(GRP * gg + GRP // 2 * par, par, j)
                last = GRP * (NG // 2 - 1)
                with eng.Fori(0, GRP // 2) as j:
                    body(last, 0, j)
                with eng.Fori(0, GRP // 2 - 1) as j:
                    body(last + GRP // 2, 1, j, build=False)
                body(last + GRP // 2, 1, GRP // 2 - 1, build=False, ahead=False)

            def slot_of(s, par, j):
                return bass.ds(GRP * (1 - par) + 2 * j + s, 1)

            def round_tile(act, tile, par, dst):
                act.wait_ge(s_hm, tile + 1)
                nc.scalar.activation(dst, hf[:, par:par + 1, :], ACT.Copy).then_inc(s_hh, 1)

            @block.scalar
            def _(act):
                for t_ in range(GRP):
                    round_tile(act, t_, t_ % 2, t_hi[:, t_:t_ + 1, :])

                def before(i, s, par, j, build, first):
                    if build:
                        act.wait_ge(q7["mm"], 4 * first + 4)
                        round_tile(act, 2 * i + s + GRP, s, t_hi[:, slot_of(s, par, j), :])
                sweep(act, before, lambda i, s: split_hi(act, i, s, q7), lambda *_: None)

            @block.vector
            def _(dve):
                def rest(tile, par, dst, hi):
                    dve.wait_ge(s_hh, tile + 1)
                    nc.vector.tensor_tensor(dst, hf[:, par:par + 1, :], hi.bitcast(F32), ALU.subtract).then_inc(s_hl, 1)

                for t_ in range(GRP):
                    rest(t_, t_ % 2, t_lo[:, t_:t_ + 1, :], t_hi[:, t_:t_ + 1, :])
                dve.wait_ge(s_clr, 4)

                def after(i, s, par, j, build):
                    if build:
                        sl = slot_of(s, par, j)
                        rest(2 * i + s + GRP, s, t_lo[:, sl, :], t_hi[:, sl, :])
                    dve.wait_ge(s_gat[s], 16 * i + 16)
                    dve.wait_ge(s_used, 2 * i + s + 2)
                    w = wts[:, bass.ds(2 * i + s, 1)] if not isinstance(i, int) else wts[:, 2 * i + s:2 * i + s + 1]
                    nc.vector.scalar_tensor_tensor(out=x1[:, 0, :], in0=ring_v[:, s, :], scalar=w, in1=x1[:, 0, :],
                                                   op0=ALU.mult, op1=ALU.add).then_inc(s_used, 1)
                    if s == 1:
                        dve.wait_ge(s_gat[2], 16 * i + 16)
                        dve.wait_ge(s_used_s, i + 1)
                        w = wts[:, bass.ds(i + NEXP, 1)] if not isinstance(i, int) else wts[:, i + NEXP:i + NEXP + 1]
                        nc.vector.scalar_tensor_tensor(out=x1[:, 4, :], in0=ring_v[:, 2, :], scalar=w, in1=x1[:, 4, :],
                                                       op0=ALU.mult, op1=ALU.add).then_inc(s_used_s, 1)
                    for h in range(2):
                        dve.wait_ge(q7["mm"], 4 * i + 2 * s + h + 5)
                        dst = out_t[:, bass.ds(4 * j + 2 * s + h, 1), :] if not isinstance(j, int) else out_t[:, 4 * j + 2 * s + h:4 * j + 2 * s + h + 1, :]
                        nc.vector.tensor_tensor(dst, acc[:, s, h:h + 1, 0:ND], dst, ALU.add).then_inc(q7["dve"], 1)

                sweep(dve, lambda *_: None, lambda i, s: split_lo(dve, i, s, q7), after)

            @block.tensor
            def _(pe):
                pe.sem_inc(q7["mm"], 4)
                pe.sem_inc(q7["dve"], 4)

                with pe.Fori(0, NG // 2) as gg:
                    for par in range(2):
                        with pe.Fori(0, GRP // 2) as j:
                            for s, h in ((0, 0), (0, 1), (1, 0), (1, 1)):
                                n = 2 * KC * gg + KC * par + 4 * j + 2 * s + h
                                pe.wait_ge(q7["lo"], n + 1)
                                pe.wait_ge(q7["dve"], n + 1)
                                pe.wait_ge(s_hl, 2 * GRP * gg + GRP * par + GRP + 1)
                                for c in range(GRP):
                                    if c == GRP - 1:
                                        pe.wait_ge(s_hl, 2 * GRP * gg + GRP * par + GRP + 2)
                                    wh, wl = (w[:, c * P:(c + 1) * P] for w in slot(q7, 2 * s + h))
                                    t_ = GRP * par + c
                                    for p_, (l_, r_) in enumerate(((wh, t_hi), (wh, t_lo), (wl, t_hi))):
                                        last = nc.tensor.matmul(acc[:, s, h, 0:ND], l_, r_[:, t_, :], start=(c == 0 and p_ == 0),
                                                                stop=(c == GRP - 1 and p_ == 2))
                                last.then_inc(q7["mm"], 1)

        recycle()

        g_fin = at("g_final", [P, D], F32, O_W)
        y = at("y", [P, 2, D], F32, O_R1)
        sq = at("squares", [P, D], F32, O_R1 + 16384)
        second = at("sample_second_sum", [T_S, D], F32, O_R1 + 24576)
        fin = at("fin", [P, 3, 8], F32, O_WTS)
        s_gf, s_ft, s_fadd, s_fsq, s_fms, s_frt, s_frs, s_fy = (sem(f"final_{x}") for x in (
            "g_loaded", "transposed", "added", "squared", "mean", "root", "rstd", "normed"))
        s_fold, s_back = sem("sample_second_moved"), sem("x1_reloaded")
        ORDER = (0, 4, 1, 2, 3)
        s_ys = [sem(f"y_stored{k}") for k in range(2)]
        with nc.Block() as block:
            @block.sync
            def _(sp):
                sp.dma_start(g_fin[:], a["norm_final_g"].rearrange("(o d) -> o d", o=1).to_broadcast([P, D])).then_inc(s_gf, 16)
                sp.dma_start(second[:], x1[T_S:P, 4, :]).then_inc(s_fold, 16)
                sp.dma_start(x1[:, 1:4, :], x1_dram.rearrange("(b p) d -> p b d", p=P)).then_inc(s_back, 16)
                for n, b in enumerate(ORDER):
                    r = ROWS[b]
                    sp.wait_ge(s_fy, n + 1)
                    sp.dma_start(a["y"][b * P:b * P + r, :], y[0:r, n % 2, :]).then_inc(s_ys[n % 2], 16)
                sp.wait_ge(s_ys[0], 48)
                sp.wait_ge(s_ys[1], 32)

            @block.tensor
            def _(pe):
                for b in range(1, 4):
                    for g in range(4):
                        n = 4 * (b - 1) + g
                        if n >= 4:
                            pe.wait_ge(s_fadd, 4 + n - 3)
                        for c in range(4):
                            last = nc.tensor.transpose(tps[0:ROWS[b], g, c * P:(c + 1) * P],
                                                       out_t[:, 4 * g + c, (b - 1) * P:(b - 1) * P + ROWS[b]], ident[:])
                        last.then_inc(s_ft, 1)

            @block.scalar
            def _(act):
                for n, b in enumerate(ORDER):
                    r = ROWS[b]
                    if n:
                        act.wait_ge(s_fadd, 4 * n)
                        act.wait_ge(s_fsq, n)
                    nc.scalar.activation(sq[0:r], x1[0:r, b, :], ACT.Square, accum_out=fin[0:r, 0, b:b + 1]).then_inc(s_fsq, 1)
                    act.wait_ge(s_fms, n + 1)
                    nc.scalar.activation(fin[0:r, 1, b:b + 1], fin[0:r, 1, b:b + 1], ACT.Sqrt).then_inc(s_frt, 1)

            @block.vector
            def _(dve):
                def add(n):
                    b = ORDER[n]
                    r = ROWS[b]
                    dve.wait_ge(s_fold, 16) if b == 4 else dve.wait_ge(s_back, 16)
                    for g in range(4):
                        dst = x1[0:r, b, g * 512:(g + 1) * 512]
                        if b == 4:
                            src = second[:, g * 512:(g + 1) * 512]
                        else:
                            dve.wait_ge(s_ft, 4 * (b - 1) + g + 1)
                            src = tps[0:r, g, :]
                        nc.vector.tensor_tensor(dst, src, dst, ALU.add).then_inc(s_fadd, 1)

                def mean(n):
                    b = ORDER[n]
                    r = ROWS[b]
                    dve.wait_ge(s_fsq, n + 1)
                    nc.vector.tensor_scalar(fin[0:r, 1, b:b + 1], fin[0:r, 0, b:b + 1], 1.0 / D, EPS, ALU.mult, ALU.add).then_inc(s_fms, 1)

                def norm(n):
                    b = ORDER[n]
                    r = ROWS[b]
                    dve.wait_ge(s_frt, n + 1)
                    nc.vector.reciprocal(fin[0:r, 2, b:b + 1], fin[0:r, 1, b:b + 1]).then_inc(s_frs, 1)
                    dve.wait_ge(s_frs, n + 1)
                    if n >= 2:
                        dve.wait_ge(s_ys[n % 2], 16 * (n // 2))
                    nc.vector.scalar_tensor_tensor(out=y[0:r, n % 2, :], in0=x1[0:r, b, :], scalar=fin[0:r, 2, b:b + 1], in1=g_fin[0:r],
                                                   op0=ALU.mult, op1=ALU.mult).then_inc(s_fy, 1)

                dve.wait_ge(s_gf, 16)
                mean(0)
                for n in range(NBLK):
                    if n + 1 < NBLK:
                        add(n + 1)
                    norm(n)
                    if n + 1 < NBLK:
                        mean(n + 1)


_OUTS = {
    "y": (T, D), "z_out": (P, F0 - K0, T), "mem_out": (P, 2 * MEM, N_MEM), "logf_out": (FOX, T), "state_out": (P, 4, DB, STATE),
}


def _half_stripes(w):
    n = w.shape[1] // P
    return np.ascontiguousarray(w.reshape(2, 8, P, n, P).transpose(3, 0, 2, 1, 4)).reshape(n * 2 * P, 1024)


def _expert_stripes(v):
    return np.ascontiguousarray(v.reshape(NTILE // GRP, GRP, P, KC, P).transpose(0, 3, 2, 1, 4)).reshape(NTILE // GRP * KC * P, GRP * P)


def _constants():
    ident = np.eye(P, dtype=np.float32)
    negsel_p = np.zeros((FOX, FOX, P), np.float32)
    negsel_s = np.zeros((DB, FOX, DB, FOX, DT), np.float32)
    for h in range(FOX):
        negsel_p[h, h, :] = -1.0 / SCALE
        for b in range(DB):
            negsel_s[b, h, b, h, :] = -1.0 / SCALE
    smask = np.full((FOX, DT, DB, DB, DT), NEG, np.float32)
    for b in range(DB):
        for t in range(DT):
            smask[:, t, b, b, 0:t + 1] = 0.0
    causal = np.where(np.arange(P)[None, :] <= np.arange(P)[:, None], 0.0, NEG).astype(np.float32)
    cnt = np.array([[1.0 / min(t + 1, w) for t in range(16)] for w in WINDOWS], np.float32)
    return {
        "ident": ident, "negsel_p": negsel_p, "negsel_s": negsel_s.reshape(DB * FOX, DB, FOX * DT),
        "smask": smask.reshape(FOX * DT, DB, T_S), "causal": causal,
        "cnt_inv": np.ascontiguousarray(np.broadcast_to(cnt, (P, 4, 16))),
        "token": np.ascontiguousarray((np.arange(P)[:, None] + (np.arange(8)[None, :] - 1) * P).astype(np.float32)),
        "head_row": np.ascontiguousarray(np.broadcast_to((np.arange(DB * FOX) % FOX).astype(np.float32)[:, None], (DB * FOX, 8))),
        "iota16": np.ascontiguousarray(np.broadcast_to(np.arange(PTOP, dtype=np.float32), (P, PTOP))),
    }


def kernel(**inputs):
    import concourse.bacc as bacc
    from concourse.bass_utils import run_bass_kernel_spmd

    g = {k: np.asarray(v) for k, v in inputs.items()}
    w_in = g["w_in"][0]
    pw, fw, mw = 512, 1024, 512
    cols = {}
    o = 0
    for name, n in (("u", pw), ("q", fw), ("k", fw), ("v", fw), ("f", FOX), ("qm", mw), ("g", 3 * D)):
        cols[name] = w_in[:, o:o + n]
        o += n
    w_z = np.concatenate([cols["q"], cols["qm"], cols["k"], cols["v"], cols["u"], cols["f"], np.zeros((D, P - FOX), np.float32)], axis=1)
    w_gate = cols["g"].reshape(D, 3, KC, P).transpose(0, 2, 1, 3).reshape(D, 3 * D)
    arrays = {
        "x": np.concatenate([g["x_prompt"].reshape(T_P, D), g["x_sample"].reshape(T_S, D)]),
        "mem_prompt": g["mem_prompt"].reshape(N_MEM, D),
        "w_z": _half_stripes(w_z), "w_gate": _half_stripes(w_gate),
        "w_mem": _half_stripes(np.concatenate([g["w_mem_k"][0], g["w_mem_v"][0]], axis=1)),
        "w_up": _half_stripes(np.concatenate([g["w_up_pool"][0], g["w_up_fox"][0], g["w_up_mem"][0]], axis=0)),
        "w_out": _half_stripes(g["w_out"][0]), "w_pq": _half_stripes(g["w_peer_q"][0]),
        "cache_k": np.ascontiguousarray(g["cache_k"][0].transpose(0, 3, 2, 1)).reshape(N_PHYS * HD, FOX * PAGE),
        "cache_v": g["cache_v"][0].reshape(N_PHYS * PAGE, FOX * HD),
        "cache_logf": np.ascontiguousarray(g["cache_logf"][0].transpose(0, 2, 1)).reshape(N_PHYS * FOX, PAGE),
        "mem_cache_k": np.ascontiguousarray(g["cache_mem_k"][0].transpose(0, 3, 2, 1)).reshape(DB * HD, MEM * N_MEM),
        "mem_cache_v": np.ascontiguousarray(g["cache_mem_v"][0].reshape(DB, 2, P, MEM * HD).transpose(0, 2, 1, 3)).reshape(DB * P, 2 * MEM * HD),
        "state_pool": np.ascontiguousarray(g["state_pool"][0].reshape(DB, STATE, 4, P).transpose(3, 2, 0, 1)),
        "page_table": g["page_table"].reshape(1, DB * PAGES),
        "pool_w": np.ascontiguousarray(g["pool_w"][0].transpose(1, 0, 2)),
        "pool_scale": np.ascontiguousarray(g["pool_scale"][0].reshape(4, P).T),
        "b_f": g["b_f"].reshape(FOX, 1),
        "subkeys": np.ascontiguousarray(g["peer_subkeys"][0].transpose(3, 0, 1, 2)).reshape(P, 2 * PH, NKEY),
        "peer_u": g["peer_u"][0], "peer_v": g["peer_v"][0],
        "w_peer_u": _half_stripes(g["peer_u"][0].T), "w_peer_v": _expert_stripes(g["peer_v"][0]),
        "norm_mix_g": g["norm_mix_g"][0], "mem_norm_g": g["mem_norm_g"][0], "norm_ffn_g": g["norm_ffn_g"][0],
        "norm_final_g": g["norm_final_g"],
        **_constants(),
    }
    nc = bacc.Bacc("TRN2", target_bir_lowering=False, num_devices=1)
    a, given = {}, {}
    for name, x in arrays.items():
        x = np.ascontiguousarray(x)
        given["in_" + name] = x
        a[name] = nc.dram_tensor("in_" + name, x.shape, mybir.dt.from_np(x.dtype), kind="ExternalInput").ap()
    for name, shape in _OUTS.items():
        a[name] = nc.dram_tensor("out_" + name, shape, F32, kind="ExternalOutput").ap()
    build(nc, a)
    r = run_bass_kernel_spmd(nc, [given], core_ids=[0]).results[0]
    y, zo, mo, lf, st = (np.asarray(r["out_" + n]) for n in _OUTS)

    def rows(z_part, t0, t1):
        return np.ascontiguousarray(z_part[:, :, t0:t1].transpose(2, 1, 0)).reshape(t1 - t0, -1)

    k, v, u = zo[:, 0:8], zo[:, 8:16], zo[:, 16:20]
    return (
        y[0:T_P].reshape(1, T_P, D), y[T_P:T].reshape(DB, DT, D),
        rows(k, 0, T_P).reshape(1, 1, T_P, FOX, HD), rows(v, 0, T_P).reshape(1, 1, T_P, FOX, HD),
        np.ascontiguousarray(lf[:, 0:T_P].T).reshape(1, 1, T_P, FOX),
        rows(u, T_P - STATE, T_P).reshape(1, 1, STATE, 512),
        rows(mo[:, 0:MEM], 0, N_MEM).reshape(1, 1, N_MEM, MEM, HD), rows(mo[:, MEM:], 0, N_MEM).reshape(1, 1, N_MEM, MEM, HD),
        rows(k, T_P, T).reshape(1, DB, DT, FOX, HD), rows(v, T_P, T).reshape(1, DB, DT, FOX, HD),
        np.ascontiguousarray(lf[:, T_P:T].T).reshape(1, DB, DT, FOX),
        np.ascontiguousarray(st.transpose(2, 3, 1, 0)).reshape(1, DB, STATE, 512),
    )
```
